# Optimizing a Trainium2 kernel written in Bass

```python
import math
import jax, jax.numpy as jnp
from jax import lax
import numpy as np

D_MODEL = 2048
BATCH = 1
SEQ = 512
DEPTH = 1
DEC_BATCH = 8
DEC_SEQ = 4
PAST_LEN = 2048
PAGE_SIZE = 128

N_HEADS = 16
HEAD_DIM = 64
ATTN_WIDTH = N_HEADS * HEAD_DIM
POOL_WINDOWS = (2, 4, 8, 16)
POOL_GROUPS = len(POOL_WINDOWS)
POOL_WIDTH = D_MODEL // 2
POOL_GROUP_CH = POOL_WIDTH // POOL_GROUPS
POOL_OUT_CH = D_MODEL // POOL_GROUPS
POOL_STATE = max(POOL_WINDOWS) - 1
D_FF = ((8 * D_MODEL // 3 + 255) // 256) * 256
IN_COLS = 3 * ATTN_WIDTH + POOL_WIDTH + 2 * D_MODEL
Q_BLOCK = 128
RMS_EPS = 1e-6
SB_BIAS_HI = -5.0
SB_BIAS_LO = -10.0

kernel_name = "stickbreak_pool_gated_hybrid_step"

def rms_norm(x, g):
    xf = x.astype(jnp.float32)
    xf = xf * lax.rsqrt(jnp.mean(xf * xf, axis=-1, keepdims=True) + RMS_EPS)
    return xf.astype(x.dtype) * g

def in_proj(x, norm_g, w_in, q_g, k_g):
    b, t = x.shape[:2]
    h = rms_norm(x, norm_g) @ w_in
    cuts = [ATTN_WIDTH, 2 * ATTN_WIDTH, 3 * ATTN_WIDTH, 3 * ATTN_WIDTH + POOL_WIDTH,
            3 * ATTN_WIDTH + POOL_WIDTH + D_MODEL]
    q, k, v, u, g_attn, g_pool = jnp.split(h, cuts, axis=-1)
    q = rms_norm(q.reshape(b, t, N_HEADS, HEAD_DIM), q_g)
    k = rms_norm(k.reshape(b, t, N_HEADS, HEAD_DIM), k_g)
    v = v.reshape(b, t, N_HEADS, HEAD_DIM)
    return q, k, v, u, g_attn, g_pool

def stick_breaking(q, k, v, sb_bias, q_pos, k_pos):
    z = jnp.einsum('bthd,bshd->bhts', q.astype(jnp.float32), k.astype(jnp.float32)) * (HEAD_DIM ** -0.5)
    z = z + sb_bias.astype(jnp.float32)[None, :, None, None]
    causal = k_pos[None, :] < q_pos[:, None]
    log_keep = jnp.where(causal, jax.nn.log_sigmoid(-z), 0.0)
    after = lax.cumsum(log_keep, axis=3, reverse=True) - log_keep
    log_a = jnp.where(causal, jax.nn.log_sigmoid(z) + after, -jnp.inf)
    a = jnp.exp(log_a).astype(v.dtype)
    return jnp.einsum('bhts,bshd->bthd', a, v)

def stick_breaking_blocked(q, k, v, sb_bias):
    b, s = q.shape[:2]
    nb = s // Q_BLOCK
    pos = jnp.arange(s, dtype=jnp.int32)
    q_blocks = q.reshape(b, nb, Q_BLOCK, N_HEADS, HEAD_DIM).swapaxes(0, 1)
    p_blocks = pos.reshape(nb, Q_BLOCK)
    out = lax.map(lambda qp: stick_breaking(qp[0], k, v, sb_bias, qp[1], pos), (q_blocks, p_blocks))
    return out.swapaxes(0, 1).reshape(b, s, N_HEADS, HEAD_DIM)

def pool_branch(u_ext, pos, w_pool, pool_scale):
    b = u_ext.shape[0]
    t = pos.shape[0]
    uf = u_ext.astype(jnp.float32)
    cs = jnp.concatenate([jnp.zeros((b, 1, POOL_WIDTH), jnp.float32), jnp.cumsum(uf, axis=1)], axis=1)
    u_new = uf[:, POOL_STATE:]
    groups = []
    for g, w in enumerate(POOL_WINDOWS):
        lo, hi = g * POOL_GROUP_CH, (g + 1) * POOL_GROUP_CH
        win_sum = cs[:, POOL_STATE + 1:, lo:hi] - cs[:, POOL_STATE + 1 - w:POOL_STATE + 1 - w + t, lo:hi]
        cnt = jnp.minimum(w, pos + 1).astype(jnp.float32)[None, :, None]
        groups.append(win_sum / cnt - u_new[..., lo:hi])
    p = jnp.stack(groups, axis=2).astype(u_ext.dtype)
    out = jnp.einsum('btgc,gce->btge', p, w_pool).reshape(b, t, D_MODEL)
    return out * pool_scale

def merge_and_ffn(x, o_attn, o_pool, g_attn, g_pool, w_attn_proj, w_out, norm2_g, w_gate_up, w_down):
    b, t = x.shape[:2]
    a = o_attn.reshape(b, t, ATTN_WIDTH) @ w_attn_proj
    mixed = jax.nn.sigmoid(g_attn) * a + jax.nn.sigmoid(g_pool) * o_pool
    h = x + mixed @ w_out
    gate, up = jnp.split(rms_norm(h, norm2_g) @ w_gate_up, 2, axis=-1)
    return h + (jax.nn.silu(gate) * up) @ w_down

def setup_inputs(seed: int = 0) -> dict:
    key = jax.random.key(seed)
    ks = jax.random.split(key, 20)
    n_pages = PAST_LEN // PAGE_SIZE
    n_used = DEC_BATCH * n_pages
    n_pool = n_used + (n_used + 3) // 4
    f32 = jnp.float32

    def nrm(k, shape, scale=1.0):
        return jax.random.normal(k, shape, f32) * scale

    page_table = jax.random.permutation(ks[5], n_pool)[:n_used].reshape(DEC_BATCH, n_pages).astype(jnp.int32)
    sb_bias = jnp.broadcast_to(jnp.linspace(SB_BIAS_HI, SB_BIAS_LO, N_HEADS, dtype=f32), (DEPTH, N_HEADS)) \
        + nrm(ks[17], (DEPTH, N_HEADS), 0.1)
    return {
        "x_prompt": nrm(ks[0], (BATCH, SEQ, D_MODEL)),
        "x_sample": nrm(ks[1], (DEC_BATCH, DEC_SEQ, D_MODEL)),
        "cache_k": nrm(ks[2], (DEPTH, n_pool, PAGE_SIZE, N_HEADS, HEAD_DIM)),
        "cache_v": nrm(ks[3], (DEPTH, n_pool, PAGE_SIZE, N_HEADS, HEAD_DIM)),
        "state_pool": nrm(ks[4], (DEPTH, DEC_BATCH, POOL_STATE, POOL_WIDTH)),
        "page_table": page_table,
        "norm1_g": 1.0 + nrm(ks[6], (DEPTH, D_MODEL), 0.1),
        "w_in": nrm(ks[7], (DEPTH, D_MODEL, IN_COLS), D_MODEL ** -0.5),
        "q_norm_g": 1.0 + nrm(ks[8], (DEPTH, HEAD_DIM), 0.1),
        "k_norm_g": 1.0 + nrm(ks[9], (DEPTH, HEAD_DIM), 0.1),
        "sb_bias": sb_bias,
        "w_attn_proj": nrm(ks[10], (DEPTH, ATTN_WIDTH, D_MODEL), ATTN_WIDTH ** -0.5),
        "w_pool": nrm(ks[11], (DEPTH, POOL_GROUPS, POOL_GROUP_CH, POOL_OUT_CH), POOL_GROUP_CH ** -0.5),
        "pool_scale": 1.0 + nrm(ks[12], (DEPTH, D_MODEL), 0.1),
        "w_out": nrm(ks[13], (DEPTH, D_MODEL, D_MODEL), D_MODEL ** -0.5),
        "norm2_g": 1.0 + nrm(ks[14], (DEPTH, D_MODEL), 0.1),
        "w_gate_up": nrm(ks[15], (DEPTH, D_MODEL, 2 * D_FF), D_MODEL ** -0.5),
        "w_down": nrm(ks[16], (DEPTH, D_FF, D_MODEL), D_FF ** -0.5),
    }

def reference(x_prompt, x_sample, cache_k, cache_v, state_pool, page_table, norm1_g, w_in,
              q_norm_g, k_norm_g, sb_bias, w_attn_proj, w_pool, pool_scale, w_out, norm2_g, w_gate_up, w_down):
    b_p, seq = x_prompt.shape[:2]
    b_s, t_s = x_sample.shape[:2]
    n_pages = page_table.shape[1]
    past_len = n_pages * cache_k.shape[2]
    pos_p = jnp.arange(seq, dtype=jnp.int32)
    pos_s = past_len + jnp.arange(t_s, dtype=jnp.int32)
    k_pos_s = jnp.arange(past_len + t_s, dtype=jnp.int32)

    xp, xs = x_prompt, x_sample
    kp_l, vp_l, up_l, ks_l, vs_l, us_l = [], [], [], [], [], []
    for l in range(DEPTH):
        q, k, v, u, ga, gb = in_proj(xp, norm1_g[l], w_in[l], q_norm_g[l], k_norm_g[l])
        o_attn = stick_breaking_blocked(q, k, v, sb_bias[l])
        u_ext = jnp.concatenate([jnp.zeros((b_p, POOL_STATE, POOL_WIDTH), u.dtype), u], axis=1)
        o_pool = pool_branch(u_ext, pos_p, w_pool[l], pool_scale[l])
        kp_l.append(k)
        vp_l.append(v)
        up_l.append(u_ext[:, -POOL_STATE:])
        xp = merge_and_ffn(xp, o_attn, o_pool, ga, gb, w_attn_proj[l], w_out[l], norm2_g[l],
                           w_gate_up[l], w_down[l])

        q, k, v, u, ga, gb = in_proj(xs, norm1_g[l], w_in[l], q_norm_g[l], k_norm_g[l])
        k_past = cache_k[l][page_table].reshape(b_s, past_len, N_HEADS, HEAD_DIM)
        v_past = cache_v[l][page_table].reshape(b_s, past_len, N_HEADS, HEAD_DIM)
        k_all = jnp.concatenate([k_past, k], axis=1)
        v_all = jnp.concatenate([v_past, v], axis=1)
        o_attn = stick_breaking(q, k_all, v_all, sb_bias[l], pos_s, k_pos_s)
        u_ext = jnp.concatenate([state_pool[l], u], axis=1)
        o_pool = pool_branch(u_ext, pos_s, w_pool[l], pool_scale[l])
        ks_l.append(k)
        vs_l.append(v)
        us_l.append(u_ext[:, -POOL_STATE:])
        xs = merge_and_ffn(xs, o_attn, o_pool, ga, gb, w_attn_proj[l], w_out[l], norm2_g[l],
                           w_gate_up[l], w_down[l])

    k_prompt_new = jnp.stack(kp_l, axis=0)
    v_prompt_new = jnp.stack(vp_l, axis=0)
    pool_prompt_new = jnp.stack(up_l, axis=0)
    k_sample_new = jnp.stack(ks_l, axis=0)
    v_sample_new = jnp.stack(vs_l, axis=0)
    pool_sample_new = jnp.stack(us_l, axis=0)
    return (xp, xs, k_prompt_new, v_prompt_new, pool_prompt_new, k_sample_new, v_sample_new, pool_sample_new)


_drawn_inputs = setup_inputs


def setup_inputs(seed=0):
    import zlib

    import numpy as np

    out = dict(_drawn_inputs(seed))
    spreads = {}
    factors = {'q_norm_g': 8.0}
    for name, (base, spread) in spreads.items():
        noise = np.random.default_rng([zlib.crc32(name.encode()), seed]).standard_normal(out[name].shape)
        drawn = base * np.exp(spread * noise) if base else spread * noise
        out[name] = __import__('jax').numpy.asarray(drawn.astype(out[name].dtype))
    for name, factor in factors.items():
        out[name] = (out[name] * factor).astype(out[name].dtype)
    return out
```

```python
from contextlib import ExitStack

import numpy as np

import concourse.bass as bass
from concourse import mybir

F32 = mybir.dt.float32
F32R = mybir.dt.float32r
I32 = mybir.dt.int32
ACT = mybir.ActivationFunctionType
ALU = mybir.AluOpType

P = 128
D = 2048
SEQ = 512
NB, NT = 8, 4
NSAMP = NB * NT
T = SEQ + NSAMP
HALF = T // 2
H, HD = 16, 64
AW = H * HD
PAIRS = AW // P
HT = H * NT
PW = D // 2
PT = PW // P
HIST = 15
WINDOWS = (2, 4, 8, 16)
SEG = HIST + NT
UW = HIST + SEQ + NB * SEG
FF = 5632
KD = D // P
IN_TILES = (3 * AW + PW + 2 * D) // P
PAGE = 128
NPAGE = 16
EPS = 1e-6
MASKED = -1e30
FT = FF // P
CHUNKS = 4
CF = FT // CHUNKS
TOKEN_TILES = [(i * P, min(P, T - i * P)) for i in range(-(-T // P))]

SCORE_SEGS = [(0, 0), (512, 1), (1024, 2), (896, 3)]
SAMPLE_COL = 1280
SCORES = SAMPLE_COL + NSAMP

C_IDENT, C_ONES, C_PAIR, C_TRI, C_FOLD = 0, P, 2 * P, 3 * P, 4 * P
C_CORR = C_FOLD + HT
C_WIDTH = C_CORR + 4 * 16
V_NORM1, V_NORM2, V_PSCALE, V_QG, V_KG = 0, KD, 2 * KD, 3 * KD, 3 * KD + 1
V_ROWS = 3 * KD + 2


def constants():
    c = np.zeros((P, C_WIDTH), np.float32)
    r = np.arange(P)
    c[:, C_IDENT:C_IDENT + P] = np.eye(P)
    c[:, C_ONES:C_ONES + P] = 1.0
    c[:, C_PAIR:C_PAIR + P] = (r[:, None] // HD == r[None, :] // HD)
    c[:, C_TRI:C_TRI + P] = (r[:, None] >= r[None, :])
    c[:, C_FOLD:C_FOLD + HT] = (r[:, None] % HT == np.arange(HT)[None, :])
    for g, w in enumerate(WINDOWS):
        c[:, C_CORR + 16 * g:C_CORR + 16 * g + 16] = w / np.minimum(w, np.arange(16) + 1.0)
    mask = np.zeros((P, SCORES), np.float32)
    for col, kb in SCORE_SEGS:
        mask[:, col:col + P] = np.where(r[:, None] < r[None, :], 0.0, MASKED)
    q = np.arange(NSAMP)
    seen = (r[:, None] // NT == q[None, :] // NT) & (r[:, None] % NT < q[None, :] % NT)
    mask[:, SAMPLE_COL:] = np.where(seen & (r[:, None] < NSAMP), 0.0, MASKED)
    return c, mask


def later(n, k=1):
    return not isinstance(n, int) or n >= k


def by_pairs(eng, start, stop, step, tail=0):
    for n in (start, start + 1):
        step(n, n // 2, n % 2)
    with eng.Fori(0, (stop - tail - start - 2) // 2) as i:
        for p in range(2):
            step(i * 2 + (start + 2 + p), i + (start + 2) // 2, p)
    for n in range(stop - tail, stop):
        step(n, n // 2, n % 2)


class Memory:

    def __init__(self, nc):
        base = -(-nc.sbuf_base // 64) * 64
        size = (nc.sbuf_top - base) // 64 * 64
        self.size = size

        def at(name, shape, dtype, offset):
            width = int(np.prod(shape[1:])) * 4
            assert 0 <= offset and offset + width <= size, (name, offset, width, size)
            return nc.alloc_sbuf_tensor_at(name, shape, dtype, offset=base + offset)

        def run(offset, *specs):
            out = []
            for name, shape, dtype in specs:
                out.append(at(name, shape, dtype, offset))
                offset += -(-int(np.prod(shape[1:])) * 4 // 32) * 32
            return out, offset

        self.at, self.run = at, run
        tok = 4 * T
        (self.const, self.vec, self.bias, self.biasT, self.pages, self.carry), low = run(
            0, ("const", [P, C_WIDTH], F32), ("vec", [P, 64], F32), ("bias", [P, H], F32),
            ("biasT", [P, H, NT], F32), ("pages", [1, NB * NPAGE], I32), ("carry", [P, NB, HT], F32))
        self.low = low
        self.after_q = low + PAIRS * tok
        (self.qT, self.kT, self.v_nat, self.v_new, self.uT), self.after_qkv = run(
            low, ("qT", [P, PAIRS, T], F32), ("kT", [P, PAIRS, T], F32),
            ("v_nat", [P, SEQ // P, AW], F32), ("v_new", [NSAMP, AW], F32), ("uT", [P, PT, UW], F32))
        top = size - 2 * KD * tok
        self.xn_hi, self.xn_lo = run(top, ("xn_hi", [P, KD, T], F32R), ("xn_lo", [P, KD, T], F32R))[0]
        self.top = top
        self.top_o = size - 3 * PAIRS * tok
        self.oT, self.pool_hi, self.pool_lo = run(
            self.top_o, ("oT", [P, PAIRS, T], F32), ("pool_hi", [P, PT, T], F32R),
            ("pool_lo", [P, PT, T], F32R))[0]
        self.free = -(-4 * (C_WIDTH + 64) // 32) * 32
        (self.mix_hi, self.mix_lo), self.after_mix = run(
            self.free, ("mix_hi", [P, KD, T], F32R), ("mix_lo", [P, KD, T], F32R))
        (self.hT, self.rstd2), self.after_h = run(
            self.after_mix, ("hT", [P, KD, T], F32), ("rstd2", [P, T], F32))
        self.hn_hi, self.hn_lo = run(top, ("hn_hi", [P, KD, T], F32R), ("hn_lo", [P, KD, T], F32R))[0]

    def c(self, col, rows=P, width=P):
        return self.const[0:rows, col:col + width]


class Weights:

    KT = 8

    def __init__(self, nc, ctx, mem, phase, offset):
        shape = [P, self.KT, P]
        specs = [(f"{phase}_{part}{b}", shape, F32 if part == "raw" else F32R)
                 for part in ("raw", "hi", "lo") for b in range(2)]
        tensors, self.end = mem.run(offset, *specs)
        self.raw, self.hi, self.lo = tensors[0:2], tensors[2:4], tensors[4:6]
        self.nc = nc
        self.loaded = [ctx.enter_context(nc.semaphore(f"{phase}_w_loaded{b}")) for b in range(2)]
        self.hi_made = [ctx.enter_context(nc.semaphore(f"{phase}_w_hi_made{b}")) for b in range(2)]
        self.lo_made = [ctx.enter_context(nc.semaphore(f"{phase}_w_lo_made{b}")) for b in range(2)]
        self.used = [ctx.enter_context(nc.semaphore(f"{phase}_w_used{b}")) for b in range(2)]

    def load(self, sp, n, b, src, kts=KT):
        if later(n):
            sp.wait_ge(self.lo_made[b], n)
        sp.dma_start(self.raw[b][:, 0:kts, :], src).then_inc(self.loaded[b], 16)

    def split_hi(self, act, n, b, kts=KT):
        act.wait_ge(self.loaded[b], n * 16 + 16)
        if later(n):
            act.wait_ge(self.used[b], n)
        self.nc.scalar.copy(self.hi[b][:, 0:kts, :], self.raw[b][:, 0:kts, :]).then_inc(self.hi_made[b], 1)

    def split_lo(self, dve, n, b, kts=KT):
        dve.wait_ge(self.hi_made[b], n + 1)
        self.nc.vector.tensor_tensor(self.lo[b][:, 0:kts, :], self.raw[b][:, 0:kts, :],
                                     self.hi[b][:, 0:kts, :].bitcast(F32),
                                     ALU.subtract).then_inc(self.lo_made[b], 1)

    def multiply(self, pe, n, b, banks, x_hi, x_lo, kt0=0, kts=KT, start=True, stop=True):
        pe.wait_ge(self.lo_made[b], n + 1)
        for k in range(kts):
            for i, (w, x) in enumerate(((self.hi, x_hi), (self.hi, x_lo), (self.lo, x_hi))):
                for half in range(2):
                    mm = self.nc.tensor.matmul(
                        banks[:, half, 0:HALF], w[b][:, k, :], x(kt0 + k, half),
                        start=start and k == 0 and i == 0, stop=stop and k == kts - 1 and i == 2)
        mm.then_inc(self.used[b], 1)


def tile_of(x):
    return lambda k, half: x[:, k, half * HALF:(half + 1) * HALF]


def halves(banks):
    return banks[:, :, 0:HALF]


def by_halves(x):
    return x.rearrange("p (h t) -> p h t", h=2)


def norm_inputs(nc, mem, ps, a, scratch):
    with ExitStack() as ctx:
        sem = lambda name: ctx.enter_context(nc.semaphore("a_" + name))
        (xin0, xin1, xs0, xs1, junk, xg, xt, vrows, brow, ms, var, rstd), _ = mem.run(
            mem.low, ("a_x0", [P, D], F32), ("a_x1", [P, D], F32), ("a_xs0", [P, D], F32),
            ("a_xs1", [P, D], F32), ("a_junk", [P, D], F32), ("a_xg", [P, 2, 4, P], F32),
            ("a_xt", [P, 2, 4, P], F32), ("a_vrows", [V_ROWS, P], F32), ("a_brow", [1, H], F32),
            ("a_ms", [P, 8], F32), ("a_var", [P, 8], F32), ("a_rstd", [P, 8], F32))
        xin, xs = (xin0, xin1), (xs0, xs1)
        x_in = [sem(f"x_in{i}") for i in range(2)]
        params_in, vec_turned, vec_made, bias_made = (
            sem("params_in"), sem("vec_turned"), sem("vec_made"), sem("bias_made"))
        squared, var_made, rooted, rstd_made, scaled = (
            sem("squared"), sem("var_made"), sem("rooted"), sem("rstd_made"), sem("scaled"))
        turned, x_kept, weighted, hi_made, lo_made = (
            sem("turned"), sem("x_kept"), sem("weighted"), sem("hi_made"), sem("lo_made"))
        raw_turned, raw_kept = sem("raw_turned"), sem("raw_kept")
        raw_out = [sem(f"raw_out{i}") for i in range(2)]
        tiles = TOKEN_TILES
        units = [(i, j) for i in range(len(tiles)) for j in range(KD // 4)]

        def source(i):
            if i < SEQ // P:
                return a["x_prompt"][0, i * P:(i + 1) * P, :]
            return a["x_sample"].rearrange("b t d -> (b t) d")

        with nc.Block(no_gpsimd_drain=True) as block:

            @block.sync
            def _(sp):
                def load_x(i):
                    n = tiles[i][1]
                    if i >= 2:
                        sp.wait_ge(raw_turned, 4 * (i - 1))
                        sp.wait_ge(scaled, i - 1)
                    sp.dma_start(xin[i % 2][0:n, :], source(i)).then_inc(x_in[i % 2], 16)

                for i in range(2):
                    load_x(i)
                    if i == 0:
                        sp.dma_start(mem.const[:, :], a["const"]).then_inc(params_in, 16)
                        for name, row in (("norm1_g", V_NORM1), ("norm2_g", V_NORM2), ("pool_scale", V_PSCALE)):
                            sp.dma_start(vrows[row:row + KD, :],
                                         a[name][0].rearrange("(k p) -> k p", p=P)).then_inc(params_in, 16)
                        for name, row in (("q_norm_g", V_QG), ("k_norm_g", V_KG)):
                            for e in range(2):
                                sp.dma_start(vrows[row:row + 1, e * HD:(e + 1) * HD], a[name]).then_inc(params_in, 16)
                        sp.dma_start(brow[:, :], a["sb_bias"]).then_inc(params_in, 16)
                        sp.dma_start(mem.pages[:, :], a["page_table"].rearrange("b n -> (b n)").unsqueeze(0)).then_inc(params_in, 16)
                for u, (i, j) in enumerate(units):
                    t0, n = tiles[i]
                    sp.wait_ge(raw_kept, u + 1)
                    sp.dma_start(scratch["xT"][4 * j:4 * j + 4, :, t0:t0 + n].rearrange("k p t -> p k t"),
                                 xt[:, u % 2, :, 0:n]).then_inc(raw_out[u % 2], 16)
                    if j == KD // 4 - 1 and i + 2 < len(tiles):
                        load_x(i + 2)
                for h in range(2):
                    sp.wait_ge(raw_out[h], 16 * len(units) // 2)

            @block.tensor
            def _(pe):
                pe.wait_ge(params_in, 16 * 10)
                nc.tensor.transpose(ps[:, 0, 0:V_ROWS], vrows[:, :], mem.c(C_IDENT, V_ROWS, V_ROWS))
                nc.tensor.matmul(ps[:, 1, 0:H], mem.c(C_ONES, 1), brow[:, :],
                                 start=True, stop=True).then_inc(vec_turned, 1)
                pe.wait_ge(vec_made, 1)
                pe.wait_ge(bias_made, 1)
                for i, (_, n) in enumerate(tiles):
                    for which in range(2):
                        for j in range(KD // 4):
                            u = 4 * i + j
                            bank = 4 * which + u % 4
                            if which == 0:
                                pe.wait_ge(x_in[i % 2], 16 * (i // 2 + 1))
                                if u >= 4:
                                    pe.wait_ge(raw_kept, u - 3)
                            else:
                                pe.wait_ge(scaled, i + 1)
                                if u >= 4:
                                    pe.wait_ge(weighted, u - 3)
                            x = (xin, xs)[which][i % 2]
                            for k in range(4):
                                tr = nc.tensor.transpose(ps[:, bank, k * P:k * P + n],
                                                         x[0:n, (4 * j + k) * P:(4 * j + k + 1) * P],
                                                         mem.c(C_IDENT, n, n))
                            tr.then_inc((raw_turned, turned)[which], 1)

            @block.scalar
            def _(act):
                act.wait_ge(vec_turned, 1)
                nc.scalar.copy(mem.bias[:, :], ps[:, 1, 0:H]).then_inc(bias_made, 1)
                act.wait_ge(bias_made, 1)
                nc.scalar.copy(mem.biasT[:, :, :], mem.bias[:, :].unsqueeze(2).to_broadcast([P, H, NT])).then_inc(bias_made, 1)

                def root(i):
                    n = tiles[i][1]
                    act.wait_ge(x_in[i % 2], 16 * (i // 2 + 1))
                    if i:
                        act.wait_ge(squared, i)
                    nc.scalar.activation(junk[0:n, :], xin[i % 2][0:n, :], ACT.Square,
                                         accum_out=ms[0:n, i:i + 1]).then_inc(squared, 1)
                    act.wait_ge(var_made, i + 1)
                    nc.scalar.activation(rstd[0:n, i:i + 1], var[0:n, i:i + 1], ACT.Sqrt).then_inc(rooted, 1)

                root(0)
                for i, (t0, n) in enumerate(tiles):
                    if i + 1 < len(tiles):
                        root(i + 1)
                    for j in range(KD // 4):
                        u = 4 * i + j
                        act.wait_ge(raw_turned, u + 1)
                        if u >= 2:
                            act.wait_ge(raw_out[u % 2], 16 * (u // 2))
                        nc.scalar.copy(xt[:, u % 2, :, 0:n],
                                       ps[:, u % 4, :].rearrange("p (k t) -> p k t", k=4)[:, :, 0:n]).then_inc(raw_kept, 1)
                        act.wait_ge(weighted, u + 1)
                        nc.scalar.copy(mem.xn_hi[:, 4 * j:4 * j + 4, t0:t0 + n], xg[:, u % 2, :, 0:n]).then_inc(hi_made, 1)

            @block.vector
            def _(dve):
                dve.wait_ge(vec_turned, 1)
                nc.vector.tensor_copy(mem.vec[:, 0:V_ROWS], ps[:, 0, 0:V_ROWS]).then_inc(vec_made, 1)
                dve.wait_ge(vec_made, 1)
                nc.vector.tensor_scalar(mem.vec[:, V_QG:V_QG + 1], mem.vec[:, V_QG:V_QG + 1], HD ** -0.5,
                                        None, ALU.mult).then_inc(vec_made, 1)

                def scale(i):
                    n = tiles[i][1]
                    dve.wait_ge(squared, i + 1)
                    nc.vector.tensor_scalar(var[0:n, i:i + 1], ms[0:n, i:i + 1], 1.0 / D, EPS,
                                            ALU.mult, ALU.add).then_inc(var_made, 1)
                    dve.wait_ge(rooted, i + 1)
                    nc.vector.reciprocal(rstd[0:n, i:i + 1], rstd[0:n, i:i + 1]).then_inc(rstd_made, 1)
                    dve.wait_ge(rstd_made, i + 1)
                    if i >= 2:
                        dve.wait_ge(turned, 4 * (i - 1))
                    nc.vector.tensor_scalar(xs[i % 2][0:n, :], xin[i % 2][0:n, :], rstd[0:n, i:i + 1],
                                            None, ALU.mult).then_inc(scaled, 1)

                scale(0)
                for i, (t0, n) in enumerate(tiles):
                    if i + 1 < len(tiles):
                        scale(i + 1)
                    for j in range(KD // 4):
                        u = 4 * i + j
                        dve.wait_ge(turned, u + 1)
                        if u >= 2:
                            dve.wait_ge(lo_made, u - 1)
                        g = mem.vec[:, V_NORM1 + 4 * j:V_NORM1 + 4 * j + 4].unsqueeze(2).to_broadcast([P, 4, n])
                        nc.vector.tensor_tensor(xg[:, u % 2, :, 0:n],
                                                ps[:, 4 + u % 4, :].rearrange("p (k t) -> p k t", k=4)[:, :, 0:n],
                                                g, ALU.mult).then_inc(weighted, 1)
                        dve.wait_ge(hi_made, u + 1)
                        nc.vector.tensor_tensor(mem.xn_lo[:, 4 * j:4 * j + 4, t0:t0 + n], xg[:, u % 2, :, 0:n],
                                                mem.xn_hi[:, 4 * j:4 * j + 4, t0:t0 + n].bitcast(F32),
                                                ALU.subtract).then_inc(lo_made, 1)


Q, K, V, U, GATE = range(5)
KIND_START = (0, 8, 16, 24, 32, IN_TILES)


def kind_of(n):
    return max(k for k in range(5) if KIND_START[k] <= n)


def project_in(nc, mem, ps, a, o, scratch):
    with ExitStack() as ctx:
        sem = lambda name: ctx.enter_context(nc.semaphore("b_" + name))
        W = Weights(nc, ctx, mem, "b", mem.after_qkv)
        (raw0, raw1, sq, root, inv, kn0, kn1, nat0, nat1, natS0, natS1), end = mem.run(
            W.end, ("b_t0", [P, T], F32), ("b_t1", [P, T], F32), ("b_sq", [P, T], F32),
            ("b_root", [P, T], F32), ("b_inv", [P, T], F32), ("b_kn0", [P, T], F32), ("b_kn1", [P, T], F32),
            ("b_nat0", [P, 4, P], F32), ("b_nat1", [P, 4, P], F32),
            ("b_natS0", [NSAMP, P], F32), ("b_natS1", [NSAMP, P], F32))
        assert end <= mem.top, (end, mem.top)
        res, kn, nat, nat_s = (raw0, raw1), (kn0, kn1), (nat0, nat1), (natS0, natS1)
        res_made = sem("res_made")
        squared, summed, rooted = sem("squared"), sem("summed"), sem("rooted")
        inverted, normed = sem("inverted"), sem("normed")
        u_placed = sem("u_placed")
        turned, nat_made = sem("turned"), sem("nat_made")
        kept = [sem(f"kept{i}") for i in range(2)]
        v_out = sem("v_out")
        w_in = a["w_in"][0].rearrange("(b k p) c -> b p k c", b=2, p=P)
        mm_banks = [ps[:, 2 * p:2 * p + 2, :] for p in range(2)]
        sum_banks = ps[:, 4:6, :]
        first_turned = KIND_START[K]
        k_out = [o["k_prompt"][0, 0].rearrange("(b p) h d -> p b (h d)", p=P),
                 o["k_sample"][0].rearrange("b t h d -> (b t) (h d)")]
        state = a["state_pool"][0]
        for_each = lambda eng, step: [by_pairs(eng, KIND_START[k], KIND_START[k + 1], lambda n, i, p, k=k: step(
            n, i, p, k, kind_of(n - 1) if isinstance(n, int) and n else k,
            kind_of(n - 2) if isinstance(n, int) and n > 1 else k), tail=2 * (k == GATE)) for k in range(5)]

        with nc.Block(no_gpsimd_drain=True) as block:

            @block.sync
            def _(sp):
                def columns(n, b):
                    return w_in[b][:, :, bass.ds(n * P, P)]

                def step(n, i, p, kind, k1, k2):
                    if not (isinstance(n, int) and n == IN_TILES - 1):
                        for b in range(2):
                            W.load(sp, n + 1, b, columns(n + 1, b))
                    if later(n, 2):
                        store(n - 2, i - 1, p, k2)

                def store(n, i, p, kind):
                    if kind in (K, U):
                        cols = bass.ds((n - KIND_START[kind]) * P, P)
                        sp.wait_ge(nat_made, n - (first_turned - 1))
                        if kind == K:
                            sp.dma_start(k_out[0][:, :, cols], nat[p][:, :, :]).then_inc(kept[p], 16)
                            sp.dma_start(k_out[1][:, cols], nat_s[p][:, :]).then_inc(kept[p], 16)
                        else:
                            sp.dma_start(o["pool_prompt"][0, 0][:, cols], nat[p][P - HIST:P, 0, :]).then_inc(kept[p], 16)
                            sp.dma_start(o["pool_sample"][0][:, HIST - NT:HIST, cols],
                                         nat_s[p][:, :]).then_inc(kept[p], 16)
                    if kind == GATE:
                        sp.wait_ge(res_made, n + 1)
                        sp.dma_start(scratch["gates"][bass.ds(n - KIND_START[GATE], 1), :, :].rearrange("a p t -> p a t"),
                                     res[p][:, :].unsqueeze(1)).then_inc(kept[p], 16)

                sp.dma_start(o["pool_sample"][0][:, 0:HIST - NT, :], state[:, NT:HIST, :]).then_inc(v_out, 16)
                for b in range(2):
                    W.load(sp, 0, b, columns(0, b))
                for_each(sp, step)
                for n in (IN_TILES - 2, IN_TILES - 1):
                    store(n, n // 2, n % 2, GATE)
                sp.wait_ge(nat_made, KIND_START[GATE] - first_turned)
                sp.dma_start(o["v_prompt"][0, 0].rearrange("(b p) h d -> p b (h d)", p=P),
                             mem.v_nat[:, :, :]).then_inc(v_out, 16)
                sp.dma_start(o["v_sample"][0].rearrange("b t h d -> (b t) (h d)"), mem.v_new[:, :]).then_inc(v_out, 16)
                sp.wait_ge(v_out, 48)
                for p in range(2):
                    sp.wait_ge(kept[p], 32 * 8 + 16 * 16)

            @block.tensor
            def _(pe):
                def step(n, i, p, kind, k1, k2):
                    if later(n, 2):
                        pe.wait_ge(res_made, n - 1)
                    W.multiply(pe, n, 0, mm_banks[p], tile_of(mem.xn_hi), tile_of(mem.xn_lo), 0, stop=False)
                    if later(n) and k1 in (Q, K):
                        pe.wait_ge(squared, n)
                        if later(n, 2):
                            pe.wait_ge(rooted, n - 1)
                        for h in range(2):
                            mm = nc.tensor.matmul(sum_banks[:, h, 0:HALF], mem.c(C_PAIR),
                                                  sq[:, h * HALF:(h + 1) * HALF], start=True, stop=True)
                        mm.then_inc(summed, 1)
                    W.multiply(pe, n, 1, mm_banks[p], tile_of(mem.xn_hi), tile_of(mem.xn_lo), W.KT, start=False)
                    if k1 in (K, V, U) and later(n, first_turned + 1):
                        src = (kn if k1 == K else res)[1 - p]
                        m = n - first_turned
                        if k1 == K:
                            pe.wait_ge(normed, n)
                        else:
                            pe.wait_ge(res_made, n)
                        if later(n, first_turned + 2):
                            pe.wait_ge(nat_made, m - 1)
                        for t in range(3 if k1 == U else 0, 4):
                            nc.tensor.transpose(ps[:, 6, (t % (3 if k1 == U else 4)) * P:(t % (3 if k1 == U else 4) + 1) * P],
                                                src[:, t * P:(t + 1) * P], mem.c(C_IDENT))
                        nc.tensor.transpose(ps[0:NSAMP, 7, 0:P], src[:, SEQ:T], mem.c(C_IDENT)).then_inc(turned, 1)

                for_each(pe, step)

            @block.scalar
            def _(act):
                def step(n, i, p, kind, k1, k2):
                    last = isinstance(n, int) and n == IN_TILES - 1
                    if not last:
                        W.split_hi(act, n + 1, 0)
                    if later(n) and k1 in (Q, K):
                        act.wait_ge(summed, n)
                        if later(n, 2):
                            act.wait_ge(inverted, n - 1)
                        nc.scalar.activation(by_halves(root[:, :]), halves(sum_banks), ACT.Sqrt,
                                             scale=1.0 / HD, bias=mem.vec[:, 63:64]).then_inc(rooted, 1)
                    if not last:
                        W.split_hi(act, n + 1, 1)
                    act.wait_ge(W.used[1], n + 1)
                    if later(n, 2):
                        if k2 in (Q, K):
                            act.wait_ge(normed, n - 1)
                        if k2 in (V, U):
                            act.wait_ge(turned, n - (first_turned + 1))
                        if k2 == U:
                            act.wait_ge(u_placed, n - (KIND_START[U] + 1))
                        if k2 == GATE and later(n, KIND_START[GATE] + 2):
                            act.wait_ge(kept[p], 32 * 8 + (i - KIND_START[GATE] // 2) * 16)
                    out = by_halves(res[p][:, :])
                    if kind == GATE:
                        nc.scalar.activation(out, halves(mm_banks[p]), ACT.Sigmoid).then_inc(res_made, 1)
                    else:
                        nc.scalar.copy(out, halves(mm_banks[p])).then_inc(res_made, 1)
                    if kind in (Q, K):
                        act.wait_ge(res_made, n + 1)
                        if later(n):
                            act.wait_ge(summed, n)
                        nc.scalar.square(sq[:, :], res[p][:, :]).then_inc(squared, 1)
                    if k1 in (K, V, U) and later(n, first_turned + 1):
                        to_natural(n - 1, i, p, k1)

                def to_natural(n, i, p, kind):
                    act.wait_ge(turned, n - (first_turned - 1))
                    q = 1 - p
                    if kind == V:
                        cols = bass.ds((n - KIND_START[V]) * P, P)
                        nc.scalar.copy(mem.v_nat[:, :, cols], ps[:, 6, :].rearrange("p (b c) -> p b c", c=P))
                        nc.scalar.copy(mem.v_new[:, cols], ps[0:NSAMP, 7, 0:P]).then_inc(nat_made, 1)
                        return
                    pair = i - q if isinstance(i, int) else i - q
                    before = pair - KIND_START[K] // 2 if kind == K else pair - KIND_START[U] // 2 + 4
                    if not isinstance(before, int) or before > 0:
                        act.wait_ge(kept[q], before * 32)
                    if kind == K:
                        nc.scalar.copy(nat[q][:, :, :], ps[:, 6, :].rearrange("p (b c) -> p b c", c=P))
                    else:
                        nc.scalar.copy(nat[q][:, 0, :], ps[:, 6, 0:P])
                    nc.scalar.copy(nat_s[q][:, :], ps[0:NSAMP, 7, 0:P]).then_inc(nat_made, 1)

                for b in range(2):
                    W.split_hi(act, 0, b)
                for_each(act, step)

            @block.vector
            def _(dve):
                def step(n, i, p, kind, k1, k2):
                    last = isinstance(n, int) and n == IN_TILES - 1
                    if not last:
                        W.split_lo(dve, n + 1, 0)
                    q = 1 - p
                    if later(n) and k1 in (Q, K):
                        dve.wait_ge(rooted, n)
                        if later(n, 2):
                            dve.wait_ge(normed, n - 1)
                        nc.vector.reciprocal(inv[:, :], root[:, :]).then_inc(inverted, 1)
                        dve.wait_ge(inverted, n)
                        g = mem.vec[:, (V_QG, V_KG)[k1]:(V_QG, V_KG)[k1] + 1]
                        m = n - (KIND_START[k1] + 1)
                        to = (mem.qT, mem.kT)[k1][:, bass.ds(m, 1), :].rearrange("p a t -> p (a t)")
                        first = nc.vector.scalar_tensor_tensor(out=to, in0=res[q][:, :], scalar=g, in1=inv[:, :],
                                                               op0=ALU.mult, op1=ALU.mult)
                        if k1 == Q:
                            first.then_inc(normed, 1)
                        else:
                            if later(n, first_turned + 3):
                                dve.wait_ge(turned, n - (first_turned + 2))
                            nc.vector.scalar_tensor_tensor(out=kn[q][:, :], in0=res[q][:, :], scalar=g, in1=inv[:, :],
                                                           op0=ALU.mult, op1=ALU.mult).then_inc(normed, 1)
                    if later(n) and k1 == U:
                        dve.wait_ge(res_made, n)
                        m = bass.ds(n - (KIND_START[U] + 1), 1)
                        nc.vector.tensor_copy(mem.uT[:, m, HIST:HIST + SEQ], res[q][:, 0:SEQ].unsqueeze(1))
                        nc.vector.tensor_copy(
                            mem.uT[:, m, HIST + SEQ:UW].rearrange("p a (b s) -> p (a b) s", b=NB)[:, :, HIST:SEG],
                            res[q][:, SEQ:T].rearrange("p (b t) -> p b t", b=NB)).then_inc(u_placed, 1)
                    if not last:
                        W.split_lo(dve, n + 1, 1)

                nc.vector.memset(mem.vec[:, 63:64], EPS)
                for b in range(2):
                    W.split_lo(dve, 0, b)
                for_each(dve, step)



def attend_prompt(nc, mem, ps, a):
    with ExitStack() as ctx:
        sem = lambda name: ctx.enter_context(nc.semaphore("c_" + name))
        (mask, zb0, zb1, soft, sp0, sp1, ks0, ks1, qs0, qs1, vs0, vs1, vn0, vn1, bs0, bs1, win0, win1, state), end = mem.run(
            mem.after_qkv, ("c_mask", [P, SCORES], F32), ("c_zb0", [P, SCORES], F32), ("c_zb1", [P, SCORES], F32),
            ("c_soft", [P, SCORES], F32), ("c_sp0", [P, SCORES], F32), ("c_sp1", [P, SCORES], F32),
            ("c_ks0", [P, SEQ + P], F32), ("c_ks1", [P, SEQ + P], F32), ("c_qs0", [P, T], F32), ("c_qs1", [P, T], F32),
            ("c_vs0", [P, SEQ // P, P], F32), ("c_vs1", [P, SEQ // P, P], F32),
            ("c_vn0", [NSAMP, P], F32), ("c_vn1", [NSAMP, P], F32), ("c_bs0", [P, 2], F32), ("c_bs1", [P, 2], F32),
            ("c_win0", [P, UW], F32), ("c_win1", [P, UW], F32), ("c_state", [NB * HIST, PW], F32))
        assert end <= mem.top_o, (end, mem.top_o)
        zb, sp_, ks, qs, vs, vn, bs = (zb0, zb1), (sp0, sp1), (ks0, ks1), (qs0, qs1), (vs0, vs1), (vn0, vn1), (bs0, bs1)
        state_in, mask_in, state_turned, u_ready, padded = (
            sem("state_in"), sem("mask_in"), sem("state_turned"), sem("u_ready"), sem("padded"))
        staged, scored, biased, softened, summands = (
            sem("staged"), sem("scored"), sem("biased"), sem("softened"), sem("summands"))
        summed, decayed, weighted, applied, o_kept = (
            sem("summed"), sem("decayed"), sem("weighted"), sem("applied"), sem("o_kept"))
        sp_made, zeroed, pool_step = sem("sp_made"), sem("zeroed"), sem("pool_step")
        z_ps = ps[:, 0:3, :].rearrange("p b c -> p (b c)")
        cum_ps = ps[:, 3:6, :].rearrange("p b c -> p (b c)")
        heads = lambda eng, body: (body(0), _loop(eng, 1, H // 4 - 1, body), body(H // 4 - 1))

        with nc.Block(no_gpsimd_drain=True) as block:

            @block.sync
            def _(sp):
                sp.dma_start(state[:, :], a["state_pool"][0].rearrange("b r c -> (b r) c")).then_inc(state_in, 16)
                sp.dma_start(mask[:, :], a["mask"]).then_inc(mask_in, 16)

            @block.tensor
            def _(pe):
                pe.wait_ge(state_in, 16)
                for m in range(PT):
                    tr = nc.tensor.transpose(ps[:, 6 + m // 4, m % 4 * P:m % 4 * P + NB * HIST],
                                             state[:, m * P:(m + 1) * P], mem.c(C_IDENT, NB * HIST, NB * HIST))
                tr.then_inc(state_turned, 1)

                def score(j, u):
                    pair, e = u // 2 % 2, HD * (u % 2)
                    pe.wait_ge(staged, j_pair(j, u) + 1)
                    if later(j):
                        pe.wait_ge(biased, j)
                    for col, kb in SCORE_SEGS:
                        nc.tensor.matmul(z_ps[:, col:col + SEQ - kb * P], ks[pair][e:e + HD, kb * P:(kb + 1) * P],
                                         qs[pair][e:e + HD, kb * P:SEQ], start=True, stop=True)
                    nc.tensor.matmul(z_ps[:, SAMPLE_COL:SCORES], ks[pair][e:e + HD, SEQ:SEQ + P],
                                     qs[pair][e:e + HD, SEQ:T], start=True, stop=True).then_inc(scored, 1)

                def accumulate(j, u):
                    pe.wait_ge(sp_made, j + 1)
                    if later(j):
                        pe.wait_ge(decayed, j)
                    src = sp_[u % 2]
                    for col, kb in SCORE_SEGS:
                        for col2, kb2 in sorted(SCORE_SEGS, key=lambda x: x[1]):
                            if kb2 >= kb:
                                nc.tensor.matmul(cum_ps[:, col + (kb2 - kb) * P:col + SEQ - kb * P],
                                                 mem.c(C_TRI if kb2 == kb else C_ONES),
                                                 src[:, col2:col2 + SEQ - kb2 * P], start=kb2 == kb, stop=kb2 == 3)
                    nc.tensor.matmul(cum_ps[:, SAMPLE_COL:SCORES], mem.c(C_TRI), src[:, SAMPLE_COL:SCORES],
                                     start=True, stop=True).then_inc(summed, 1)

                def apply(j, u):
                    pair, e = u // 2 % 2, HD * (u % 2)
                    pe.wait_ge(weighted, j + 1)
                    if e == 0 and later(j):
                        pe.wait_ge(o_kept, j_pair(j, u))
                    w = sp_[u % 2]
                    for col, kb in sorted(SCORE_SEGS, key=lambda x: x[1]):
                        nc.tensor.matmul(ps[e:e + HD, 6, kb * P:SEQ], vs[pair][:, kb, e:e + HD],
                                         w[:, col:col + SEQ - kb * P], start=kb == 0, stop=kb == 3)
                    nc.tensor.matmul(ps[e:e + HD, 7, 0:NSAMP], vn[pair][:, e:e + HD],
                                     w[0:NSAMP, SAMPLE_COL:SCORES], start=True, stop=True).then_inc(applied, 1)

                def body(i):
                    for u in range(4):
                        j = i * 4 + u
                        if not (isinstance(i, int) and j == H - 1):
                            score(j + 1, u + 1)
                        if later(j):
                            apply(j - 1, u - 1)
                        accumulate(j, u)

                pe.wait_ge(padded, 1)
                pe.wait_ge(u_ready, 1)
                score(0, 0)
                heads(pe, body)
                apply(H - 1, 3)

            @block.scalar
            def _(act):
                def softplus_tail(j, u):
                    act.wait_ge(biased, j + 1)
                    if later(j):
                        act.wait_ge(sp_made, j)
                    nc.scalar.activation(soft[:, :], zb[u % 2][:, :], ACT.Abs).then_inc(softened, 1)
                    act.wait_ge(softened, j * 3 + 1)
                    nc.scalar.activation(soft[:, :], soft[:, :], ACT.Exp, scale=-1.0).then_inc(softened, 1)
                    act.wait_ge(softened, j * 3 + 2)
                    nc.scalar.activation(soft[:, :], soft[:, :], ACT.Ln, bias=1.0).then_inc(softened, 1)

                def weight(j, u):
                    act.wait_ge(decayed, j + 1)
                    nc.scalar.activation(sp_[u % 2][:, :], zb[u % 2][:, :], ACT.Exp).then_inc(weighted, 1)

                def keep(j, u):
                    act.wait_ge(applied, j + 1)
                    r = bass.ds(j_pair(j, u), 1)
                    nc.scalar.copy(mem.oT[:, r, 0:SEQ], ps[:, 6, :].unsqueeze(1))
                    nc.scalar.copy(mem.oT[:, r, SEQ:T], ps[:, 7, 0:NSAMP].unsqueeze(1)).then_inc(o_kept, 1)

                def body(i):
                    for u in range(4):
                        j = i * 4 + u
                        if not (isinstance(i, int) and j == H - 1):
                            softplus_tail(j + 1, u + 1)
                        if u % 2 == 0 and later(j, 2):
                            keep(j - 1, u - 1)
                        weight(j, u)

                act.preload_act_table_set("natural_log_exp_and_others")
                softplus_tail(0, 0)
                heads(act, body)
                keep(H - 1, 3)

            @block.vector
            def _(dve):
                for b in range(2):
                    nc.vector.memset(ks[b][:, SEQ + NSAMP:], 0.0)
                nc.vector.memset(mem.uT[:, :, 0:HIST], 0.0).then_inc(padded, 1)
                dve.wait_ge(state_turned, 1)
                for m in range(PT):
                    cp = nc.vector.tensor_copy(
                        mem.uT[:, m, HIST + SEQ:UW].rearrange("p (b s) -> p b s", b=NB)[:, :, 0:HIST],
                        ps[:, 6 + m // 4, m % 4 * P:m % 4 * P + NB * HIST].rearrange("p (b s) -> p b s", b=NB))
                cp.then_inc(u_ready, 1)
                dve.wait_ge(mask_in, 16)

                def bias(j, u):
                    dve.wait_ge(scored, j + 1)
                    if later(j, 2):
                        dve.wait_ge(weighted, j - 1)
                    nc.vector.scalar_tensor_tensor(out=zb[u % 2][:, :], in0=z_ps[:, 0:SCORES],
                                                   scalar=bs[u // 2 % 2][:, u % 2:u % 2 + 1], in1=mask[:, :],
                                                   op0=ALU.add, op1=ALU.add).then_inc(biased, 1)

                def softplus(j, u):
                    dve.wait_ge(softened, j * 3 + 3)
                    if later(j, 2):
                        dve.wait_ge(applied, j - 1)
                    nc.vector.scalar_tensor_tensor(out=sp_[u % 2][:, :], in0=zb[u % 2][:, :], scalar=0.0,
                                                   in1=soft[:, :], op0=ALU.max, op1=ALU.add).then_inc(sp_made, 1)
                    dve.wait_ge(sp_made, j + 1)
                    nc.vector.tensor_copy(
                        mem.carry[:, :, :].rearrange("p b (h t) -> p b h t", t=NT)[:, :, bass.ds(j, 1), :],
                        sp_[u % 2][:, SAMPLE_COL:SCORES].rearrange("p (b t) -> p b t", t=NT).unsqueeze(2))

                def decay(j, u):
                    dve.wait_ge(summed, j + 1)
                    nc.vector.tensor_tensor(zb[u % 2][:, :], zb[u % 2][:, :], cum_ps[:, 0:SCORES],
                                            ALU.subtract).then_inc(decayed, 1)

                def body(i):
                    for u in range(4):
                        j = i * 4 + u
                        if not (isinstance(i, int) and j == H - 1):
                            bias(j + 1, u + 1)
                            softplus(j + 1, u + 1)
                        decay(j, u)

                bias(0, 0)
                softplus(0, 0)
                heads(dve, body)

            @block.gpsimd
            def _(pool):
                def stage(r):
                    q = r % 2
                    if r >= 2:
                        pool.wait_ge(applied, 2 * (r - 1))
                    nc.gpsimd.tensor_copy(bs[q][:, :], mem.bias[:, 2 * r:2 * r + 2])
                    nc.gpsimd.tensor_copy(qs[q][:, :], mem.qT[:, r, :])
                    nc.gpsimd.tensor_copy(ks[q][:, 0:T], mem.kT[:, r, :])
                    nc.gpsimd.tensor_copy(vs[q][:, :, :], mem.v_nat[:, :, r * P:(r + 1) * P])
                    nc.gpsimd.tensor_copy(vn[q][:, :], mem.v_new[:, r * P:(r + 1) * P]).then_inc(staged, 1)

                steps = [0]

                def link(ins):
                    steps[0] += 1
                    ins.then_inc(pool_step, 1)
                    pool.wait_ge(pool_step, steps[0])

                def new_tokens(x, part):
                    if part == 0:
                        return x[:, HIST:HIST + SEQ]
                    return x[:, HIST + SEQ:UW].rearrange("p (b s) -> p b s", b=NB)[:, :, HIST:SEG]

                def pool_tile(m):
                    g = m * P // (PW // len(WINDOWS))
                    w = WINDOWS[g]
                    src, bufs, n, first = mem.uT[:, m, :], (win0[:, :], win1[:, :]), 1, 0
                    turn = 0
                    while n < w:
                        first += n
                        link(nc.gpsimd.tensor_tensor(bufs[turn][:, first:UW], src[:, first:UW],
                                                     src[:, first - n:UW - n], ALU.add))
                        src, turn, n = bufs[turn], 1 - turn, 2 * n
                    corr = mem.const[:, C_CORR + 16 * g:C_CORR + 16 * g + 16]
                    link(nc.gpsimd.tensor_tensor(src[:, HIST:HIST + 16], src[:, HIST:HIST + 16], corr, ALU.mult))
                    link(nc.gpsimd.tensor_scalar(bufs[turn][:, HIST:UW], src[:, HIST:UW], 1.0 / w, None, ALU.mult))
                    link(nc.gpsimd.tensor_tensor(src[:, HIST:UW], bufs[turn][:, HIST:UW], mem.uT[:, m, HIST:UW],
                                                 ALU.subtract))
                    for part, (t0, t1) in enumerate(((0, SEQ), (SEQ, T))):
                        to = [x[:, m, t0:t1] if part == 0 else x[:, m, t0:t1].rearrange("p (b t) -> p b t", b=NB)
                              for x in (mem.pool_hi, mem.pool_lo)]
                        link(nc.gpsimd.tensor_copy(to[0], new_tokens(src, part)))
                        link(nc.gpsimd.tensor_tensor(to[1], new_tokens(src, part), to[0].bitcast(F32), ALU.subtract))

                pool.wait_ge(padded, 1)
                stage(0)
                stage(1)
                pool.wait_ge(u_ready, 1)
                for r in range(PAIRS):
                    pool_tile(r)
                    if r + 2 < PAIRS:
                        stage(r + 2)


def j_pair(j, u):
    if isinstance(j, int):
        return j // 2
    return (j - u % 2) // 2


def _loop(eng, start, stop, body):
    with eng.Fori(start, stop) as i:
        body(i)


def attend_cache(nc, mem, ps, a):
    GP = 4
    GROUPS = NPAGE // GP
    with ExitStack() as ctx:
        sem = lambda name: ctx.enter_context(nc.semaphore("d_" + name))
        specs = [(f"d_k{j}", [P, AW], F32) for j in range(GP)] + [(f"d_v{j}", [P, AW], F32) for j in range(GP)] + [
            (f"d_kt_{part}{i}", [P, PAIRS, 2 * PAGE], F32R) for part in ("hi", "lo") for i in range(2)] + [
            ("d_qb", [P, PAIRS * (P + 2 * NT)], F32R), ("d_zr", [P, GP * PAGE], F32), ("d_soft", [P, GP * HT], F32),
            ("d_zb0", [P, GP * HT], F32), ("d_zb1", [P, GP * HT], F32), ("d_sp0", [P, GP * HT], F32),
            ("d_sp1", [P, GP * HT], F32), ("d_w0", [P, GP * HT], F32), ("d_w1", [P, GP * HT], F32),
            ("d_lost0", [P, GP + 1, HT], F32), ("d_lost1", [P, GP + 1, HT], F32), ("d_zero", [P, HT], F32), ("d_oacc", [HT, AW], F32)]
        tensors, end = mem.run(mem.after_q, *specs)
        assert end <= mem.top_o, (end, mem.top_o)
        kp, vp, kt_hi, kt_lo = tensors[0:4], tensors[4:8], tensors[8:10], tensors[10:12]
        qb, zr, soft = tensors[12:15]
        zb, sp_, wt, lost = tensors[15:17], tensors[17:19], tensors[19:21], tensors[21:23]
        zero, oacc = tensors[23], tensors[24]
        zeroed = sem("zeroed")
        k_in = [sem(f"k_in{j}") for j in range(GP)]
        v_in = [sem(f"v_in{j}") for j in range(GP)]
        k_turned, kt_hi_made, kt_lo_made = sem("k_turned"), sem("kt_hi_made"), sem("kt_lo_made")
        q_hi_made, q_lo_made, q_zeroed = sem("q_hi_made"), sem("q_lo_made"), sem("q_zeroed")
        scored, rows_kept, turned, biased = sem("scored"), sem("rows_kept"), sem("turned"), sem("biased")
        softened, sp_made, lost_made = sem("softened"), sem("sp_made"), sem("lost_made")
        summed, decayed, weighted = sem("summed"), sem("decayed"), sem("weighted")
        applied, acc_kept, extracted, added = sem("applied"), sem("acc_kept"), sem("extracted"), sem("added")
        LOST_STEPS = GROUPS * GP
        LOST_BEFORE = [0] + [1 + GP * s for s in range(1, GROUPS)]

        def lost_ready(b, s):
            if s < 0:
                b, s = b - 1, s + GROUPS
            return b * LOST_STEPS + (LOST_BEFORE[s] + GP - 1 + (s == 0))

        UNITS = 2 * GP
        cache = [a[n][0].rearrange("n p h d -> n p (h d)") for n in ("cache_k", "cache_v")]
        n_pages = cache[0].shape[0]
        stride = P + 2 * NT
        q_cols = lambda e, lo: qb[e * HD:(e + 1) * HD, :].rearrange("p (a c) -> p a c", c=stride)[
            :, :, lo * HT + NT * e:lo * HT + NT * e + NT]
        q_src = lambda b, e: mem.qT[e * HD:(e + 1) * HD, :, bass.ds(b * NT + SEQ, NT)]

        with nc.Block(no_gpsimd_drain=True) as block:

            @block.sync
            def _(sp):
                def load(b, s, which):
                    g = b * GROUPS + s
                    for j in range(GP):
                        at = b * NPAGE + (NPAGE - GP * (s + 1) + j)
                        page = sp.value_load(mem.pages[0:1, bass.ds(at, 1)], min_val=0, max_val=n_pages - 1)
                        if later(g):
                            if which == 0:
                                sp.wait_ge(k_turned, (g - 1) * UNITS + (2 * j + 2))
                            else:
                                sp.wait_ge(applied, (g - 1) * GP + (j + 1))
                        sp.dma_start((kp, vp)[which][j][:, :], cache[which][bass.ds(page, 1), :, :].rearrange(
                            "a p c -> p (a c)")).then_inc((k_in, v_in)[which][j], 16)

                def body(b):
                    for s in range(GROUPS):
                        load(b, s, 0)
                        load(b, s, 1)

                body(0)
                _loop(sp, 1, NB, body)

            @block.tensor
            def _(pe):
                def turn(g, j, half, s):
                    k = 2 * j + half
                    pe.wait_ge(k_in[j], g * 16 + 16)
                    if later(g) or k >= 4:
                        pe.wait_ge(kt_lo_made, g * UNITS + (k - 3))
                    for r in range(4):
                        tr = nc.tensor.transpose(ps[:, k % 4, r * P:(r + 1) * P],
                                                 kp[j][:, (4 * half + r) * P:(4 * half + r + 1) * P], mem.c(C_IDENT))
                    tr.then_inc(k_turned, 1)

                def score(g, sub):
                    pe.wait_ge(kt_lo_made, g * UNITS + 4 * (sub + 1))
                    if later(g) or sub:
                        pe.wait_ge(rows_kept, g * 2 + sub)
                    for p in range(PAIRS):
                        for kt in (kt_hi, kt_lo):
                            mm = nc.tensor.matmul(ps[:, 4, sub * 2 * PAGE:(sub + 1) * 2 * PAGE],
                                                  qb[:, p * P:(p + 1) * P], kt[sub][:, p, :],
                                                  start=p == 0 and kt is kt_hi, stop=p == PAIRS - 1 and kt is kt_lo)
                    mm.then_inc(scored, 1)

                def turn_scores(g):
                    pe.wait_ge(rows_kept, g * 2 + 2)
                    if later(g):
                        pe.wait_ge(decayed, g)
                    for j in range(GP):
                        mm = nc.tensor.matmul(ps[:, 5, j * HT:(j + 1) * HT], zr[:, j * PAGE:(j + 1) * PAGE],
                                              mem.c(C_FOLD, P, HT), start=True, stop=True)
                    mm.then_inc(turned, 1)

                def accumulate(g, par, lost_at):
                    pe.wait_ge(sp_made, g + 1)
                    pe.wait_ge(lost_made, lost_at)
                    pe.wait_ge(biased, g + 1)
                    out = ps[:, 5, GP * HT:2 * GP * HT]
                    nc.tensor.matmul(out, mem.c(C_TRI), sp_[par][:, :], start=True, stop=False)
                    nc.tensor.matmul(out, mem.c(C_ONES), lost[par][:, 1:GP + 1, :].rearrange("p g c -> p (g c)"),
                                     start=False, stop=True).then_inc(summed, 1)

                def apply(g, par, j, s):
                    pe.wait_ge(weighted, g + 1)
                    pe.wait_ge(v_in[j], g * 16 + 16)
                    if s == 0 and j == 0 and later(g):
                        pe.wait_ge(acc_kept, g // GROUPS if isinstance(g, int) else g_batch(g))
                    for half in range(2):
                        mm = nc.tensor.matmul(ps[0:HT, 6 + half, :], wt[par][:, j * HT:(j + 1) * HT],
                                              vp[j][:, half * 512:(half + 1) * 512],
                                              start=s == 0 and j == 0, stop=s == GROUPS - 1 and j == GP - 1)
                    mm.then_inc(applied, 1)

                batch = [0]

                def g_batch(g):
                    return batch[0]

                def extract(b, wait_bank):
                    pe.wait_ge(acc_kept, b)
                    pe.wait_ge(kt_lo_made, wait_bank)
                    for p in range(PAIRS):
                        mm = nc.tensor.matmul(ps[:, 0, p * 2 * NT:(p + 1) * 2 * NT], oacc[:, p * P:(p + 1) * P],
                                              mem.c(C_IDENT + p * 2 * NT, HT, 2 * NT), start=True, stop=True)
                    mm.then_inc(extracted, 1)

                def body(b):
                    for s in range(GROUPS):
                        g = b * GROUPS + s
                        before = (s - 1) % GROUPS
                        batch[0] = b
                        for k in range(4):
                            if k == 0 and s == 1 and later(b):
                                pe.wait_ge(added, b)
                            turn(g, k // 2, k % 2, s)
                        if later(g):
                            accumulate(g - 1, (s - 1) % 2, lost_ready(b, s - 1))
                        for k in range(4, UNITS):
                            turn(g, k // 2, k % 2, s)
                        if s == 0:
                            pe.wait_ge(q_lo_made, b + 1)
                        score(g, 0)
                        if later(g):
                            for j in range(2):
                                apply(g - 1, (s - 1) % 2, j, before)
                        score(g, 1)
                        if later(g):
                            for j in range(2, GP):
                                apply(g - 1, (s - 1) % 2, j, before)
                        turn_scores(g)
                        if s == 0 and later(b):
                            extract(b, g * UNITS + 5)

                body(0)
                _loop(pe, 1, NB, body)
                g = NB * GROUPS - 1
                accumulate(g, g % 2, NB * LOST_STEPS)
                for j in range(GP):
                    apply(g, g % 2, j, GROUPS - 1)
                extract(NB, (g + 1) * UNITS)

            @block.scalar
            def _(act):
                def part_keys(g, k):
                    j, half = k // 2, k % 2
                    act.wait_ge(k_turned, g * UNITS + k + 1)
                    if k % 4 == 0 and later(g):
                        act.wait_ge(scored, (g - 1) * 2 + k // 4 + 1)
                    nc.scalar.copy(kt_hi[j // 2][:, 4 * half:4 * half + 4, j % 2 * PAGE:(j % 2 + 1) * PAGE],
                                   ps[:, k % 4, :].rearrange("p (r c) -> p r c", c=P)).then_inc(kt_hi_made, 1)

                def keep_rows(g, sub):
                    act.wait_ge(scored, g * 2 + sub + 1)
                    if later(g):
                        act.wait_ge(turned, g)
                    cols = slice(sub * 2 * PAGE, (sub + 1) * 2 * PAGE)
                    nc.scalar.copy(zr[:, cols], ps[:, 4, cols]).then_inc(rows_kept, 1)

                def softplus_tail(g, par):
                    act.wait_ge(biased, g + 1)
                    if later(g):
                        act.wait_ge(sp_made, g)
                    nc.scalar.activation(soft[:, :], zb[par][:, :], ACT.Abs).then_inc(softened, 1)
                    act.wait_ge(softened, g * 3 + 1)
                    nc.scalar.activation(soft[:, :], soft[:, :], ACT.Exp, scale=-1.0).then_inc(softened, 1)
                    act.wait_ge(softened, g * 3 + 2)
                    nc.scalar.activation(soft[:, :], soft[:, :], ACT.Ln, bias=1.0).then_inc(softened, 1)

                def weight(g, par):
                    act.wait_ge(decayed, g + 1)
                    if later(g, 2):
                        act.wait_ge(applied, (g - 1) * GP)
                    nc.scalar.activation(wt[par][:, :], zb[par][:, :], ACT.Exp).then_inc(weighted, 1)

                def keep_acc(b):
                    act.wait_ge(applied, b * NPAGE)
                    if later(b, 2):
                        act.wait_ge(extracted, b - 1)
                    nc.scalar.copy(oacc[:, :], ps[0:HT, 6:8, :].rearrange("p b c -> p (b c)")).then_inc(acc_kept, 1)

                def body(b):
                    for s in range(GROUPS):
                        g = b * GROUPS + s
                        for k in range(6):
                            part_keys(g, k)
                            if s == 0 and k == 0:
                                if later(b):
                                    act.wait_ge(scored, b * (2 * GROUPS))
                                else:
                                    act.wait_ge(q_zeroed, 1)
                                for e in range(2):
                                    cp = nc.scalar.copy(q_cols(e, 0), q_src(b, e))
                                cp.then_inc(q_hi_made, 1)
                        if later(g):
                            weight(g - 1, (s - 1) % 2)
                        for k in range(6, UNITS):
                            part_keys(g, k)
                        for sub in range(2):
                            keep_rows(g, sub)
                        if s == 0 and later(b):
                            keep_acc(b)
                        softplus_tail(g, s % 2)

                act.preload_act_table_set("natural_log_exp_and_others")
                body(0)
                _loop(act, 1, NB, body)
                weight(NB * GROUPS - 1, 1)
                keep_acc(NB)

            @block.vector
            def _(dve):
                def part_keys(g, k):
                    j, half = k // 2, k % 2
                    dve.wait_ge(kt_hi_made, g * UNITS + k + 1)
                    at = (slice(None), slice(4 * half, 4 * half + 4), slice(j % 2 * PAGE, (j % 2 + 1) * PAGE))
                    nc.vector.tensor_tensor(kt_lo[j // 2][at], ps[:, k % 4, :].rearrange("p (r c) -> p r c", c=P),
                                            kt_hi[j // 2][at].bitcast(F32), ALU.subtract).then_inc(kt_lo_made, 1)

                def decay(g, par):
                    dve.wait_ge(summed, g + 1)
                    nc.vector.tensor_tensor(zb[par][:, :], zb[par][:, :], ps[:, 5, GP * HT:2 * GP * HT],
                                            ALU.subtract).then_inc(decayed, 1)

                def bias(g, par):
                    dve.wait_ge(turned, g + 1)
                    if later(g, 2):
                        dve.wait_ge(weighted, g - 1)
                    nc.vector.tensor_tensor(
                        zb[par][:, :].rearrange("p (j c) -> p j c", j=GP),
                        ps[:, 5, 0:GP * HT].rearrange("p (j c) -> p j c", j=GP),
                        mem.biasT[:, :, :].rearrange("p h t -> p (h t)").unsqueeze(1).to_broadcast([P, GP, HT]),
                        ALU.add).then_inc(biased, 1)

                def softplus(g, par, b, s):
                    dve.wait_ge(softened, g * 3 + 3)
                    if later(g, 2):
                        dve.wait_ge(summed, g - 1)
                        dve.wait_ge(lost_made, lost_ready(b, s - 2) + (s != 1))
                    nc.vector.scalar_tensor_tensor(out=sp_[par][:, :], in0=zb[par][:, :], scalar=0.0, in1=soft[:, :],
                                                   op0=ALU.max, op1=ALU.add).then_inc(sp_made, 1)

                def add(b):
                    dve.wait_ge(extracted, b)
                    for e in range(2):
                        to = mem.oT[e * HD:(e + 1) * HD, :, bass.ds(b * NT + (SEQ - NT), NT)]
                        op = nc.vector.tensor_tensor(to, ps[e * HD:(e + 1) * HD, 0, 0:PAIRS * 2 * NT].rearrange(
                            "p (a c) -> p a c", c=2 * NT)[:, :, e * NT:(e + 1) * NT], to, ALU.add)
                    op.then_inc(added, 1)

                def body(b):
                    for s in range(GROUPS):
                        g = b * GROUPS + s
                        for k in range(4):
                            part_keys(g, k)
                            if s == 0 and k == 0:
                                dve.wait_ge(q_hi_made, b + 1)
                                for e in range(2):
                                    op = nc.vector.tensor_tensor(q_cols(e, 1), q_src(b, e), q_cols(e, 0).bitcast(F32),
                                                                 ALU.subtract)
                                op.then_inc(q_lo_made, 1)
                        if later(g):
                            decay(g - 1, (s - 1) % 2)
                        for k in range(4, UNITS):
                            part_keys(g, k)
                        bias(g, s % 2)
                        if s == 0 and later(b):
                            add(b)
                        softplus(g, s % 2, b, s)

                nc.vector.memset(qb[:, :].bitcast(F32), 0.0).then_inc(q_zeroed, 1)
                dve.wait_ge(q_zeroed, 1)
                body(0)
                _loop(dve, 1, NB, body)
                decay(NB * GROUPS - 1, 1)
                add(NB)

            @block.gpsimd
            def _(pool):
                def lose(b, s):
                    g = b * GROUPS + s
                    par = s % 2
                    done = b * LOST_STEPS + LOST_BEFORE[s]
                    pool.wait_ge(sp_made, g + 1)
                    if later(g):
                        pool.wait_ge(summed, g)
                    if later(g):
                        pool.wait_ge(lost_made, done)
                    if s == 0:
                        nc.gpsimd.tensor_tensor(lost[0][:, GP, :],
                                                mem.carry[:, bass.ds(b, 1), :].rearrange("p a c -> p (a c)"),
                                                zero[:, :], ALU.add).then_inc(lost_made, 1)
                        done += 1
                    for i, j in enumerate(range(GP - 1, -1, -1)):
                        if j == 0 and s == GROUPS - 1:
                            break
                        to = lost[par][:, j, :] if j else lost[1 - par][:, GP, :]
                        pool.wait_ge(lost_made, done + i)
                        nc.gpsimd.tensor_tensor(to, lost[par][:, j + 1, :],
                                                sp_[par][:, j * HT:(j + 1) * HT], ALU.add).then_inc(lost_made, 1)

                nc.gpsimd.memset(zero[:, :], 0.0).then_inc(zeroed, 1)
                pool.wait_ge(zeroed, 1)
                def body(b):
                    for s in range(GROUPS):
                        lose(b, s)

                body(0)
                _loop(pool, 1, NB, body)


def merge_branches(nc, mem, ps, a, scratch):
    with ExitStack() as ctx:
        sem = lambda name: ctx.enter_context(nc.semaphore("e_" + name))
        W = Weights(nc, ctx, mem, "e", mem.after_mix)
        specs = [("e_o_hi", [P, PAIRS, T], F32R), ("e_o_lo", [P, PAIRS, T], F32R)] + [
            (f"e_{n}{i}", [P, T], F32) for n in ("gate_a", "gate_p", "mixed") for i in range(2)] + [
            ("e_part_a", [P, T], F32), ("e_part_p", [P, T], F32)]
        tensors, end = mem.run(W.end, *specs)
        assert end <= mem.top_o, (end, mem.top_o)
        o_hi, o_lo = tensors[0:2]
        gate_a, gate_p, mixed = tensors[2:4], tensors[4:6], tensors[6:8]
        part_a, part_p = tensors[8:10]
        o_hi_made, o_lo_made = sem("o_hi_made"), sem("o_lo_made")
        gates_in = [sem(f"gates_in{i}") for i in range(2)]
        gated, mixed_made, hi_made, lo_made = sem("gated"), sem("mixed_made"), sem("hi_made"), sem("lo_made")
        w_attn = a["w_attn_proj"][0].rearrange("(k p) c -> p k c", p=P)
        w_pool = a["w_pool"][0].rearrange("g (k p) c -> g p k c", p=P)
        PK = PT // len(WINDOWS)
        GM = KD // len(WINDOWS)
        KTS = (PAIRS, PK)
        banks = [[ps[:, 4 * p + 2 * i:4 * p + 2 * i + 2, :] for i in range(2)] for p in range(2)]
        groups = lambda eng, body: (body(0), _loop(eng, 1, len(WINDOWS) - 1, body), body(len(WINDOWS) - 1))
        last = lambda m: isinstance(m, int) and m == KD - 1

        with nc.Block(no_gpsimd_drain=True) as block:

            @block.sync
            def _(sp):
                def load(m, g, j):
                    W.load(sp, m, 0, w_attn[:, :, bass.ds(m * P, P)], PAIRS)
                    W.load(sp, m, 1, w_pool[bass.ds(g, 1), :, :, j * P:(j + 1) * P].rearrange("g p k c -> p (g k) c"), PK)
                    for buf, first in ((gate_a, 0), (gate_p, KD)):
                        if later(m, 2):
                            sp.wait_ge(mixed_made, m - 1)
                        sp.dma_start(buf[j % 2][:, :].unsqueeze(1), scratch["gates"][bass.ds(m + first, 1), :, :].rearrange(
                            "a p t -> p a t")).then_inc(gates_in[j % 2], 16)

                def body(g):
                    for j in range(GM):
                        load(g * GM + j, g, j)

                groups(sp, body)

            @block.tensor
            def _(pe):
                def body(g):
                    for j in range(GM):
                        m, p = g * GM + j, j % 2
                        if later(m, 2):
                            pe.wait_ge(gated, 2 * (m - 1))
                        if isinstance(m, int) and m == 0:
                            for k in range(PAIRS):
                                pe.wait_ge(o_lo_made, k + 1)
                                first_part(k)
                        else:
                            W.multiply(pe, m, 0, banks[p][0], tile_of(o_hi), tile_of(o_lo), 0, PAIRS)
                        group_tile = lambda x: lambda k, half: x[:, bass.ds(g * PK + k, 1), half * HALF:(half + 1) * HALF]
                        W.multiply(pe, m, 1, banks[p][1], group_tile(mem.pool_hi), group_tile(mem.pool_lo), 0, PK)

                def first_part(k):
                    pe.wait_ge(W.lo_made[0], 1)
                    for i, (w, x) in enumerate(((W.hi, o_hi), (W.hi, o_lo), (W.lo, o_hi))):
                        for half in range(2):
                            mm = nc.tensor.matmul(banks[0][0][:, half, 0:HALF], w[0][:, k, :],
                                                  x[:, k, half * HALF:(half + 1) * HALF],
                                                  start=k == 0 and i == 0, stop=k == PAIRS - 1 and i == 2)
                    if k == PAIRS - 1:
                        mm.then_inc(W.used[0], 1)

                groups(pe, body)

            @block.scalar
            def _(act):
                def body(g):
                    for j in range(GM):
                        m = g * GM + j
                        if not last(m):
                            for b in range(2):
                                W.split_hi(act, m + 1, b, KTS[b])
                        act.wait_ge(mixed_made, m + 1)
                        nc.scalar.copy(mem.mix_hi[:, bass.ds(m, 1), :], mixed[j % 2][:, :].unsqueeze(1)).then_inc(hi_made, 1)

                for b in range(2):
                    W.split_hi(act, 0, b, KTS[b])
                for k in range(PAIRS):
                    nc.scalar.copy(o_hi[:, k, :], mem.oT[:, k, :]).then_inc(o_hi_made, 1)
                groups(act, body)

            @block.vector
            def _(dve):
                def gate(m, p):
                    dve.wait_ge(gates_in[p], (m - p) // 2 * 32 + 32)
                    dve.wait_ge(W.used[1], m + 1)
                    if later(m):
                        dve.wait_ge(mixed_made, m)
                    nc.vector.tensor_tensor(by_halves(part_a[:, :]), halves(banks[p][0]),
                                            by_halves(gate_a[p][:, :]), ALU.mult).then_inc(gated, 1)
                    nc.vector.scalar_tensor_tensor(out=by_halves(part_p[:, :]), in0=halves(banks[p][1]),
                                                   scalar=mem.vec[:, bass.ds(m + V_PSCALE, 1)],
                                                   in1=by_halves(gate_p[p][:, :]), op0=ALU.mult,
                                                   op1=ALU.mult).then_inc(gated, 1)

                def body(g):
                    for j in range(GM):
                        m = g * GM + j
                        if not last(m):
                            for b in range(2):
                                W.split_lo(dve, m + 1, b, KTS[b])
                        gate(m, j % 2)
                        if later(m):
                            part(m - 1, 1 - j % 2)

                def part(m, p):
                    dve.wait_ge(hi_made, m + 1)
                    nc.vector.tensor_tensor(mem.mix_lo[:, bass.ds(m, 1), :], mixed[p][:, :].unsqueeze(1),
                                            mem.mix_hi[:, bass.ds(m, 1), :].bitcast(F32), ALU.subtract).then_inc(lo_made, 1)

                for b in range(2):
                    W.split_lo(dve, 0, b, KTS[b])
                for k in range(PAIRS):
                    dve.wait_ge(o_hi_made, k + 1)
                    nc.vector.tensor_tensor(o_lo[:, k, :], mem.oT[:, k, :], o_hi[:, k, :].bitcast(F32),
                                            ALU.subtract).then_inc(o_lo_made, 1)
                groups(dve, body)
                part(KD - 1, (KD - 1) % 2)

            @block.gpsimd
            def _(pool):
                def body(g):
                    for j in range(GM):
                        m = g * GM + j
                        pool.wait_ge(gated, 2 * m + 2)
                        if later(m, 2):
                            pool.wait_ge(lo_made, m - 1)
                        nc.gpsimd.tensor_tensor(mixed[j % 2][:, :], part_a[:, :], part_p[:, :], ALU.add).then_inc(mixed_made, 1)

                groups(pool, body)


def project_out(nc, mem, ps, a, scratch):
    with ExitStack() as ctx:
        sem = lambda name: ctx.enter_context(nc.semaphore("f_" + name))
        W = Weights(nc, ctx, mem, "f", mem.after_h)
        (x0, x1, sq, total), end = mem.run(W.end, ("f_x0", [P, T], F32), ("f_x1", [P, T], F32),
                                           ("f_sq", [P, T], F32), ("f_total", [P, T], F32))
        assert end <= mem.top, (end, mem.top)
        xr = (x0, x1)
        x_in = [sem(f"x_in{i}") for i in range(2)]
        h_made, hi_made, lo_made, squared, totalled = (
            sem("h_made"), sem("hi_made"), sem("lo_made"), sem("squared"), sem("totalled"))
        cleared, summed, rooted, inverted = sem("cleared"), sem("summed"), sem("rooted"), sem("inverted")
        w_out = a["w_out"][0].rearrange("(b k p) c -> b p k c", b=2, p=P)
        banks = [ps[:, 2 * p:2 * p + 2, :] for p in range(2)]
        is_last = lambda m: isinstance(m, int) and m == KD - 1

        with nc.Block(no_gpsimd_drain=True) as block:

            @block.sync
            def _(sp):
                def load(m, i, p):
                    for b in range(2):
                        W.load(sp, m, b, w_out[b][:, :, bass.ds(m * P, P)])
                    if later(m, 2):
                        sp.wait_ge(h_made, m - 1)
                    sp.dma_start(xr[p][:, :].unsqueeze(1), scratch["xT"][bass.ds(m, 1), :, :].rearrange(
                        "a p t -> p a t")).then_inc(x_in[p], 16)

                by_pairs(sp, 0, KD, load)

            @block.tensor
            def _(pe):
                def step(m, i, p):
                    if later(m, 2):
                        pe.wait_ge(h_made, m - 1)
                    for b in range(2):
                        W.multiply(pe, m, b, banks[p], tile_of(mem.mix_hi), tile_of(mem.mix_lo), b * W.KT,
                                   start=b == 0, stop=b == 1)

                by_pairs(pe, 0, KD, step)
                pe.wait_ge(totalled, KD)
                for half in range(2):
                    mm = nc.tensor.matmul(ps[:, 4 + half, 0:HALF], mem.c(C_ONES), total[:, half * HALF:(half + 1) * HALF],
                                          start=True, stop=True)
                mm.then_inc(summed, 1)

            @block.scalar
            def _(act):
                def step(m, i, p):
                    if not is_last(m):
                        for b in range(2):
                            W.split_hi(act, m + 1, b)
                    act.wait_ge(h_made, m + 1)
                    if later(m):
                        act.wait_ge(totalled, m)
                    h = mem.hT[:, bass.ds(m, 1), :]
                    nc.scalar.activation(mem.hn_hi[:, bass.ds(m, 1), :], h, ACT.Copy,
                                         scale=mem.vec[:, bass.ds(m + V_NORM2, 1)]).then_inc(hi_made, 1)
                    nc.scalar.square(sq[:, :].unsqueeze(1), h).then_inc(squared, 1)

                for b in range(2):
                    W.split_hi(act, 0, b)
                by_pairs(act, 0, KD, step, tail=2)
                act.wait_ge(summed, 1)
                nc.scalar.activation(by_halves(total[:, :]), ps[:, 4:6, 0:HALF], ACT.Sqrt, scale=1.0 / D,
                                     bias=mem.vec[:, 63:64]).then_inc(rooted, 1)

            @block.vector
            def _(dve):
                def step(m, i, p):
                    if not is_last(m):
                        for b in range(2):
                            W.split_lo(dve, m + 1, b)
                    dve.wait_ge(x_in[p], i * 16 + 16)
                    dve.wait_ge(W.used[1], m + 1)
                    nc.vector.tensor_tensor(by_halves(mem.hT[:, bass.ds(m, 1), :].rearrange("p a t -> p (a t)")),
                                            halves(banks[p]), by_halves(xr[p][:, :]), ALU.add).then_inc(h_made, 1)
                    dve.wait_ge(hi_made, m + 1)
                    nc.vector.scalar_tensor_tensor(out=mem.hn_lo[:, bass.ds(m, 1), :], in0=mem.hT[:, bass.ds(m, 1), :],
                                                   scalar=mem.vec[:, bass.ds(m + V_NORM2, 1)],
                                                   in1=mem.hn_hi[:, bass.ds(m, 1), :].bitcast(F32),
                                                   op0=ALU.mult, op1=ALU.subtract).then_inc(lo_made, 1)

                for b in range(2):
                    W.split_lo(dve, 0, b)
                by_pairs(dve, 0, KD, step, tail=2)
                dve.wait_ge(rooted, 1)
                nc.vector.reciprocal(mem.rstd2[:, :], total[:, :]).then_inc(inverted, 1)

            @block.gpsimd
            def _(pool):
                nc.gpsimd.memset(total[:, :], 0.0).then_inc(cleared, 1)
                pool.wait_ge(cleared, 1)

                def step(m, i, p):
                    pool.wait_ge(squared, m + 1)
                    if later(m):
                        pool.wait_ge(totalled, m)
                    nc.gpsimd.tensor_tensor(total[:, :], total[:, :], sq[:, :], ALU.add).then_inc(totalled, 1)

                by_pairs(pool, 0, KD, step)


def feed_forward(nc, mem, ps, a):
    SLOTS = 2 * CF + KD
    DOWN = (6, CF - 6)
    FULL = (Weights.KT, Weights.KT)
    with ExitStack() as ctx:
        sem = lambda name: ctx.enter_context(nc.semaphore("g_" + name))
        (act_hi, act_lo, gate, up, silu, hidden), end = mem.run(
            mem.free, ("g_act_hi", [P, CF, T], F32R), ("g_act_lo", [P, CF, T], F32R), ("g_gate", [P, T], F32),
            ("g_up", [P, T], F32), ("g_silu", [P, T], F32), ("g_hidden", [P, T], F32))
        assert end <= mem.after_mix, (end, mem.after_mix)
        W = Weights(nc, ctx, mem, "g", mem.after_h)
        assert W.end <= mem.top
        vacated = sem("vacated")
        silu_made, hidden_made, hi_made, lo_made = sem("silu_made"), sem("hidden_made"), sem("hi_made"), sem("lo_made")
        w_gu = a["w_gate_up"][0].rearrange("(b k p) c -> b p k c", b=2, p=P)
        w_down = a["w_down"][0].rearrange("(f p) c -> p f c", p=P)
        banks = [ps[:, 2 * p:2 * p + 2, :] for p in range(2)]

        def chunk(eng, c, hidden_slots, down_slot):
            hidden_slots(c, 0, FULL)
            with eng.Fori(1, CF - 1) as f:
                hidden_slots(c, f, FULL)
            hidden_slots(c, CF - 1, DOWN)
            with eng.Fori(0, KD // 2 - 1) as i:
                for p in range(2):
                    down_slot(c, i * 2 + p, p, DOWN)
            down_slot(c, KD - 2, 0, DOWN)
            down_slot(c, KD - 1, 1, None if isinstance(c, int) and c == CHUNKS - 1 else FULL)

        def chunks(eng, hidden_slots, down_slot):
            chunk(eng, 0, hidden_slots, down_slot)
            with eng.Fori(1, CHUNKS - 1) as c:
                chunk(eng, c, hidden_slots, down_slot)
            chunk(eng, CHUNKS - 1, hidden_slots, down_slot)

        hidden_n = lambda c, f, which: c * SLOTS + f * 2 + which
        down_n = lambda c, m: c * SLOTS + m + 2 * CF

        with nc.Block(no_gpsimd_drain=True) as block:

            @block.sync
            def _(sp):
                def hidden_slots(c, f, after):
                    for which in range(2):
                        for b in range(2):
                            W.load(sp, hidden_n(c, f, which), b,
                                   w_gu[b][:, :, bass.ds((c * CF + f + which * FT) * P, P)])

                def down_slot(c, m, p, after):
                    for b in range(2):
                        W.load(sp, down_n(c, m), b, w_down[:, bass.ds(c * CF + b * DOWN[0], DOWN[b]), bass.ds(m * P, P)],
                               DOWN[b])

                chunks(sp, hidden_slots, down_slot)

            @block.tensor
            def _(pe):
                def hidden_slots(c, f, after):
                    for which in range(2):
                        n = hidden_n(c, f, which)
                        if later(n, 2):
                            pe.wait_ge(vacated, n - 1)
                        for b in range(2):
                            W.multiply(pe, n, b, banks[which], tile_of(mem.hn_hi), tile_of(mem.hn_lo), b * W.KT,
                                       start=b == 0, stop=b == 1)

                def down_slot(c, m, p, after):
                    n = down_n(c, m)
                    pe.wait_ge(vacated, n - 1)
                    for b in range(2):
                        pe.wait_ge(lo_made, c * CF + (DOWN[0] if b == 0 else CF))
                        W.multiply(pe, n, b, banks[p], tile_of(act_hi), tile_of(act_lo), b * DOWN[0], DOWN[b],
                                   start=b == 0, stop=b == 1)

                chunks(pe, hidden_slots, down_slot)

            @block.scalar
            def _(act):
                def split_next(n, after):
                    if after is not None:
                        for b in range(2):
                            W.split_hi(act, n + 1, b, after[b])

                def hidden_slots(c, f, after):
                    n, h = hidden_n(c, f, 0), c * CF + f
                    split_next(n, FULL)
                    act.wait_ge(vacated, n + 1)
                    if later(h):
                        act.wait_ge(hidden_made, h)
                    nc.scalar.activation(silu[:, :], gate[:, :], ACT.Silu).then_inc(silu_made, 1)
                    split_next(n + 1, after)
                    act.wait_ge(hidden_made, h + 1)
                    if later(c):
                        act.wait_ge(W.used[1], c * SLOTS)
                    nc.scalar.copy(act_hi[:, bass.ds(f, 1), :], hidden[:, :].unsqueeze(1)).then_inc(hi_made, 1)

                def down_slot(c, m, p, after):
                    split_next(down_n(c, m), after)

                for b in range(2):
                    W.split_hi(act, 0, b)
                chunks(act, hidden_slots, down_slot)

            @block.vector
            def _(dve):
                def split_next(n, after):
                    if after is not None:
                        for b in range(2):
                            W.split_lo(dve, n + 1, b, after[b])

                def scale(n, p, to):
                    dve.wait_ge(W.used[1], n + 1)
                    nc.vector.tensor_tensor(by_halves(to[:, :]), halves(banks[p]), by_halves(mem.rstd2[:, :]),
                                            ALU.mult).then_inc(vacated, 1)

                def hidden_slots(c, f, after):
                    n, h = hidden_n(c, f, 0), c * CF + f
                    split_next(n, FULL)
                    if later(h):
                        dve.wait_ge(silu_made, h)
                    scale(n, 0, gate)
                    split_next(n + 1, after)
                    if later(h):
                        dve.wait_ge(hidden_made, h)
                    scale(n + 1, 1, up)
                    dve.wait_ge(silu_made, h + 1)
                    dve.wait_ge(vacated, n + 2)
                    if later(h):
                        dve.wait_ge(lo_made, h)
                    nc.vector.tensor_tensor(hidden[:, :], silu[:, :], up[:, :], ALU.mult).then_inc(hidden_made, 1)
                    dve.wait_ge(hi_made, h + 1)
                    nc.vector.tensor_tensor(act_lo[:, bass.ds(f, 1), :], hidden[:, :].unsqueeze(1),
                                            act_hi[:, bass.ds(f, 1), :].bitcast(F32), ALU.subtract).then_inc(lo_made, 1)

                def down_slot(c, m, p, after):
                    n = down_n(c, m)
                    split_next(n, after)
                    dve.wait_ge(W.used[1], n + 1)
                    if later(c):
                        dve.wait_ge(vacated, c * SLOTS)
                    h = by_halves(mem.hT[:, bass.ds(m, 1), :].rearrange("p a t -> p (a t)"))
                    nc.vector.tensor_tensor(h, halves(banks[p]), h, ALU.add).then_inc(vacated, 1)

                for b in range(2):
                    W.split_lo(dve, 0, b)
                chunks(dve, hidden_slots, down_slot)


def store_outputs(nc, mem, ps, o):
    with ExitStack() as ctx:
        sem = lambda name: ctx.enter_context(nc.semaphore("h_" + name))
        SIDE = 4
        bufs, _ = mem.run(mem.low, *[(f"h_y{i}", [P, 512], F32) for i in range(SIDE)])
        turned, kept = sem("turned"), [sem(f"kept{i}") for i in range(2)]
        stored = [sem(f"stored{i}") for i in range(SIDE)]
        units = [(t0, n, q) for t0, n in TOKEN_TILES for q in range(KD // 4)]
        y_new = o["y_sample"].rearrange("b t d -> (b t) d")

        with nc.Block(no_gpsimd_drain=True) as block:

            @block.tensor
            def _(pe):
                for u, (t0, n, q) in enumerate(units):
                    if u >= 8:
                        pe.wait_ge(kept[u % 2], u // 2 - 3)
                    for k in range(4):
                        tr = nc.tensor.transpose(ps[0:n, u % 8, k * P:(k + 1) * P], mem.hT[:, 4 * q + k, t0:t0 + n],
                                                 mem.c(C_IDENT))
                    tr.then_inc(turned, 1)

            def keep(eng, copy, odd):
                for u, (t0, n, q) in enumerate(units):
                    if u % 2 != odd:
                        continue
                    eng.wait_ge(turned, u + 1)
                    if u >= SIDE:
                        eng.wait_ge(stored[u % SIDE], 16 * (u // SIDE))
                    copy(bufs[u % SIDE][0:n, :], ps[0:n, u % 8, :]).then_inc(kept[odd], 1)

            @block.scalar
            def _(act):
                keep(act, nc.scalar.copy, 0)

            @block.vector
            def _(dve):
                keep(dve, nc.vector.tensor_copy, 1)

            @block.sync
            def _(sp):
                for u, (t0, n, q) in enumerate(units):
                    sp.wait_ge(kept[u % 2], u // 2 + 1)
                    to = o["y_prompt"][0, t0:t0 + n] if t0 < SEQ else y_new
                    sp.dma_start(to[:, q * 512:(q + 1) * 512], bufs[u % SIDE][0:n, :]).then_inc(stored[u % SIDE], 16)
                for i in range(SIDE):
                    sp.wait_ge(stored[i], 16 * (len(units) // SIDE))


OUTPUTS = [
    ("y_prompt", (1, SEQ, D)), ("y_sample", (NB, NT, D)),
    ("k_prompt", (1, 1, SEQ, H, HD)), ("v_prompt", (1, 1, SEQ, H, HD)), ("pool_prompt", (1, 1, HIST, PW)),
    ("k_sample", (1, NB, NT, H, HD)), ("v_sample", (1, NB, NT, H, HD)), ("pool_sample", (1, NB, HIST, PW)),
]

def build(nc, a, o):
    scratch = {
        "xT": nc.dram_tensor("x_feature_major", (KD, P, T), F32, kind="Internal").ap(),
        "gates": nc.dram_tensor("gates", (2 * KD, P, T), F32, kind="Internal").ap(),
    }
    mem = Memory(nc)
    with nc.psum_tensor("ps", [P, 8, 512], F32) as ps:
        norm_inputs(nc, mem, ps, a, scratch)
        project_in(nc, mem, ps, a, o, scratch)
        attend_prompt(nc, mem, ps, a)
        attend_cache(nc, mem, ps, a)
        merge_branches(nc, mem, ps, a, scratch)
        project_out(nc, mem, ps, a, scratch)
        feed_forward(nc, mem, ps, a)
        store_outputs(nc, mem, ps, o)


def kernel(**inputs):
    import concourse.bacc as bacc
    from concourse.bass_utils import run_bass_kernel_spmd

    nc = bacc.Bacc("TRN2", target_bir_lowering=False, num_devices=1)
    arrays = {name: np.ascontiguousarray(x) for name, x in inputs.items()}
    arrays["const"], arrays["mask"] = constants()
    a = {name: nc.dram_tensor(name, x.shape, mybir.dt.from_np(x.dtype), kind="ExternalInput").ap()
         for name, x in arrays.items()}
    o = {name: nc.dram_tensor(name, shape, F32, kind="ExternalOutput").ap() for name, shape in OUTPUTS}
    build(nc, a, o)
    got = run_bass_kernel_spmd(nc, [arrays], core_ids=[0]).results[0]
    return tuple(got[name] for name, _ in OUTPUTS)
```

```python
from contextlib import ExitStack

import numpy as np

import concourse.bass as bass
from concourse import mybir

F32 = mybir.dt.float32
F32R = mybir.dt.float32r
I32 = mybir.dt.int32
ACT = mybir.ActivationFunctionType
ALU = mybir.AluOpType

P = 128
D = 2048
SEQ = 512
NB, NT = 8, 4
NSAMP = NB * NT
T = SEQ + NSAMP
HALF = T // 2
H, HD = 16, 64
AW = H * HD
PAIRS = AW // P
HT = H * NT
PW = D // 2
PT = PW // P
HIST = 15
WINDOWS = (2, 4, 8, 16)
SEG = HIST + NT
UW = HIST + SEQ + NB * SEG
FF = 5632
KD = D // P
IN_TILES = (3 * AW + PW + 2 * D) // P
PAGE = 128
NPAGE = 16
EPS = 1e-6
MASKED = -1e30
FT = FF // P
CHUNKS = 4
CF = FT // CHUNKS
TOKEN_TILES = [(i * P, min(P, T - i * P)) for i in range(-(-T // P))]

SCORE_SEGS = [(0, 0), (512, 1), (1024, 2), (896, 3)]
SAMPLE_COL = 1280
SCORES = SAMPLE_COL + NSAMP

C_IDENT, C_ONES, C_PAIR, C_TRI, C_FOLD = 0, P, 2 * P, 3 * P, 4 * P
C_CORR = C_FOLD + HT
C_WIDTH = C_CORR + 4 * 16
V_NORM1, V_NORM2, V_PSCALE, V_QG, V_KG = 0, KD, 2 * KD, 3 * KD, 3 * KD + 1
V_ROWS = 3 * KD + 2


def constants():
    c = np.zeros((P, C_WIDTH), np.float32)
    r = np.arange(P)
    c[:, C_IDENT:C_IDENT + P] = np.eye(P)
    c[:, C_ONES:C_ONES + P] = 1.0
    c[:, C_PAIR:C_PAIR + P] = (r[:, None] // HD == r[None, :] // HD)
    c[:, C_TRI:C_TRI + P] = (r[:, None] >= r[None, :])
    c[:, C_FOLD:C_FOLD + HT] = (r[:, None] % HT == np.arange(HT)[None, :])
    for g, w in enumerate(WINDOWS):
        c[:, C_CORR + 16 * g:C_CORR + 16 * g + 16] = w / np.minimum(w, np.arange(16) + 1.0)
    mask = np.zeros((P, SCORES), np.float32)
    for col, kb in SCORE_SEGS:
        mask[:, col:col + P] = np.where(r[:, None] < r[None, :], 0.0, MASKED)
    q = np.arange(NSAMP)
    seen = (r[:, None] // NT == q[None, :] // NT) & (r[:, None] % NT < q[None, :] % NT)
    mask[:, SAMPLE_COL:] = np.where(seen & (r[:, None] < NSAMP), 0.0, MASKED)
    return c, mask


def later(n, k=1):
    return not isinstance(n, int) or n >= k


def by_pairs(eng, start, stop, step, tail=0):
    for n in (start, start + 1):
        step(n, n // 2, n % 2)
    with eng.Fori(0, (stop - tail - start - 2) // 2) as i:
        for p in range(2):
            step(i * 2 + (start + 2 + p), i + (start + 2) // 2, p)
    for n in range(stop - tail, stop):
        step(n, n // 2, n % 2)


class Memory:

    def __init__(self, nc):
        base = -(-nc.sbuf_base // 64) * 64
        size = (nc.sbuf_top - base) // 64 * 64
        self.size = size

        def at(name, shape, dtype, offset):
            width = int(np.prod(shape[1:])) * 4
            assert 0 <= offset and offset + width <= size, (name, offset, width, size)
            return nc.alloc_sbuf_tensor_at(name, shape, dtype, offset=base + offset)

        def run(offset, *specs):
            out = []
            for name, shape, dtype in specs:
                out.append(at(name, shape, dtype, offset))
                offset += -(-int(np.prod(shape[1:])) * 4 // 32) * 32
            return out, offset

        self.at, self.run = at, run
        tok = 4 * T
        (self.const, self.vec, self.bias, self.biasT, self.pages, self.carry), low = run(
            0, ("const", [P, C_WIDTH], F32), ("vec", [P, 64], F32), ("bias", [P, H], F32),
            ("biasT", [P, H, NT], F32), ("pages", [1, NB * NPAGE], I32), ("carry", [P, NB, HT], F32))
        self.low = low
        self.after_q = low + PAIRS * tok
        (self.qT, self.kT, self.v_nat, self.v_new, self.uT), self.after_qkv = run(
            low, ("qT", [P, PAIRS, T], F32), ("kT", [P, PAIRS, T], F32),
            ("v_nat", [P, SEQ // P, AW], F32), ("v_new", [NSAMP, AW], F32), ("uT", [P, PT, UW], F32))
        top = size - 2 * KD * tok
        self.xn_hi, self.xn_lo = run(top, ("xn_hi", [P, KD, T], F32R), ("xn_lo", [P, KD, T], F32R))[0]
        self.top = top
        self.top_o = size - 3 * PAIRS * tok
        self.oT, self.pool_hi, self.pool_lo = run(
            self.top_o, ("oT", [P, PAIRS, T], F32), ("pool_hi", [P, PT, T], F32R),
            ("pool_lo", [P, PT, T], F32R))[0]
        self.free = -(-4 * (C_WIDTH + 64) // 32) * 32
        (self.mix_hi, self.mix_lo), self.after_mix = run(
            self.free, ("mix_hi", [P, KD, T], F32R), ("mix_lo", [P, KD, T], F32R))
        (self.hn_hi, self.hn_lo) = run(top, ("hn_hi", [P, KD, T], F32R), ("hn_lo", [P, KD, T], F32R))[0]
        (self.hT, self.total, self.rstd2), end = run(
            top - (KD + 2) * tok, ("hT", [P, KD, T], F32), ("total", [P, T], F32), ("rstd2", [P, T], F32))
        assert end <= top
        self.before_h = top - (KD + 2) * tok

    def c(self, col, rows=P, width=P):
        return self.const[0:rows, col:col + width]


class Weights:

    KT = 8

    def __init__(self, nc, buffers, semaphores, first=0):
        self.nc, self.buffers, self.semaphores, self.first = nc, buffers, semaphores, first
        self.raw, self.hi, self.lo = buffers
        self.loaded, self.hi_made, self.lo_made, self.used = semaphores

    @classmethod
    def place(cls, nc, ctx, mem, phase, offset):
        shape = [P, cls.KT, P]
        specs = [(f"{phase}_{part}{b}", shape, F32 if part == "raw" else F32R)
                 for part in ("raw", "hi", "lo") for b in range(2)]
        tensors, end = mem.run(offset, *specs)
        semaphores = [[ctx.enter_context(nc.semaphore(f"{phase}_w_{event}{b}")) for b in range(2)]
                      for event in ("loaded", "hi_made", "lo_made", "used")]
        return cls(nc, (tensors[0:2], tensors[2:4], tensors[4:6]), semaphores), end

    def after(self, slots):
        return Weights(self.nc, self.buffers, self.semaphores, self.first + slots)

    def load(self, sp, n, b, src, kts=KT):
        n = n + self.first
        if later(n):
            sp.wait_ge(self.lo_made[b], n)
        sp.dma_start(self.raw[b][:, 0:kts, :], src).then_inc(self.loaded[b], 16)

    def split_hi(self, act, n, b, kts=KT):
        n = n + self.first
        act.wait_ge(self.loaded[b], n * 16 + 16)
        if later(n):
            act.wait_ge(self.used[b], n)
        self.nc.scalar.copy(self.hi[b][:, 0:kts, :], self.raw[b][:, 0:kts, :]).then_inc(self.hi_made[b], 1)

    def split_lo(self, dve, n, b, kts=KT):
        n = n + self.first
        dve.wait_ge(self.hi_made[b], n + 1)
        self.nc.vector.tensor_tensor(self.lo[b][:, 0:kts, :], self.raw[b][:, 0:kts, :],
                                     self.hi[b][:, 0:kts, :].bitcast(F32),
                                     ALU.subtract).then_inc(self.lo_made[b], 1)

    def multiply(self, pe, n, b, banks, x_hi, x_lo, kt0=0, kts=KT, start=True, stop=True, at=0,
                 x_ready=None, last=True):
        pe.wait_ge(self.lo_made[b], n + (self.first + 1))
        for k in range(kts):
            if x_ready:
                x_ready(kt0 + k)
            for i, (w, x) in enumerate(((self.hi, x_hi), (self.hi, x_lo), (self.lo, x_hi))):
                for half in range(2):
                    mm = self.nc.tensor.matmul(
                        banks[:, half, 0:HALF], w[b][:, at + k, :], x(kt0 + k, half),
                        start=start and k == 0 and i == 0, stop=stop and k == kts - 1 and i == 2)
        if last:
            mm.then_inc(self.used[b], 1)

    def wait_slot(self, eng, n):
        eng.wait_ge(self.used[1], n + (self.first + 1))


def tile_of(x):
    return lambda k, half: x[:, k, half * HALF:(half + 1) * HALF]


def halves(banks):
    return banks[:, :, 0:HALF]


def by_halves(x):
    return x.rearrange("p (h t) -> p h t", h=2)


def norm_inputs(nc, mem, ps, a, scratch):
    with ExitStack() as ctx:
        sem = lambda name: ctx.enter_context(nc.semaphore("a_" + name))
        (xin0, xin1, xs0, xs1, junk, xg, xt, vrows, brow, ms, var, rstd), _ = mem.run(
            mem.low, ("a_x0", [P, D], F32), ("a_x1", [P, D], F32), ("a_xs0", [P, D], F32),
            ("a_xs1", [P, D], F32), ("a_junk", [P, D], F32), ("a_xg", [P, 2, 4, P], F32),
            ("a_xt", [P, 2, 4, P], F32), ("a_vrows", [V_ROWS, P], F32), ("a_brow", [1, H], F32),
            ("a_ms", [P, 8], F32), ("a_var", [P, 8], F32), ("a_rstd", [P, 8], F32))
        xin, xs = (xin0, xin1), (xs0, xs1)
        x_in = [sem(f"x_in{i}") for i in range(2)]
        params_in, vec_turned, vec_made, bias_made = (
            sem("params_in"), sem("vec_turned"), sem("vec_made"), sem("bias_made"))
        squared, var_made, rooted, rstd_made, scaled = (
            sem("squared"), sem("var_made"), sem("rooted"), sem("rstd_made"), sem("scaled"))
        turned, x_kept, weighted, hi_made, lo_made = (
            sem("turned"), sem("x_kept"), sem("weighted"), sem("hi_made"), sem("lo_made"))
        raw_turned, raw_kept = sem("raw_turned"), sem("raw_kept")
        raw_out = [sem(f"raw_out{i}") for i in range(2)]
        tiles = TOKEN_TILES
        units = [(i, j) for i in range(len(tiles)) for j in range(KD // 4)]

        def source(i):
            if i < SEQ // P:
                return a["x_prompt"][0, i * P:(i + 1) * P, :]
            return a["x_sample"].rearrange("b t d -> (b t) d")

        with nc.Block(no_gpsimd_drain=True) as block:

            @block.sync
            def _(sp):
                def load_x(i):
                    n = tiles[i][1]
                    if i >= 2:
                        sp.wait_ge(raw_turned, 4 * (i - 1))
                        sp.wait_ge(scaled, i - 1)
                    sp.dma_start(xin[i % 2][0:n, :], source(i)).then_inc(x_in[i % 2], 16)

                for i in range(2):
                    load_x(i)
                    if i == 0:
                        sp.dma_start(mem.const[:, :], a["const"]).then_inc(params_in, 16)
                        for name, row in (("norm1_g", V_NORM1), ("norm2_g", V_NORM2), ("pool_scale", V_PSCALE)):
                            sp.dma_start(vrows[row:row + KD, :],
                                         a[name][0].rearrange("(k p) -> k p", p=P)).then_inc(params_in, 16)
                        for name, row in (("q_norm_g", V_QG), ("k_norm_g", V_KG)):
                            for e in range(2):
                                sp.dma_start(vrows[row:row + 1, e * HD:(e + 1) * HD], a[name]).then_inc(params_in, 16)
                        sp.dma_start(brow[:, :], a["sb_bias"]).then_inc(params_in, 16)
                        sp.dma_start(mem.pages[:, :], a["page_table"].rearrange("b n -> (b n)").unsqueeze(0)).then_inc(params_in, 16)
                for u, (i, j) in enumerate(units):
                    t0, n = tiles[i]
                    sp.wait_ge(raw_kept, u + 1)
                    sp.dma_start(scratch["xT"][4 * j:4 * j + 4, :, t0:t0 + n].rearrange("k p t -> p k t"),
                                 xt[:, u % 2, :, 0:n]).then_inc(raw_out[u % 2], 16)
                    if j == KD // 4 - 1 and i + 2 < len(tiles):
                        load_x(i + 2)
                for h in range(2):
                    sp.wait_ge(raw_out[h], 16 * len(units) // 2)

            @block.tensor
            def _(pe):
                pe.wait_ge(params_in, 16 * 10)
                nc.tensor.transpose(ps[:, 0, 0:V_ROWS], vrows[:, :], mem.c(C_IDENT, V_ROWS, V_ROWS))
                nc.tensor.matmul(ps[:, 1, 0:H], mem.c(C_ONES, 1), brow[:, :],
                                 start=True, stop=True).then_inc(vec_turned, 1)
                pe.wait_ge(vec_made, 1)
                pe.wait_ge(bias_made, 1)
                for i, (_, n) in enumerate(tiles):
                    for which in range(2):
                        for j in range(KD // 4):
                            u = 4 * i + j
                            bank = 4 * which + u % 4
                            if which == 0:
                                pe.wait_ge(x_in[i % 2], 16 * (i // 2 + 1))
                                if u >= 4:
                                    pe.wait_ge(raw_kept, u - 3)
                            else:
                                pe.wait_ge(scaled, i + 1)
                                if u >= 4:
                                    pe.wait_ge(weighted, u - 3)
                            x = (xin, xs)[which][i % 2]
                            for k in range(4):
                                tr = nc.tensor.transpose(ps[:, bank, k * P:k * P + n],
                                                         x[0:n, (4 * j + k) * P:(4 * j + k + 1) * P],
                                                         mem.c(C_IDENT, n, n))
                            tr.then_inc((raw_turned, turned)[which], 1)

            @block.scalar
            def _(act):
                act.wait_ge(vec_turned, 1)
                nc.scalar.copy(mem.bias[:, :], ps[:, 1, 0:H]).then_inc(bias_made, 1)
                act.wait_ge(bias_made, 1)
                nc.scalar.copy(mem.biasT[:, :, :], mem.bias[:, :].unsqueeze(2).to_broadcast([P, H, NT])).then_inc(bias_made, 1)

                def root(i):
                    n = tiles[i][1]
                    act.wait_ge(x_in[i % 2], 16 * (i // 2 + 1))
                    if i:
                        act.wait_ge(squared, i)
                    nc.scalar.activation(junk[0:n, :], xin[i % 2][0:n, :], ACT.Square,
                                         accum_out=ms[0:n, i:i + 1]).then_inc(squared, 1)
                    act.wait_ge(var_made, i + 1)
                    nc.scalar.activation(rstd[0:n, i:i + 1], var[0:n, i:i + 1], ACT.Sqrt).then_inc(rooted, 1)

                root(0)
                for i, (t0, n) in enumerate(tiles):
                    if i + 1 < len(tiles):
                        root(i + 1)
                    for j in range(KD // 4):
                        u = 4 * i + j
                        act.wait_ge(raw_turned, u + 1)
                        if u >= 2:
                            act.wait_ge(raw_out[u % 2], 16 * (u // 2))
                        nc.scalar.copy(xt[:, u % 2, :, 0:n],
                                       ps[:, u % 4, :].rearrange("p (k t) -> p k t", k=4)[:, :, 0:n]).then_inc(raw_kept, 1)
                        act.wait_ge(weighted, u + 1)
                        nc.scalar.copy(mem.xn_hi[:, 4 * j:4 * j + 4, t0:t0 + n], xg[:, u % 2, :, 0:n]).then_inc(hi_made, 1)

            @block.vector
            def _(dve):
                dve.wait_ge(vec_turned, 1)
                nc.vector.tensor_copy(mem.vec[:, 0:V_ROWS], ps[:, 0, 0:V_ROWS]).then_inc(vec_made, 1)
                dve.wait_ge(vec_made, 1)
                nc.vector.tensor_scalar(mem.vec[:, V_QG:V_QG + 1], mem.vec[:, V_QG:V_QG + 1], HD ** -0.5,
                                        None, ALU.mult).then_inc(vec_made, 1)

                def scale(i):
                    n = tiles[i][1]
                    dve.wait_ge(squared, i + 1)
                    nc.vector.tensor_scalar(var[0:n, i:i + 1], ms[0:n, i:i + 1], 1.0 / D, EPS,
                                            ALU.mult, ALU.add).then_inc(var_made, 1)
                    dve.wait_ge(rooted, i + 1)
                    nc.vector.reciprocal(rstd[0:n, i:i + 1], rstd[0:n, i:i + 1]).then_inc(rstd_made, 1)
                    dve.wait_ge(rstd_made, i + 1)
                    if i >= 2:
                        dve.wait_ge(turned, 4 * (i - 1))
                    nc.vector.tensor_scalar(xs[i % 2][0:n, :], xin[i % 2][0:n, :], rstd[0:n, i:i + 1],
                                            None, ALU.mult).then_inc(scaled, 1)

                scale(0)
                for i, (t0, n) in enumerate(tiles):
                    if i + 1 < len(tiles):
                        scale(i + 1)
                    for j in range(KD // 4):
                        u = 4 * i + j
                        dve.wait_ge(turned, u + 1)
                        if u >= 2:
                            dve.wait_ge(lo_made, u - 1)
                        g = mem.vec[:, V_NORM1 + 4 * j:V_NORM1 + 4 * j + 4].unsqueeze(2).to_broadcast([P, 4, n])
                        nc.vector.tensor_tensor(xg[:, u % 2, :, 0:n],
                                                ps[:, 4 + u % 4, :].rearrange("p (k t) -> p k t", k=4)[:, :, 0:n],
                                                g, ALU.mult).then_inc(weighted, 1)
                        dve.wait_ge(hi_made, u + 1)
                        nc.vector.tensor_tensor(mem.xn_lo[:, 4 * j:4 * j + 4, t0:t0 + n], xg[:, u % 2, :, 0:n],
                                                mem.xn_hi[:, 4 * j:4 * j + 4, t0:t0 + n].bitcast(F32),
                                                ALU.subtract).then_inc(lo_made, 1)


Q, K, V, U, GATE = range(5)
KIND_START = (0, 8, 16, 24, 32, IN_TILES)


def kind_of(n):
    return max(k for k in range(5) if KIND_START[k] <= n)


def project_in(nc, mem, ps, a, o, scratch):
    with ExitStack() as ctx:
        sem = lambda name: ctx.enter_context(nc.semaphore("b_" + name))
        W, end = Weights.place(nc, ctx, mem, "b", mem.after_qkv)
        (raw0, raw1, sq, root, inv, kn0, kn1, nat0, nat1, natS0, natS1), end = mem.run(
            end, ("b_t0", [P, T], F32), ("b_t1", [P, T], F32), ("b_sq", [P, T], F32),
            ("b_root", [P, T], F32), ("b_inv", [P, T], F32), ("b_kn0", [P, T], F32), ("b_kn1", [P, T], F32),
            ("b_nat0", [P, 4, P], F32), ("b_nat1", [P, 4, P], F32),
            ("b_natS0", [NSAMP, P], F32), ("b_natS1", [NSAMP, P], F32))
        assert end <= mem.top, (end, mem.top)
        res, kn, nat, nat_s = (raw0, raw1), (kn0, kn1), (nat0, nat1), (natS0, natS1)
        res_made = sem("res_made")
        squared, summed, rooted = sem("squared"), sem("summed"), sem("rooted")
        inverted, normed = sem("inverted"), sem("normed")
        u_placed = sem("u_placed")
        turned, nat_made = sem("turned"), sem("nat_made")
        kept = [sem(f"kept{i}") for i in range(2)]
        v_out = sem("v_out")
        w_in = a["w_in"][0].rearrange("(b k p) c -> b p k c", b=2, p=P)
        mm_banks = [ps[:, 2 * p:2 * p + 2, :] for p in range(2)]
        sum_banks = ps[:, 4:6, :]
        first_turned = KIND_START[K]
        k_out = [o["k_prompt"][0, 0].rearrange("(b p) h d -> p b (h d)", p=P),
                 o["k_sample"][0].rearrange("b t h d -> (b t) (h d)")]
        state = a["state_pool"][0]
        for_each = lambda eng, step: [by_pairs(eng, KIND_START[k], KIND_START[k + 1], lambda n, i, p, k=k: step(
            n, i, p, k, kind_of(n - 1) if isinstance(n, int) and n else k,
            kind_of(n - 2) if isinstance(n, int) and n > 1 else k), tail=2 * (k == GATE)) for k in range(5)]

        with nc.Block(no_gpsimd_drain=True) as block:

            @block.sync
            def _(sp):
                def columns(n, b):
                    return w_in[b][:, :, bass.ds(n * P, P)]

                def step(n, i, p, kind, k1, k2):
                    if not (isinstance(n, int) and n == IN_TILES - 1):
                        for b in range(2):
                            W.load(sp, n + 1, b, columns(n + 1, b))
                    if later(n, 2):
                        store(n - 2, i - 1, p, k2)

                def store(n, i, p, kind):
                    if kind in (K, U):
                        cols = bass.ds((n - KIND_START[kind]) * P, P)
                        sp.wait_ge(nat_made, n - (first_turned - 1))
                        if kind == K:
                            sp.dma_start(k_out[0][:, :, cols], nat[p][:, :, :]).then_inc(kept[p], 16)
                            sp.dma_start(k_out[1][:, cols], nat_s[p][:, :]).then_inc(kept[p], 16)
                        else:
                            sp.dma_start(o["pool_prompt"][0, 0][:, cols], nat[p][P - HIST:P, 0, :]).then_inc(kept[p], 16)
                            sp.dma_start(o["pool_sample"][0][:, HIST - NT:HIST, cols],
                                         nat_s[p][:, :]).then_inc(kept[p], 16)
                    if kind == GATE:
                        sp.wait_ge(res_made, n + 1)
                        sp.dma_start(scratch["gates"][bass.ds(n - KIND_START[GATE], 1), :, :].rearrange("a p t -> p a t"),
                                     res[p][:, :].unsqueeze(1)).then_inc(kept[p], 16)

                sp.dma_start(o["pool_sample"][0][:, 0:HIST - NT, :], state[:, NT:HIST, :]).then_inc(v_out, 16)
                for b in range(2):
                    W.load(sp, 0, b, columns(0, b))
                for_each(sp, step)
                for n in (IN_TILES - 2, IN_TILES - 1):
                    store(n, n // 2, n % 2, GATE)
                sp.wait_ge(nat_made, KIND_START[GATE] - first_turned)
                sp.dma_start(o["v_prompt"][0, 0].rearrange("(b p) h d -> p b (h d)", p=P),
                             mem.v_nat[:, :, :]).then_inc(v_out, 16)
                sp.dma_start(o["v_sample"][0].rearrange("b t h d -> (b t) (h d)"), mem.v_new[:, :]).then_inc(v_out, 16)
                sp.wait_ge(v_out, 48)
                for p in range(2):
                    sp.wait_ge(kept[p], 32 * 8 + 16 * 16)

            @block.tensor
            def _(pe):
                def step(n, i, p, kind, k1, k2):
                    if later(n, 2):
                        pe.wait_ge(res_made, n - 1)
                    W.multiply(pe, n, 0, mm_banks[p], tile_of(mem.xn_hi), tile_of(mem.xn_lo), 0, stop=False)
                    if later(n) and k1 in (Q, K):
                        pe.wait_ge(squared, n)
                        if later(n, 2):
                            pe.wait_ge(rooted, n - 1)
                        for h in range(2):
                            mm = nc.tensor.matmul(sum_banks[:, h, 0:HALF], mem.c(C_PAIR),
                                                  sq[:, h * HALF:(h + 1) * HALF], start=True, stop=True)
                        mm.then_inc(summed, 1)
                    W.multiply(pe, n, 1, mm_banks[p], tile_of(mem.xn_hi), tile_of(mem.xn_lo), W.KT, start=False)
                    if k1 in (K, V, U) and later(n, first_turned + 1):
                        src = (kn if k1 == K else res)[1 - p]
                        m = n - first_turned
                        if k1 == K:
                            pe.wait_ge(normed, n)
                        else:
                            pe.wait_ge(res_made, n)
                        if later(n, first_turned + 2):
                            pe.wait_ge(nat_made, m - 1)
                        for t in range(3 if k1 == U else 0, 4):
                            nc.tensor.transpose(ps[:, 6, (t % (3 if k1 == U else 4)) * P:(t % (3 if k1 == U else 4) + 1) * P],
                                                src[:, t * P:(t + 1) * P], mem.c(C_IDENT))
                        nc.tensor.transpose(ps[0:NSAMP, 7, 0:P], src[:, SEQ:T], mem.c(C_IDENT)).then_inc(turned, 1)

                for_each(pe, step)

            @block.scalar
            def _(act):
                def step(n, i, p, kind, k1, k2):
                    last = isinstance(n, int) and n == IN_TILES - 1
                    if not last:
                        W.split_hi(act, n + 1, 0)
                    if later(n) and k1 in (Q, K):
                        act.wait_ge(summed, n)
                        if later(n, 2):
                            act.wait_ge(inverted, n - 1)
                        nc.scalar.activation(by_halves(root[:, :]), halves(sum_banks), ACT.Sqrt,
                                             scale=1.0 / HD, bias=mem.vec[:, 63:64]).then_inc(rooted, 1)
                    if not last:
                        W.split_hi(act, n + 1, 1)
                    W.wait_slot(act, n)
                    if later(n, 2):
                        if k2 in (Q, K):
                            act.wait_ge(normed, n - 1)
                        if k2 in (V, U):
                            act.wait_ge(turned, n - (first_turned + 1))
                        if k2 == U:
                            act.wait_ge(u_placed, n - (KIND_START[U] + 1))
                        if k2 == GATE and later(n, KIND_START[GATE] + 2):
                            act.wait_ge(kept[p], 32 * 8 + (i - KIND_START[GATE] // 2) * 16)
                    out = by_halves(res[p][:, :])
                    if kind == GATE:
                        nc.scalar.activation(out, halves(mm_banks[p]), ACT.Sigmoid).then_inc(res_made, 1)
                    else:
                        nc.scalar.copy(out, halves(mm_banks[p])).then_inc(res_made, 1)
                    if kind in (Q, K):
                        act.wait_ge(res_made, n + 1)
                        if later(n):
                            act.wait_ge(summed, n)
                        nc.scalar.square(sq[:, :], res[p][:, :]).then_inc(squared, 1)
                    if k1 in (K, V, U) and later(n, first_turned + 1):
                        to_natural(n - 1, i, p, k1)

                def to_natural(n, i, p, kind):
                    act.wait_ge(turned, n - (first_turned - 1))
                    q = 1 - p
                    if kind == V:
                        cols = bass.ds((n - KIND_START[V]) * P, P)
                        nc.scalar.copy(mem.v_nat[:, :, cols], ps[:, 6, :].rearrange("p (b c) -> p b c", c=P))
                        nc.scalar.copy(mem.v_new[:, cols], ps[0:NSAMP, 7, 0:P]).then_inc(nat_made, 1)
                        return
                    pair = i - q if isinstance(i, int) else i - q
                    before = pair - KIND_START[K] // 2 if kind == K else pair - KIND_START[U] // 2 + 4
                    if not isinstance(before, int) or before > 0:
                        act.wait_ge(kept[q], before * 32)
                    if kind == K:
                        nc.scalar.copy(nat[q][:, :, :], ps[:, 6, :].rearrange("p (b c) -> p b c", c=P))
                    else:
                        nc.scalar.copy(nat[q][:, 0, :], ps[:, 6, 0:P])
                    nc.scalar.copy(nat_s[q][:, :], ps[0:NSAMP, 7, 0:P]).then_inc(nat_made, 1)

                for b in range(2):
                    W.split_hi(act, 0, b)
                for_each(act, step)

            @block.vector
            def _(dve):
                def step(n, i, p, kind, k1, k2):
                    last = isinstance(n, int) and n == IN_TILES - 1
                    if not last:
                        W.split_lo(dve, n + 1, 0)
                    q = 1 - p
                    if later(n) and k1 in (Q, K):
                        dve.wait_ge(rooted, n)
                        if later(n, 2):
                            dve.wait_ge(normed, n - 1)
                        nc.vector.reciprocal(inv[:, :], root[:, :]).then_inc(inverted, 1)
                        dve.wait_ge(inverted, n)
                        g = mem.vec[:, (V_QG, V_KG)[k1]:(V_QG, V_KG)[k1] + 1]
                        m = n - (KIND_START[k1] + 1)
                        to = (mem.qT, mem.kT)[k1][:, bass.ds(m, 1), :].rearrange("p a t -> p (a t)")
                        first = nc.vector.scalar_tensor_tensor(out=to, in0=res[q][:, :], scalar=g, in1=inv[:, :],
                                                               op0=ALU.mult, op1=ALU.mult)
                        if k1 == Q:
                            first.then_inc(normed, 1)
                        else:
                            if later(n, first_turned + 3):
                                dve.wait_ge(turned, n - (first_turned + 2))
                            nc.vector.scalar_tensor_tensor(out=kn[q][:, :], in0=res[q][:, :], scalar=g, in1=inv[:, :],
                                                           op0=ALU.mult, op1=ALU.mult).then_inc(normed, 1)
                    if later(n) and k1 == U:
                        dve.wait_ge(res_made, n)
                        m = bass.ds(n - (KIND_START[U] + 1), 1)
                        nc.vector.tensor_copy(mem.uT[:, m, HIST:HIST + SEQ], res[q][:, 0:SEQ].unsqueeze(1))
                        nc.vector.tensor_copy(
                            mem.uT[:, m, HIST + SEQ:UW].rearrange("p a (b s) -> p (a b) s", b=NB)[:, :, HIST:SEG],
                            res[q][:, SEQ:T].rearrange("p (b t) -> p b t", b=NB)).then_inc(u_placed, 1)
                    if not last:
                        W.split_lo(dve, n + 1, 1)

                nc.vector.memset(mem.vec[:, 63:64], EPS)
                for b in range(2):
                    W.split_lo(dve, 0, b)
                for_each(dve, step)



def attend_prompt(nc, mem, ps, a):
    with ExitStack() as ctx:
        sem = lambda name: ctx.enter_context(nc.semaphore("c_" + name))
        (mask, zb0, zb1, soft, sp0, sp1, ks0, ks1, qs0, qs1, vs0, vs1, vn0, vn1, bs0, bs1, win0, win1, state), end = mem.run(
            mem.after_qkv, ("c_mask", [P, SCORES], F32), ("c_zb0", [P, SCORES], F32), ("c_zb1", [P, SCORES], F32),
            ("c_soft", [P, SCORES], F32), ("c_sp0", [P, SCORES], F32), ("c_sp1", [P, SCORES], F32),
            ("c_ks0", [P, SEQ + P], F32), ("c_ks1", [P, SEQ + P], F32), ("c_qs0", [P, T], F32), ("c_qs1", [P, T], F32),
            ("c_vs0", [P, SEQ // P, P], F32), ("c_vs1", [P, SEQ // P, P], F32),
            ("c_vn0", [NSAMP, P], F32), ("c_vn1", [NSAMP, P], F32), ("c_bs0", [P, 2], F32), ("c_bs1", [P, 2], F32),
            ("c_win0", [P, UW], F32), ("c_win1", [P, UW], F32), ("c_state", [NB * HIST, PW], F32))
        assert end <= mem.top_o, (end, mem.top_o)
        zb, sp_, ks, qs, vs, vn, bs = (zb0, zb1), (sp0, sp1), (ks0, ks1), (qs0, qs1), (vs0, vs1), (vn0, vn1), (bs0, bs1)
        state_in, mask_in, state_turned, u_ready, padded = (
            sem("state_in"), sem("mask_in"), sem("state_turned"), sem("u_ready"), sem("padded"))
        staged, scored, biased, softened, summands = (
            sem("staged"), sem("scored"), sem("biased"), sem("softened"), sem("summands"))
        summed, decayed, weighted, applied, o_kept = (
            sem("summed"), sem("decayed"), sem("weighted"), sem("applied"), sem("o_kept"))
        sp_made, zeroed, pool_step = sem("sp_made"), sem("zeroed"), sem("pool_step")
        z_ps = ps[:, 0:3, :].rearrange("p b c -> p (b c)")
        cum_ps = ps[:, 3:6, :].rearrange("p b c -> p (b c)")
        heads = lambda eng, body: (body(0), _loop(eng, 1, H // 4 - 1, body), body(H // 4 - 1))

        with nc.Block(no_gpsimd_drain=True) as block:

            @block.sync
            def _(sp):
                sp.dma_start(state[:, :], a["state_pool"][0].rearrange("b r c -> (b r) c")).then_inc(state_in, 16)
                sp.dma_start(mask[:, :], a["mask"]).then_inc(mask_in, 16)

            @block.tensor
            def _(pe):
                pe.wait_ge(state_in, 16)
                for m in range(PT):
                    tr = nc.tensor.transpose(ps[:, 6 + m // 4, m % 4 * P:m % 4 * P + NB * HIST],
                                             state[:, m * P:(m + 1) * P], mem.c(C_IDENT, NB * HIST, NB * HIST))
                tr.then_inc(state_turned, 1)

                def score(j, u):
                    pair, e = u // 2 % 2, HD * (u % 2)
                    pe.wait_ge(staged, j_pair(j, u) + 1)
                    if later(j):
                        pe.wait_ge(biased, j)
                    for col, kb in SCORE_SEGS:
                        nc.tensor.matmul(z_ps[:, col:col + SEQ - kb * P], ks[pair][e:e + HD, kb * P:(kb + 1) * P],
                                         qs[pair][e:e + HD, kb * P:SEQ], start=True, stop=True)
                    nc.tensor.matmul(z_ps[:, SAMPLE_COL:SCORES], ks[pair][e:e + HD, SEQ:SEQ + P],
                                     qs[pair][e:e + HD, SEQ:T], start=True, stop=True).then_inc(scored, 1)

                def accumulate(j, u):
                    pe.wait_ge(sp_made, j + 1)
                    if later(j):
                        pe.wait_ge(decayed, j)
                    src = sp_[u % 2]
                    for col, kb in SCORE_SEGS:
                        for col2, kb2 in sorted(SCORE_SEGS, key=lambda x: x[1]):
                            if kb2 >= kb:
                                nc.tensor.matmul(cum_ps[:, col + (kb2 - kb) * P:col + SEQ - kb * P],
                                                 mem.c(C_TRI if kb2 == kb else C_ONES),
                                                 src[:, col2:col2 + SEQ - kb2 * P], start=kb2 == kb, stop=kb2 == 3)
                    nc.tensor.matmul(cum_ps[:, SAMPLE_COL:SCORES], mem.c(C_TRI), src[:, SAMPLE_COL:SCORES],
                                     start=True, stop=True).then_inc(summed, 1)

                def apply(j, u):
                    pair, e = u // 2 % 2, HD * (u % 2)
                    pe.wait_ge(weighted, j + 1)
                    if e == 0 and later(j):
                        pe.wait_ge(o_kept, j_pair(j, u))
                    w = sp_[u % 2]
                    for col, kb in sorted(SCORE_SEGS, key=lambda x: x[1]):
                        nc.tensor.matmul(ps[e:e + HD, 6, kb * P:SEQ], vs[pair][:, kb, e:e + HD],
                                         w[:, col:col + SEQ - kb * P], start=kb == 0, stop=kb == 3)
                    nc.tensor.matmul(ps[e:e + HD, 7, 0:NSAMP], vn[pair][:, e:e + HD],
                                     w[0:NSAMP, SAMPLE_COL:SCORES], start=True, stop=True).then_inc(applied, 1)

                def body(i):
                    for u in range(4):
                        j = i * 4 + u
                        if not (isinstance(i, int) and j == H - 1):
                            score(j + 1, u + 1)
                        if later(j):
                            apply(j - 1, u - 1)
                        accumulate(j, u)

                pe.wait_ge(padded, 1)
                pe.wait_ge(u_ready, 1)
                score(0, 0)
                heads(pe, body)
                apply(H - 1, 3)

            @block.scalar
            def _(act):
                def softplus_tail(j, u):
                    act.wait_ge(biased, j + 1)
                    if later(j):
                        act.wait_ge(sp_made, j)
                    nc.scalar.activation(soft[:, :], zb[u % 2][:, :], ACT.Abs).then_inc(softened, 1)
                    act.wait_ge(softened, j * 3 + 1)
                    nc.scalar.activation(soft[:, :], soft[:, :], ACT.Exp, scale=-1.0).then_inc(softened, 1)
                    act.wait_ge(softened, j * 3 + 2)
                    nc.scalar.activation(soft[:, :], soft[:, :], ACT.Ln, bias=1.0).then_inc(softened, 1)

                def weight(j, u):
                    act.wait_ge(decayed, j + 1)
                    nc.scalar.activation(sp_[u % 2][:, :], zb[u % 2][:, :], ACT.Exp).then_inc(weighted, 1)

                def keep(j, u):
                    act.wait_ge(applied, j + 1)
                    r = bass.ds(j_pair(j, u), 1)
                    nc.scalar.copy(mem.oT[:, r, 0:SEQ], ps[:, 6, :].unsqueeze(1))
                    nc.scalar.copy(mem.oT[:, r, SEQ:T], ps[:, 7, 0:NSAMP].unsqueeze(1)).then_inc(o_kept, 1)

                def body(i):
                    for u in range(4):
                        j = i * 4 + u
                        if not (isinstance(i, int) and j == H - 1):
                            softplus_tail(j + 1, u + 1)
                        if u % 2 == 0 and later(j, 2):
                            keep(j - 1, u - 1)
                        weight(j, u)

                act.preload_act_table_set("natural_log_exp_and_others")
                softplus_tail(0, 0)
                heads(act, body)
                keep(H - 1, 3)

            @block.vector
            def _(dve):
                for b in range(2):
                    nc.vector.memset(ks[b][:, SEQ + NSAMP:], 0.0)
                nc.vector.memset(mem.uT[:, :, 0:HIST], 0.0).then_inc(padded, 1)
                dve.wait_ge(state_turned, 1)
                for m in range(PT):
                    cp = nc.vector.tensor_copy(
                        mem.uT[:, m, HIST + SEQ:UW].rearrange("p (b s) -> p b s", b=NB)[:, :, 0:HIST],
                        ps[:, 6 + m // 4, m % 4 * P:m % 4 * P + NB * HIST].rearrange("p (b s) -> p b s", b=NB))
                cp.then_inc(u_ready, 1)
                dve.wait_ge(mask_in, 16)

                def bias(j, u):
                    dve.wait_ge(scored, j + 1)
                    if later(j, 2):
                        dve.wait_ge(weighted, j - 1)
                    nc.vector.scalar_tensor_tensor(out=zb[u % 2][:, :], in0=z_ps[:, 0:SCORES],
                                                   scalar=bs[u // 2 % 2][:, u % 2:u % 2 + 1], in1=mask[:, :],
                                                   op0=ALU.add, op1=ALU.add).then_inc(biased, 1)

                def softplus(j, u):
                    dve.wait_ge(softened, j * 3 + 3)
                    if later(j, 2):
                        dve.wait_ge(applied, j - 1)
                    nc.vector.scalar_tensor_tensor(out=sp_[u % 2][:, :], in0=zb[u % 2][:, :], scalar=0.0,
                                                   in1=soft[:, :], op0=ALU.max, op1=ALU.add).then_inc(sp_made, 1)
                    dve.wait_ge(sp_made, j + 1)
                    nc.vector.tensor_copy(
                        mem.carry[:, :, :].rearrange("p b (h t) -> p b h t", t=NT)[:, :, bass.ds(j, 1), :],
                        sp_[u % 2][:, SAMPLE_COL:SCORES].rearrange("p (b t) -> p b t", t=NT).unsqueeze(2))

                def decay(j, u):
                    dve.wait_ge(summed, j + 1)
                    nc.vector.tensor_tensor(zb[u % 2][:, :], zb[u % 2][:, :], cum_ps[:, 0:SCORES],
                                            ALU.subtract).then_inc(decayed, 1)

                def body(i):
                    for u in range(4):
                        j = i * 4 + u
                        if not (isinstance(i, int) and j == H - 1):
                            bias(j + 1, u + 1)
                            softplus(j + 1, u + 1)
                        decay(j, u)

                bias(0, 0)
                softplus(0, 0)
                heads(dve, body)

            @block.gpsimd
            def _(pool):
                def stage(r):
                    q = r % 2
                    if r >= 2:
                        pool.wait_ge(applied, 2 * (r - 1))
                    nc.gpsimd.tensor_copy(bs[q][:, :], mem.bias[:, 2 * r:2 * r + 2])
                    nc.gpsimd.tensor_copy(qs[q][:, :], mem.qT[:, r, :])
                    nc.gpsimd.tensor_copy(ks[q][:, 0:T], mem.kT[:, r, :])
                    nc.gpsimd.tensor_copy(vs[q][:, :, :], mem.v_nat[:, :, r * P:(r + 1) * P])
                    nc.gpsimd.tensor_copy(vn[q][:, :], mem.v_new[:, r * P:(r + 1) * P]).then_inc(staged, 1)

                steps = [0]

                def link(ins):
                    steps[0] += 1
                    ins.then_inc(pool_step, 1)
                    pool.wait_ge(pool_step, steps[0])

                def new_tokens(x, part):
                    if part == 0:
                        return x[:, HIST:HIST + SEQ]
                    return x[:, HIST + SEQ:UW].rearrange("p (b s) -> p b s", b=NB)[:, :, HIST:SEG]

                def pool_tile(m):
                    g = m * P // (PW // len(WINDOWS))
                    w = WINDOWS[g]
                    src, bufs, n, first = mem.uT[:, m, :], (win0[:, :], win1[:, :]), 1, 0
                    turn = 0
                    while n < w:
                        first += n
                        link(nc.gpsimd.tensor_tensor(bufs[turn][:, first:UW], src[:, first:UW],
                                                     src[:, first - n:UW - n], ALU.add))
                        src, turn, n = bufs[turn], 1 - turn, 2 * n
                    corr = mem.const[:, C_CORR + 16 * g:C_CORR + 16 * g + 16]
                    link(nc.gpsimd.tensor_tensor(src[:, HIST:HIST + 16], src[:, HIST:HIST + 16], corr, ALU.mult))
                    link(nc.gpsimd.tensor_scalar(bufs[turn][:, HIST:UW], src[:, HIST:UW], 1.0 / w, None, ALU.mult))
                    link(nc.gpsimd.tensor_tensor(src[:, HIST:UW], bufs[turn][:, HIST:UW], mem.uT[:, m, HIST:UW],
                                                 ALU.subtract))
                    for part, (t0, t1) in enumerate(((0, SEQ), (SEQ, T))):
                        to = [x[:, m, t0:t1] if part == 0 else x[:, m, t0:t1].rearrange("p (b t) -> p b t", b=NB)
                              for x in (mem.pool_hi, mem.pool_lo)]
                        link(nc.gpsimd.tensor_copy(to[0], new_tokens(src, part)))
                        link(nc.gpsimd.tensor_tensor(to[1], new_tokens(src, part), to[0].bitcast(F32), ALU.subtract))

                pool.wait_ge(padded, 1)
                stage(0)
                stage(1)
                pool.wait_ge(u_ready, 1)
                for r in range(PAIRS):
                    pool_tile(r)
                    if r + 2 < PAIRS:
                        stage(r + 2)


def j_pair(j, u):
    if isinstance(j, int):
        return j // 2
    return (j - u % 2) // 2


def _loop(eng, start, stop, body):
    with eng.Fori(start, stop) as i:
        body(i)


def attend_cache(nc, mem, ps, a):
    GP = 4
    GROUPS = NPAGE // GP
    LAST = NB * GROUPS - 1
    with ExitStack() as ctx:
        sem = lambda name: ctx.enter_context(nc.semaphore("d_" + name))
        specs = [(f"d_{x}{j}", [P, AW], F32) for x in ("k", "v") for j in range(GP)] + [
            (f"d_v_{part}{j}", [P, AW], F32R) for part in ("hi", "lo") for j in range(GP)] + [
            (f"d_kt_{part}{i}", [P, PAIRS, 2 * PAGE], F32R) for part in ("hi", "lo") for i in range(2)] + [
            ("d_qb", [P, PAIRS * (P + 2 * NT)], F32R), ("d_zr", [P, GP * PAGE], F32), ("d_soft", [P, GP * HT], F32),
            ("d_zb0", [P, GP * HT], F32), ("d_zb1", [P, GP * HT], F32), ("d_sp0", [P, GP * HT], F32),
            ("d_sp1", [P, GP * HT], F32), ("d_w", [P, GP * HT], F32),
            ("d_wp0", [P, GP, 2, HT], F32R), ("d_wp1", [P, GP, 2, HT], F32R),
            ("d_lost0", [P, GP + 1, HT], F32), ("d_lost1", [P, GP + 1, HT], F32), ("d_zero", [P, HT], F32),
            ("d_oacc", [P, AW], F32)]
        tensors, end = mem.run(mem.after_q, *specs)
        assert end <= mem.top_o, (end, mem.top_o)
        kp, vp, v_hi, v_lo, kt_hi, kt_lo = (tensors[0:4], tensors[4:8], tensors[8:12], tensors[12:16],
                                            tensors[16:18], tensors[18:20])
        qb, zr, soft = tensors[20:23]
        zb, sp_, wf, wp, lost = tensors[23:25], tensors[25:27], tensors[27], tensors[28:30], tensors[30:32]
        zero, oacc = tensors[32:34]
        k_in = [sem(f"k_in{j}") for j in range(GP)]
        v_in = [sem(f"v_in{j}") for j in range(GP)]
        k_turned, kt_hi_made, kt_lo_made = sem("k_turned"), sem("kt_hi_made"), sem("kt_lo_made")
        v_hi_made, v_lo_made = sem("v_hi_made"), sem("v_lo_made")
        q_hi_made, q_lo_made, q_zeroed, zeroed = sem("q_hi_made"), sem("q_lo_made"), sem("q_zeroed"), sem("zeroed")
        scored, rows_kept, turned, biased = sem("scored"), sem("rows_kept"), sem("turned"), sem("biased")
        sized, softened, sp_made, lost_made = sem("sized"), sem("softened"), sem("sp_made"), sem("lost_made")
        summed, decayed, weighted = sem("summed"), sem("decayed"), sem("weighted")
        w_hi_made, w_lo_made = sem("w_hi_made"), sem("w_lo_made")
        applied, acc_kept, extracted, added = sem("applied"), sem("acc_kept"), sem("extracted"), sem("added")
        LOST_STEPS = GROUPS * GP
        LOST_BEFORE = [0] + [1 + GP * s for s in range(1, GROUPS)]

        def lost_ready(b, s):
            if s < 0:
                b, s = b - 1, s + GROUPS
            return b * LOST_STEPS + (LOST_BEFORE[s] + GP - 1 + (s == 0))

        UNITS = 2 * GP
        cache = [a[n][0].rearrange("n p h d -> n p (h d)") for n in ("cache_k", "cache_v")]
        n_pages = cache[0].shape[0]
        stride = P + 2 * NT
        q_cols = lambda e, lo: qb[e * HD:(e + 1) * HD, :].rearrange("p (a c) -> p a c", c=stride)[
            :, :, lo * HT + NT * e:lo * HT + NT * e + NT]
        q_src = lambda b, e: mem.qT[e * HD:(e + 1) * HD, :, bass.ds(b * NT + SEQ, NT)]
        turned_z = ps[:, 5, 0:GP * HT]
        sums = ps[:, 5, GP * HT:2 * GP * HT]
        own = ps[:, 5, GP * HT:GP * HT + PAIRS * 2 * NT]

        def exists(g):
            return not isinstance(g, int) or 0 <= g <= LAST

        def steps(eng, body):
            body(0)
            _loop(eng, 1, NB - 1, body)
            body(NB - 1)

        with nc.Block(no_gpsimd_drain=True) as block:

            @block.sync
            def _(sp):
                def load(b, s, which, j):
                    g = b * GROUPS + s
                    if not exists(g):
                        return
                    at = b * NPAGE + (NPAGE * (s // GROUPS) + NPAGE - GP * (s % GROUPS + 1) + j)
                    page = sp.value_load(mem.pages[0:1, bass.ds(at, 1)], min_val=0, max_val=n_pages - 1)
                    if later(g):
                        if which == 0:
                            sp.wait_ge(k_turned, (g - 1) * UNITS + (2 * j + 2))
                        else:
                            sp.wait_ge(v_lo_made, (g - 1) * GP + (j + 1))
                    sp.dma_start((kp, vp)[which][j][:, :], cache[which][bass.ds(page, 1), :, :].rearrange(
                        "a p c -> p (a c)")).then_inc((k_in, v_in)[which][j], 16)

                def body(b):
                    for s in range(GROUPS):
                        load(b, s + 1, 0, 2)
                        load(b, s - 1, 1, 3)
                        load(b, s + 1, 0, 3)
                        load(b, s, 1, 0)
                        load(b, s + 2, 0, 0)
                        load(b, s, 1, 1)
                        load(b, s + 2, 0, 1)
                        load(b, s, 1, 2)

                for j in range(GP):
                    load(0, 0, 0, j)
                for j in range(2):
                    load(0, 1, 0, j)
                steps(sp, body)
                load(NB - 1, GROUPS - 1, 1, 3)

            @block.tensor
            def _(pe):
                def turn(g, k):
                    if not exists(g):
                        return
                    j, half = k // 2, k % 2
                    pe.wait_ge(k_in[j], g * 16 + 16)
                    if later(g) or k >= 4:
                        pe.wait_ge(kt_lo_made, g * UNITS + (k - 3))
                    for r in range(4):
                        tr = nc.tensor.transpose(ps[:, k % 4, r * P:(r + 1) * P],
                                                 kp[j][:, (4 * half + r) * P:(4 * half + r + 1) * P], mem.c(C_IDENT))
                    tr.then_inc(k_turned, 1)

                def score(g, sub, half):
                    pe.wait_ge(kt_lo_made, g * UNITS + 4 * (sub + 1))
                    if half == 0 and (later(g) or sub):
                        pe.wait_ge(rows_kept, g * 2 + sub)
                    for p in range(half * PAIRS // 2, (half + 1) * PAIRS // 2):
                        for kt in (kt_hi, kt_lo):
                            mm = nc.tensor.matmul(ps[:, 4, sub * 2 * PAGE:(sub + 1) * 2 * PAGE],
                                                  qb[:, p * P:(p + 1) * P], kt[sub][:, p, :],
                                                  start=p == 0 and kt is kt_hi, stop=p == PAIRS - 1 and kt is kt_lo)
                    if half:
                        mm.then_inc(scored, 1)

                def turn_scores(g):
                    if not exists(g):
                        return
                    pe.wait_ge(rows_kept, g * 2 + 2)
                    if later(g):
                        pe.wait_ge(biased, g)
                    for j in range(GP):
                        mm = nc.tensor.matmul(ps[:, 5, j * HT:(j + 1) * HT], zr[:, j * PAGE:(j + 1) * PAGE],
                                              mem.c(C_FOLD, P, HT), start=True, stop=True)
                    mm.then_inc(turned, 1)

                def accumulate(b, s):
                    g = b * GROUPS + s
                    if not exists(g):
                        return
                    pe.wait_ge(sp_made, g + 1)
                    pe.wait_ge(lost_made, lost_ready(b, s))
                    pe.wait_ge(biased, g + 1)
                    if later(g):
                        pe.wait_ge(decayed, g)
                    if s == 2 and later(b):
                        pe.wait_ge(added, b)
                    nc.tensor.matmul(sums, mem.c(C_TRI), sp_[s % 2][:, :], start=True, stop=False)
                    nc.tensor.matmul(sums, mem.c(C_ONES), lost[s % 2][:, 1:GP + 1, :].rearrange("p g c -> p (g c)"),
                                     start=False, stop=True).then_inc(summed, 1)

                def apply(b, s, j):
                    g = b * GROUPS + s
                    if not exists(g):
                        return
                    place = s % GROUPS
                    pe.wait_ge(w_lo_made, g + 1)
                    pe.wait_ge(v_lo_made, g * GP + (j + 1))
                    if place == 0 and j == 0 and later(b):
                        pe.wait_ge(acc_kept, b)
                    for half in range(2):
                        for v in (v_hi, v_lo):
                            mm = nc.tensor.matmul(ps[:, 6 + half, :], wp[s % 2][:, j, :, :].rearrange("p a c -> p (a c)"),
                                                  v[j][:, half * 512:(half + 1) * 512],
                                                  start=place == 0 and j == 0 and v is v_hi,
                                                  stop=place == GROUPS - 1 and j == GP - 1 and v is v_lo)
                    mm.then_inc(applied, 1)

                def extract(b, g):
                    pe.wait_ge(acc_kept, b)
                    pe.wait_ge(decayed, g + 1)
                    for p in range(PAIRS):
                        mm = nc.tensor.matmul(own[:, p * 2 * NT:(p + 1) * 2 * NT], oacc[:, p * P:(p + 1) * P],
                                              mem.c(C_FOLD + p * 2 * NT, P, 2 * NT), start=True, stop=True)
                    mm.then_inc(extracted, 1)

                def body(b):
                    for s in range(GROUPS):
                        g = b * GROUPS + s
                        turn(g, 4)
                        turn_scores(g - 1)
                        turn(g, 5)
                        if s == 0:
                            pe.wait_ge(q_lo_made, b + 1)
                        score(g, 0, 0)
                        turn(g, 6)
                        score(g, 0, 1)
                        turn(g, 7)
                        apply(b, s - 2, 0)
                        turn(g + 1, 0)
                        apply(b, s - 2, 1)
                        turn(g + 1, 1)
                        accumulate(b, s - 1)
                        turn(g + 1, 2)
                        apply(b, s - 2, 2)
                        score(g, 1, 0)
                        turn(g + 1, 3)
                        apply(b, s - 2, 3)
                        score(g, 1, 1)
                        if s == 2 and later(b):
                            extract(b, g - 1)

                for k in range(4):
                    turn(0, k)
                steps(pe, body)
                turn_scores(LAST)
                for j in range(GP):
                    apply(NB - 1, GROUPS - 2, j)
                accumulate(NB - 1, GROUPS - 1)
                for j in range(GP):
                    apply(NB - 1, GROUPS - 1, j)
                extract(NB, LAST)

            @block.scalar
            def _(act):
                def part_keys(g, k):
                    if not exists(g):
                        return
                    j, half = k // 2, k % 2
                    act.wait_ge(k_turned, g * UNITS + k + 1)
                    if k % 4 == 0 and later(g):
                        act.wait_ge(scored, (g - 1) * 2 + k // 4 + 1)
                    nc.scalar.copy(kt_hi[j // 2][:, 4 * half:4 * half + 4, j % 2 * PAGE:(j % 2 + 1) * PAGE],
                                   ps[:, k % 4, :].rearrange("p (r c) -> p r c", c=P)).then_inc(kt_hi_made, 1)

                def part_queries(b):
                    if later(b):
                        act.wait_ge(scored, b * (2 * GROUPS))
                    else:
                        act.wait_ge(q_zeroed, 1)
                    for e in range(2):
                        cp = nc.scalar.copy(q_cols(e, 0), q_src(b, e))
                    cp.then_inc(q_hi_made, 1)

                def keep_rows(g, sub):
                    if not exists(g):
                        return
                    act.wait_ge(scored, g * 2 + sub + 1)
                    if later(g):
                        act.wait_ge(turned, g)
                    cols = slice(sub * 2 * PAGE, (sub + 1) * 2 * PAGE)
                    nc.scalar.copy(zr[:, cols], ps[:, 4, cols]).then_inc(rows_kept, 1)

                def softplus_tail(g):
                    if not exists(g):
                        return
                    act.wait_ge(sized, g + 1)
                    nc.scalar.activation(soft[:, :], soft[:, :], ACT.Exp).then_inc(softened, 1)
                    act.wait_ge(softened, g * 2 + 1)
                    nc.scalar.activation(soft[:, :], soft[:, :], ACT.Ln, bias=1.0).then_inc(softened, 1)

                def weight(g, par):
                    if not exists(g):
                        return
                    act.wait_ge(decayed, g + 1)
                    if later(g):
                        act.wait_ge(w_lo_made, g)
                    nc.scalar.activation(wf[:, :], zb[par][:, :], ACT.Exp).then_inc(weighted, 1)

                def keep_acc(b):
                    act.wait_ge(applied, b * NPAGE)
                    if later(b, 2):
                        act.wait_ge(extracted, b - 1)
                    nc.scalar.copy(oacc[:, :], ps[:, 6:8, :].rearrange("p b c -> p (b c)")).then_inc(acc_kept, 1)

                def body(b):
                    for s in range(GROUPS):
                        g = b * GROUPS + s
                        keep_rows(g - 1, 1)
                        if s == 0:
                            part_queries(b)
                        if s == 2 and later(b):
                            keep_acc(b)
                        part_keys(g, 4)
                        part_keys(g, 5)
                        softplus_tail(g - 1)
                        part_keys(g, 6)
                        keep_rows(g, 0)
                        part_keys(g, 7)
                        for k in range(3):
                            part_keys(g + 1, k)
                        weight(g - 1, (s - 1) % 2)
                        part_keys(g + 1, 3)

                act.preload_act_table_set("natural_log_exp_and_others")
                for k in range(4):
                    part_keys(0, k)
                steps(act, body)
                keep_rows(LAST, 1)
                softplus_tail(LAST)
                weight(LAST, 1)
                keep_acc(NB)

            @block.vector
            def _(dve):
                def part_keys(g, k):
                    if not exists(g):
                        return
                    j, half = k // 2, k % 2
                    dve.wait_ge(kt_hi_made, g * UNITS + k + 1)
                    at = (slice(None), slice(4 * half, 4 * half + 4), slice(j % 2 * PAGE, (j % 2 + 1) * PAGE))
                    nc.vector.tensor_tensor(kt_lo[j // 2][at], ps[:, k % 4, :].rearrange("p (r c) -> p r c", c=P),
                                            kt_hi[j // 2][at].bitcast(F32), ALU.subtract).then_inc(kt_lo_made, 1)

                def part_queries(b):
                    dve.wait_ge(q_hi_made, b + 1)
                    for e in range(2):
                        op = nc.vector.tensor_tensor(q_cols(e, 1), q_src(b, e), q_cols(e, 0).bitcast(F32), ALU.subtract)
                    op.then_inc(q_lo_made, 1)

                def part_values(g, j):
                    if not exists(g):
                        return
                    dve.wait_ge(v_in[j], g * 16 + 16)
                    if later(g):
                        dve.wait_ge(applied, (g - 1) * GP + (j + 1))
                    nc.vector.tensor_copy(v_hi[j][:, :], vp[j][:, :]).then_inc(v_hi_made, 1)

                def decay(g, par):
                    if not exists(g):
                        return
                    dve.wait_ge(summed, g + 1)
                    nc.vector.tensor_tensor(zb[par][:, :], zb[par][:, :], sums, ALU.subtract).then_inc(decayed, 1)

                def part_weights(g, par):
                    if not exists(g):
                        return
                    dve.wait_ge(weighted, g + 1)
                    if later(g, 2):
                        dve.wait_ge(applied, (g - 1) * GP)
                    w = wf[:, :].rearrange("p (j c) -> p j c", j=GP)
                    nc.vector.tensor_copy(wp[par][:, :, 0, :], w).then_inc(w_hi_made, 1)
                    dve.wait_ge(w_hi_made, g + 1)
                    nc.vector.tensor_tensor(wp[par][:, :, 1, :], w, wp[par][:, :, 0, :].bitcast(F32),
                                            ALU.subtract).then_inc(w_lo_made, 1)

                def bias(g, par):
                    if not exists(g):
                        return
                    dve.wait_ge(turned, g + 1)
                    if later(g, 2):
                        dve.wait_ge(weighted, g - 1)
                    nc.vector.tensor_tensor(
                        zb[par][:, :].rearrange("p (j c) -> p j c", j=GP),
                        turned_z.rearrange("p (j c) -> p j c", j=GP),
                        mem.biasT[:, :, :].rearrange("p h t -> p (h t)").unsqueeze(1).to_broadcast([P, GP, HT]),
                        ALU.add).then_inc(biased, 1)
                    dve.wait_ge(biased, g + 1)
                    if later(g):
                        dve.wait_ge(sp_made, g)
                    nc.vector.scalar_tensor_tensor(out=soft[:, :], in0=zb[par][:, :], scalar=-1.0, in1=zb[par][:, :],
                                                   op0=ALU.mult, op1=ALU.min).then_inc(sized, 1)

                def softplus(b, s):
                    g, par = b * GROUPS + s, s % 2
                    if not exists(g):
                        return
                    dve.wait_ge(softened, g * 2 + 2)
                    if later(g, 2):
                        dve.wait_ge(summed, g - 1)
                        dve.wait_ge(lost_made, lost_ready(b, s - 2) + (s % GROUPS != 1))
                    nc.vector.scalar_tensor_tensor(out=sp_[par][:, :], in0=zb[par][:, :], scalar=0.0, in1=soft[:, :],
                                                   op0=ALU.max, op1=ALU.add).then_inc(sp_made, 1)

                def add(b):
                    dve.wait_ge(extracted, b)
                    for e in range(2):
                        to = mem.oT[e * HD:(e + 1) * HD, :, bass.ds(b * NT + (SEQ - NT), NT)]
                        op = nc.vector.tensor_tensor(to, own[e * HD:(e + 1) * HD, :].rearrange(
                            "p (a c) -> p a c", c=2 * NT)[:, :, e * NT:(e + 1) * NT], to, ALU.add)
                    op.then_inc(added, 1)

                def body(b):
                    for s in range(GROUPS):
                        g = b * GROUPS + s
                        if s == 0:
                            part_queries(b)
                        part_keys(g, 4)
                        part_values(g - 2, 3)
                        bias(g - 1, (s - 1) % 2)
                        part_keys(g, 5)
                        if s == 3 and later(b):
                            add(b)
                        softplus(b, s - 1)
                        part_keys(g, 6)
                        part_keys(g, 7)
                        part_keys(g + 1, 0)
                        part_values(g - 1, 0)
                        part_keys(g + 1, 1)
                        part_values(g - 1, 1)
                        decay(g - 1, (s - 1) % 2)
                        part_keys(g + 1, 2)
                        part_weights(g - 1, (s - 1) % 2)
                        part_keys(g + 1, 3)
                        part_values(g - 1, 2)

                nc.vector.memset(qb[:, :].bitcast(F32), 0.0).then_inc(q_zeroed, 1)
                dve.wait_ge(q_zeroed, 1)
                for k in range(4):
                    part_keys(0, k)
                steps(dve, body)
                bias(LAST, 1)
                part_values(LAST - 1, 3)
                softplus(NB - 1, GROUPS - 1)
                part_values(LAST, 0)
                part_values(LAST, 1)
                decay(LAST, 1)
                part_weights(LAST, 1)
                part_values(LAST, 2)
                part_values(LAST, 3)
                add(NB)

            @block.gpsimd
            def _(pool):
                def part_values(g, j):
                    if not exists(g):
                        return
                    pool.wait_ge(v_hi_made, g * GP + (j + 1))
                    nc.gpsimd.tensor_tensor(v_lo[j][:, :], vp[j][:, :], v_hi[j][:, :].bitcast(F32),
                                            ALU.subtract).then_inc(v_lo_made, 1)

                def lose(b, s):
                    if s < 0:
                        b, s = b - 1, s + GROUPS
                    g = b * GROUPS + s
                    if not exists(g):
                        return
                    par = s % 2
                    done = b * LOST_STEPS + LOST_BEFORE[s]
                    pool.wait_ge(sp_made, g + 1)
                    if later(g):
                        pool.wait_ge(summed, g)
                    if later(g):
                        pool.wait_ge(lost_made, done)
                    if s == 0:
                        nc.gpsimd.tensor_tensor(lost[0][:, GP, :],
                                                mem.carry[:, bass.ds(b, 1), :].rearrange("p a c -> p (a c)"),
                                                zero[:, :], ALU.add).then_inc(lost_made, 1)
                        done += 1
                    for i, j in enumerate(range(GP - 1, -1, -1)):
                        if j == 0 and s == GROUPS - 1:
                            break
                        to = lost[par][:, j, :] if j else lost[1 - par][:, GP, :]
                        pool.wait_ge(lost_made, done + i)
                        nc.gpsimd.tensor_tensor(to, lost[par][:, j + 1, :],
                                                sp_[par][:, j * HT:(j + 1) * HT], ALU.add).then_inc(lost_made, 1)

                def body(b):
                    for s in range(GROUPS):
                        g = b * GROUPS + s
                        part_values(g - 2, 3)
                        lose(b, s - 1)
                        for j in range(3):
                            part_values(g - 1, j)

                nc.gpsimd.memset(zero[:, :], 0.0).then_inc(zeroed, 1)
                pool.wait_ge(zeroed, 1)
                steps(pool, body)
                part_values(LAST - 1, 3)
                lose(NB - 1, GROUPS - 1)
                for j in range(GP):
                    part_values(LAST, j)


def merge_to_end(nc, mem, ps, a, o, scratch):
    with ExitStack() as ctx:
        W, w_end = Weights.place(nc, ctx, mem, "w", mem.after_mix)
        W_out, W_ffn = W.after(KD), W.after(2 * KD)
        small, end = mem.run(w_end, *[(f"small{i}", [P, T], F32) for i in range(3)])
        assert end <= mem.before_h, (end, mem.before_h)
        with nc.Block(no_gpsimd_drain=True) as block:
            gated, mixed = merge_branches(nc, block, ctx, mem, ps, a, scratch, W, W_out)
            h_ready = project_out(nc, block, ctx, mem, ps, a, scratch, W_out, W_ffn, small, gated, mixed)
            feed_forward(nc, block, ctx, mem, ps, a, o, W_ffn, w_end, h_ready)


def merge_branches(nc, block, ctx, mem, ps, a, scratch, W, W_next):
    sem = lambda name: ctx.enter_context(nc.semaphore("e_" + name))
    specs = [("e_o_hi", [P, PAIRS, T], F32R), ("e_o_lo", [P, PAIRS, T], F32R)] + [
        (f"e_{n}{i}", [P, T], F32) for n in ("gate_a", "gate_p", "mixed") for i in range(2)] + [
        ("e_part_a", [P, T], F32), ("e_part_p", [P, T], F32)]
    tensors, end = mem.run(mem.before_h, *specs)
    assert end <= mem.top_o, (end, mem.top_o)
    o_hi, o_lo = tensors[0:2]
    gate_a, gate_p, mixed = tensors[2:4], tensors[4:6], tensors[6:8]
    part_a, part_p = tensors[8:10]
    o_hi_made, o_lo_made = sem("o_hi_made"), sem("o_lo_made")
    gates_in = [sem(f"gates_in{i}") for i in range(2)]
    gated, mixed_made, hi_made, lo_made = sem("gated"), sem("mixed_made"), sem("hi_made"), sem("lo_made")
    w_attn = a["w_attn_proj"][0].rearrange("(k p) c -> p k c", p=P)
    w_pool = a["w_pool"][0].rearrange("g (k p) c -> g p k c", p=P)
    PK = PT // len(WINDOWS)
    GM = KD // len(WINDOWS)
    AK = (PAIRS - 3, 3)
    KTS = (AK[0], AK[1] + PK)
    pool_in = sem("pool_w_in")
    banks = [[ps[:, 4 * p + 2 * i:4 * p + 2 * i + 2, :] for i in range(2)] for p in range(2)]
    groups = lambda eng, body: (body(0), _loop(eng, 1, len(WINDOWS) - 1, body), body(len(WINDOWS) - 1))
    last = lambda m: isinstance(m, int) and m == KD - 1

    @block.sync
    def _(sp):
        def load(m, g, j):
            W.load(sp, m, 0, w_attn[:, 0:AK[0], bass.ds(m * P, P)], AK[0])
            W.load(sp, m, 1, w_attn[:, AK[0]:PAIRS, bass.ds(m * P, P)], AK[1])
            sp.dma_start(W.raw[1][:, AK[1]:AK[1] + PK, :], w_pool[bass.ds(g, 1), :, :, j * P:(j + 1) * P].rearrange(
                "g p k c -> p (g k) c")).then_inc(pool_in, 16)
            for buf, first in ((gate_a, 0), (gate_p, KD)):
                if later(m, 2):
                    sp.wait_ge(mixed_made, m - 1)
                sp.dma_start(buf[j % 2][:, :].unsqueeze(1), scratch["gates"][bass.ds(m + first, 1), :, :].rearrange(
                    "a p t -> p a t")).then_inc(gates_in[j % 2], 16)

        def body(g):
            for j in range(GM):
                load(g * GM + j, g, j)

        groups(sp, body)

    @block.tensor
    def _(pe):
        def body(g):
            for j in range(GM):
                m, p = g * GM + j, j % 2
                if later(m, 2):
                    pe.wait_ge(gated, 2 * (m - 1))
                ready = None
                if isinstance(m, int) and m == 0:
                    ready = lambda k: pe.wait_ge(o_lo_made, k + 1)
                W.multiply(pe, m, 0, banks[p][0], tile_of(o_hi), tile_of(o_lo), 0, AK[0], stop=False, x_ready=ready)
                W.multiply(pe, m, 1, banks[p][0], tile_of(o_hi), tile_of(o_lo), AK[0], AK[1], start=False,
                           x_ready=ready, last=False)
                group_tile = lambda x: lambda k, half: x[:, bass.ds(g * PK + k, 1), half * HALF:(half + 1) * HALF]
                W.multiply(pe, m, 1, banks[p][1], group_tile(mem.pool_hi), group_tile(mem.pool_lo), 0, PK, at=AK[1])

        groups(pe, body)

    @block.scalar
    def _(act):
        def split_hi(m, b):
            if b == 1:
                act.wait_ge(pool_in, m * 16 + 16)
            W.split_hi(act, m, b, KTS[b])

        def body(g):
            for j in range(GM):
                m = g * GM + j
                for b in range(2):
                    if last(m):
                        W_next.split_hi(act, 0, b)
                    else:
                        split_hi(m + 1, b)
                act.wait_ge(mixed_made, m + 1)
                nc.scalar.copy(mem.mix_hi[:, bass.ds(m, 1), :], mixed[j % 2][:, :].unsqueeze(1)).then_inc(hi_made, 1)

        for b in range(2):
            split_hi(0, b)
        for k in range(PAIRS):
            nc.scalar.copy(o_hi[:, k, :], mem.oT[:, k, :]).then_inc(o_hi_made, 1)
        groups(act, body)

    @block.vector
    def _(dve):
        def gate(m, p):
            dve.wait_ge(gates_in[p], (m - p) // 2 * 32 + 32)
            W.wait_slot(dve, m)
            if later(m):
                dve.wait_ge(mixed_made, m)
            nc.vector.tensor_tensor(by_halves(part_a[:, :]), halves(banks[p][0]),
                                    by_halves(gate_a[p][:, :]), ALU.mult).then_inc(gated, 1)
            nc.vector.scalar_tensor_tensor(out=by_halves(part_p[:, :]), in0=halves(banks[p][1]),
                                           scalar=mem.vec[:, bass.ds(m + V_PSCALE, 1)],
                                           in1=by_halves(gate_p[p][:, :]), op0=ALU.mult,
                                           op1=ALU.mult).then_inc(gated, 1)

        def body(g):
            for j in range(GM):
                m = g * GM + j
                if last(m):
                    W_next.split_lo(dve, 0, 0)
                    part(m - 1, 1 - j % 2)
                    gate(m, j % 2)
                    W_next.split_lo(dve, 0, 1)
                    continue
                for b in range(2):
                    W.split_lo(dve, m + 1, b, KTS[b])
                gate(m, j % 2)
                if later(m):
                    part(m - 1, 1 - j % 2)

        def part(m, p):
            dve.wait_ge(hi_made, m + 1)
            nc.vector.tensor_tensor(mem.mix_lo[:, bass.ds(m, 1), :], mixed[p][:, :].unsqueeze(1),
                                    mem.mix_hi[:, bass.ds(m, 1), :].bitcast(F32), ALU.subtract).then_inc(lo_made, 1)

        for b in range(2):
            W.split_lo(dve, 0, b, KTS[b])
        for k in range(PAIRS):
            dve.wait_ge(o_hi_made, k + 1)
            nc.vector.tensor_tensor(o_lo[:, k, :], mem.oT[:, k, :], o_hi[:, k, :].bitcast(F32),
                                    ALU.subtract).then_inc(o_lo_made, 1)
        groups(dve, body)
        part(KD - 1, (KD - 1) % 2)

    @block.gpsimd
    def _(pool):
        def body(g):
            for j in range(GM):
                m = g * GM + j
                pool.wait_ge(gated, 2 * m + 2)
                if later(m, 2):
                    pool.wait_ge(lo_made, m - 1)
                nc.gpsimd.tensor_tensor(mixed[j % 2][:, :], part_a[:, :], part_p[:, :], ALU.add).then_inc(mixed_made, 1)

        groups(pool, body)

    return gated, lo_made


def project_out(nc, block, ctx, mem, ps, a, scratch, W, W_next, small, gated, mixed):
    sem = lambda name: ctx.enter_context(nc.semaphore("f_" + name))
    (x0, x1, sq), total = small, mem.total
    xr = (x0, x1)
    x_in = [sem(f"x_in{i}") for i in range(2)]
    h_made, hi_made, lo_made, squared, totalled = (
        sem("h_made"), sem("hi_made"), sem("lo_made"), sem("squared"), sem("totalled"))
    cleared = sem("cleared")
    w_out = a["w_out"][0].rearrange("(b k p) c -> b p k c", b=2, p=P)
    banks = [ps[:, 2 * p:2 * p + 2, :] for p in range(2)]
    is_last = lambda m: isinstance(m, int) and m == KD - 1

    @block.sync
    def _(sp):
        def load(m, i, p):
            for b in range(2):
                W.load(sp, m, b, w_out[b][:, :, bass.ds(m * P, P)])
            if later(m, 2):
                sp.wait_ge(h_made, m - 1)
            sp.dma_start(xr[p][:, :].unsqueeze(1), scratch["xT"][bass.ds(m, 1), :, :].rearrange(
                "a p t -> p a t")).then_inc(x_in[p], 16)

        by_pairs(sp, 0, KD, load)

    @block.tensor
    def _(pe):
        def step(m, i, p):
            if later(m, 2):
                pe.wait_ge(h_made, m - 1)
            else:
                pe.wait_ge(gated, 2 * KD - 2)
            for b in range(2):
                if isinstance(m, int) and m == 0:
                    pe.wait_ge(mixed, (KD - 1, KD)[b])
                W.multiply(pe, m, b, banks[p], tile_of(mem.mix_hi), tile_of(mem.mix_lo), b * W.KT,
                           start=b == 0, stop=b == 1)

        by_pairs(pe, 0, KD, step)

    @block.scalar
    def _(act):
        def step(m, i, p):
            for b in range(2):
                (W_next if is_last(m) else W).split_hi(act, 0 if is_last(m) else m + 1, b)
            act.wait_ge(h_made, m + 1)
            if later(m):
                act.wait_ge(totalled, m)
            h = mem.hT[:, bass.ds(m, 1), :]
            nc.scalar.activation(mem.hn_hi[:, bass.ds(m, 1), :], h, ACT.Copy,
                                 scale=mem.vec[:, bass.ds(m + V_NORM2, 1)]).then_inc(hi_made, 1)
            nc.scalar.square(sq[:, :].unsqueeze(1), h).then_inc(squared, 1)

        by_pairs(act, 0, KD, step, tail=2)

    @block.vector
    def _(dve):
        def step(m, i, p):
            for b in range(2):
                (W_next if is_last(m) else W).split_lo(dve, 0 if is_last(m) else m + 1, b)
            dve.wait_ge(x_in[p], i * 16 + 16)
            W.wait_slot(dve, m)
            nc.vector.tensor_tensor(by_halves(mem.hT[:, bass.ds(m, 1), :].rearrange("p a t -> p (a t)")),
                                    halves(banks[p]), by_halves(xr[p][:, :]), ALU.add).then_inc(h_made, 1)
            dve.wait_ge(hi_made, m + 1)
            nc.vector.scalar_tensor_tensor(out=mem.hn_lo[:, bass.ds(m, 1), :], in0=mem.hT[:, bass.ds(m, 1), :],
                                           scalar=mem.vec[:, bass.ds(m + V_NORM2, 1)],
                                           in1=mem.hn_hi[:, bass.ds(m, 1), :].bitcast(F32),
                                           op0=ALU.mult, op1=ALU.subtract).then_inc(lo_made, 1)

        by_pairs(dve, 0, KD, step, tail=2)

    @block.gpsimd
    def _(pool):
        nc.gpsimd.memset(total[:, :], 0.0).then_inc(cleared, 1)
        pool.wait_ge(cleared, 1)

        def step(m, i, p):
            pool.wait_ge(squared, m + 1)
            if later(m):
                pool.wait_ge(totalled, m)
            nc.gpsimd.tensor_tensor(total[:, :], total[:, :], sq[:, :], ALU.add).then_inc(totalled, 1)

        by_pairs(pool, 0, KD, step)

    return h_made, lo_made, totalled


def feed_forward(nc, block, ctx, mem, ps, a, o, W, w_end, h_ready):
    SLOTS = 2 * CF + KD
    DOWN = (6, CF - 6)
    FULL = (Weights.KT, Weights.KT)
    sem = lambda name: ctx.enter_context(nc.semaphore("g_" + name))
    (act_hi, act_lo, gate, up, silu, hidden, y0, y1), end = mem.run(
        mem.free, ("g_act_hi", [P, CF, T], F32R), ("g_act_lo", [P, CF, T], F32R), ("g_gate", [P, T], F32),
        ("g_up", [P, T], F32), ("g_silu", [P, T], F32), ("g_hidden", [P, T], F32),
        ("g_y0", [P, T], F32), ("g_y1", [P, T], F32))
    assert end <= mem.after_mix, (end, mem.after_mix)
    (out0, out1, outS0, outS1), end = mem.run(
        w_end, ("g_out0", [P, SEQ // P, P], F32), ("g_out1", [P, SEQ // P, P], F32),
        ("g_outS0", [NSAMP, P], F32), ("g_outS1", [NSAMP, P], F32))
    assert end <= mem.before_h
    y, out, out_s = (y0, y1), (out0, out1), (outS0, outS1)
    h_made, h_parts, totalled = h_ready
    summed, rooted, inverted = sem("summed"), sem("rooted"), sem("inverted")
    turned, out_made, stored = sem("turned"), sem("out_made"), [sem(f"stored{i}") for i in range(2)]
    y_out = [o["y_prompt"][0].rearrange("(b p) d -> p b d", p=P), o["y_sample"].rearrange("b t d -> (b t) d")]
    vacated = sem("vacated")
    silu_made, hidden_made, hi_made, lo_made = sem("silu_made"), sem("hidden_made"), sem("hi_made"), sem("lo_made")
    w_gu = a["w_gate_up"][0].rearrange("(b k p) c -> b p k c", b=2, p=P)
    w_down = a["w_down"][0].rearrange("(f p) c -> p f c", p=P)
    banks = [ps[:, 2 * p:2 * p + 2, :] for p in range(2)]

    def chunk(eng, c, hidden_slots, down_slot):
        hidden_slots(c, 0, FULL)
        with eng.Fori(1, CF - 1) as f:
            hidden_slots(c, f, FULL)
        hidden_slots(c, CF - 1, DOWN)
        for m in range(2):
            down_slot(c, m, m, DOWN)
        with eng.Fori(1, KD // 2 - 1) as i:
            for p in range(2):
                down_slot(c, i * 2 + p, p, DOWN)
        down_slot(c, KD - 2, 0, DOWN)
        down_slot(c, KD - 1, 1, None if isinstance(c, int) and c == CHUNKS - 1 else FULL)

    def chunks(eng, hidden_slots, down_slot):
        chunk(eng, 0, hidden_slots, down_slot)
        with eng.Fori(1, CHUNKS - 1) as c:
            chunk(eng, c, hidden_slots, down_slot)
        chunk(eng, CHUNKS - 1, hidden_slots, down_slot)

    is_last = lambda c: isinstance(c, int) and c == CHUNKS - 1
    hidden_n = lambda c, f, which: c * SLOTS + f * 2 + which
    down_n = lambda c, m: c * SLOTS + m + 2 * CF

    @block.sync
    def _(sp):
        def hidden_slots(c, f, after):
            for which in range(2):
                for b in range(2):
                    W.load(sp, hidden_n(c, f, which), b,
                           w_gu[b][:, :, bass.ds((c * CF + f + which * FT) * P, P)])

        def down_slot(c, m, p, after):
            for b in range(2):
                W.load(sp, down_n(c, m), b, w_down[:, bass.ds(c * CF + b * DOWN[0], DOWN[b]), bass.ds(m * P, P)],
                       DOWN[b])
            if is_last(c) and later(m, 2):
                store(m - 2, p)

        def store(m, p):
            sp.wait_ge(out_made, m + 1)
            cols = bass.ds(m * P, P)
            sp.dma_start(y_out[0][:, :, cols], out[p][:, :, :]).then_inc(stored[p], 16)
            sp.dma_start(y_out[1][:, cols], out_s[p][:, :]).then_inc(stored[p], 16)

        chunks(sp, hidden_slots, down_slot)
        for m in (KD - 2, KD - 1):
            store(m, m % 2)
        for p in range(2):
            sp.wait_ge(stored[p], KD // 2 * 32)

    @block.tensor
    def _(pe):
        def hidden_slots(c, f, after):
            for which in range(2):
                n = hidden_n(c, f, which)
                if later(n, 2):
                    pe.wait_ge(vacated, n - 1)
                else:
                    pe.wait_ge(h_made, KD - 1 + n)
                for b in range(2):
                    if isinstance(n, int) and n == 0:
                        pe.wait_ge(h_parts, (KD - 1, KD)[b])
                    W.multiply(pe, n, b, banks[which], tile_of(mem.hn_hi), tile_of(mem.hn_lo), b * W.KT,
                               start=b == 0, stop=b == 1)
                if isinstance(n, int) and n == 0:
                    pe.wait_ge(totalled, KD)
                    for half in range(2):
                        mm = nc.tensor.matmul(ps[:, 4 + half, 0:HALF], mem.c(C_ONES),
                                              mem.total[:, half * HALF:(half + 1) * HALF], start=True, stop=True)
                    mm.then_inc(summed, 1)

        def turn(n, m, p):
            pe.wait_ge(vacated, n + 1)
            if later(m, 2):
                pe.wait_ge(out_made, m - 1)
            for t in range(SEQ // P):
                nc.tensor.transpose(ps[:, 4 + p, t * P:(t + 1) * P], y[p][:, t * P:(t + 1) * P], mem.c(C_IDENT))
            nc.tensor.transpose(ps[0:NSAMP, 6 + p, 0:P], y[p][:, SEQ:T], mem.c(C_IDENT)).then_inc(turned, 1)

        def down_slot(c, m, p, after):
            n = down_n(c, m)
            pe.wait_ge(vacated, n - 1)
            for b in range(2):
                if b == 1 and is_last(c) and later(m):
                    turn(n - 1, m - 1, 1 - p)
                pe.wait_ge(lo_made, c * CF + (DOWN[0] if b == 0 else CF))
                W.multiply(pe, n, b, banks[p], tile_of(act_hi), tile_of(act_lo), b * DOWN[0], DOWN[b],
                           start=b == 0, stop=b == 1)

        chunks(pe, hidden_slots, down_slot)
        turn(down_n(CHUNKS - 1, KD - 1), KD - 1, 1)

    @block.scalar
    def _(act):
        def split_next(n, after):
            if after is not None:
                for b in range(2):
                    W.split_hi(act, n + 1, b, after[b])

        def hidden_slots(c, f, after):
            n, h = hidden_n(c, f, 0), c * CF + f
            split_next(n, FULL)
            if isinstance(n, int) and n == 0:
                act.wait_ge(summed, 1)
                nc.scalar.activation(by_halves(mem.total[:, :]), ps[:, 4:6, 0:HALF], ACT.Sqrt, scale=1.0 / D,
                                     bias=mem.vec[:, 63:64]).then_inc(rooted, 1)
            act.wait_ge(vacated, n + 1)
            if later(h):
                act.wait_ge(hidden_made, h)
            nc.scalar.activation(silu[:, :], gate[:, :], ACT.Silu).then_inc(silu_made, 1)
            split_next(n + 1, after)
            act.wait_ge(hidden_made, h + 1)
            if later(c):
                W.wait_slot(act, c * SLOTS - 1)
            nc.scalar.copy(act_hi[:, bass.ds(f, 1), :], hidden[:, :].unsqueeze(1)).then_inc(hi_made, 1)

        def keep(m, p):
            act.wait_ge(turned, m + 1)
            if later(m, 2):
                act.wait_ge(stored[p], (m - p) // 2 * 32)
            nc.scalar.copy(out[p][:, :, :], ps[:, 4 + p, :].rearrange("p (b c) -> p b c", c=P))
            nc.scalar.copy(out_s[p][:, :], ps[0:NSAMP, 6 + p, 0:P]).then_inc(out_made, 1)

        def down_slot(c, m, p, after):
            split_next(down_n(c, m), after)
            if is_last(c) and later(m):
                keep(m - 1, 1 - p)

        chunks(act, hidden_slots, down_slot)
        keep(KD - 1, 1)

    @block.vector
    def _(dve):
        def split_next(n, after):
            if after is not None:
                for b in range(2):
                    W.split_lo(dve, n + 1, b, after[b])

        def scale(n, p, to):
            W.wait_slot(dve, n)
            nc.vector.tensor_tensor(by_halves(to[:, :]), halves(banks[p]), by_halves(mem.rstd2[:, :]),
                                    ALU.mult).then_inc(vacated, 1)

        def hidden_slots(c, f, after):
            n, h = hidden_n(c, f, 0), c * CF + f
            split_next(n, FULL)
            if isinstance(n, int) and n == 0:
                dve.wait_ge(rooted, 1)
                nc.vector.reciprocal(mem.rstd2[:, :], mem.total[:, :]).then_inc(inverted, 1)
                dve.wait_ge(inverted, 1)
            if later(h):
                dve.wait_ge(silu_made, h)
            scale(n, 0, gate)
            split_next(n + 1, after)
            if later(h):
                dve.wait_ge(hidden_made, h)
            scale(n + 1, 1, up)
            dve.wait_ge(silu_made, h + 1)
            dve.wait_ge(vacated, n + 2)
            if later(h):
                dve.wait_ge(lo_made, h)
            nc.vector.tensor_tensor(hidden[:, :], silu[:, :], up[:, :], ALU.mult).then_inc(hidden_made, 1)
            dve.wait_ge(hi_made, h + 1)
            nc.vector.tensor_tensor(act_lo[:, bass.ds(f, 1), :], hidden[:, :].unsqueeze(1),
                                    act_hi[:, bass.ds(f, 1), :].bitcast(F32), ALU.subtract).then_inc(lo_made, 1)

        def down_slot(c, m, p, after):
            n = down_n(c, m)
            split_next(n, after)
            W.wait_slot(dve, n)
            if later(c):
                dve.wait_ge(vacated, c * SLOTS)
            h = by_halves(mem.hT[:, bass.ds(m, 1), :].rearrange("p a t -> p (a t)"))
            if is_last(c) and later(m, 2):
                dve.wait_ge(turned, m - 1)
            to = by_halves(y[p][:, :]) if is_last(c) else h
            nc.vector.tensor_tensor(to, halves(banks[p]), h, ALU.add).then_inc(vacated, 1)

        chunks(dve, hidden_slots, down_slot)


OUTPUTS = [
    ("y_prompt", (1, SEQ, D)), ("y_sample", (NB, NT, D)),
    ("k_prompt", (1, 1, SEQ, H, HD)), ("v_prompt", (1, 1, SEQ, H, HD)), ("pool_prompt", (1, 1, HIST, PW)),
    ("k_sample", (1, NB, NT, H, HD)), ("v_sample", (1, NB, NT, H, HD)), ("pool_sample", (1, NB, HIST, PW)),
]

def build(nc, a, o):
    scratch = {
        "xT": nc.dram_tensor("x_feature_major", (KD, P, T), F32, kind="Internal").ap(),
        "gates": nc.dram_tensor("gates", (2 * KD, P, T), F32, kind="Internal").ap(),
    }
    mem = Memory(nc)
    with nc.psum_tensor("ps", [P, 8, 512], F32) as ps:
        norm_inputs(nc, mem, ps, a, scratch)
        project_in(nc, mem, ps, a, o, scratch)
        attend_prompt(nc, mem, ps, a)
        attend_cache(nc, mem, ps, a)
        merge_to_end(nc, mem, ps, a, o, scratch)


def kernel(**inputs):
    import concourse.bacc as bacc
    from concourse.bass_utils import run_bass_kernel_spmd

    nc = bacc.Bacc("TRN2", target_bir_lowering=False, num_devices=1)
    arrays = {name: np.ascontiguousarray(x) for name, x in inputs.items()}
    arrays["const"], arrays["mask"] = constants()
    a = {name: nc.dram_tensor(name, x.shape, mybir.dt.from_np(x.dtype), kind="ExternalInput").ap()
         for name, x in arrays.items()}
    o = {name: nc.dram_tensor(name, shape, F32, kind="ExternalOutput").ap() for name, shape in OUTPUTS}
    build(nc, a, o)
    got = run_bass_kernel_spmd(nc, [arrays], core_ids=[0]).results[0]
    return tuple(got[name] for name, _ in OUTPUTS)
```

```python
from contextlib import ExitStack

import numpy as np

import concourse.bass as bass
from concourse import mybir

F32 = mybir.dt.float32
F32R = mybir.dt.float32r
I32 = mybir.dt.int32
ACT = mybir.ActivationFunctionType
ALU = mybir.AluOpType

P = 128
D = 2048
SEQ = 512
NB, NT = 8, 4
NSAMP = NB * NT
T = SEQ + NSAMP
HALF = T // 2
H, HD = 16, 64
AW = H * HD
PAIRS = AW // P
HT = H * NT
PW = D // 2
PT = PW // P
HIST = 15
WINDOWS = (2, 4, 8, 16)
SEG = HIST + NT
UW = HIST + SEQ + NB * SEG
FF = 5632
KD = D // P
IN_TILES = (3 * AW + PW + 2 * D) // P
PAGE = 128
NPAGE = 16
EPS = 1e-6
MASKED = -1e30
FT = FF // P
CHUNKS = 4
CF = FT // CHUNKS
TOKEN_TILES = [(i * P, min(P, T - i * P)) for i in range(-(-T // P))]

SCORE_SEGS = [(0, 0), (512, 1), (1024, 2), (896, 3)]
SAMPLE_COL = 1280
SCORES = SAMPLE_COL + NSAMP

C_IDENT, C_ONES, C_PAIR, C_TRI, C_FOLD = 0, P, 2 * P, 3 * P, 4 * P
C_CORR = C_FOLD + HT
C_WIDTH = C_CORR + 4 * 16
V_NORM1, V_NORM2, V_PSCALE, V_QG, V_KG = 0, KD, 2 * KD, 3 * KD, 3 * KD + 1
V_ROWS = 3 * KD + 2


def constants():
    c = np.zeros((P, C_WIDTH), np.float32)
    r = np.arange(P)
    c[:, C_IDENT:C_IDENT + P] = np.eye(P)
    c[:, C_ONES:C_ONES + P] = 1.0
    c[:, C_PAIR:C_PAIR + P] = (r[:, None] // HD == r[None, :] // HD)
    c[:, C_TRI:C_TRI + P] = (r[:, None] >= r[None, :])
    c[:, C_FOLD:C_FOLD + HT] = (r[:, None] % HT == np.arange(HT)[None, :])
    for g, w in enumerate(WINDOWS):
        c[:, C_CORR + 16 * g:C_CORR + 16 * g + 16] = w / np.minimum(w, np.arange(16) + 1.0)
    mask = np.zeros((P, SCORES), np.float32)
    for col, kb in SCORE_SEGS:
        mask[:, col:col + P] = np.where(r[:, None] < r[None, :], 0.0, MASKED)
    q = np.arange(NSAMP)
    seen = (r[:, None] // NT == q[None, :] // NT) & (r[:, None] % NT < q[None, :] % NT)
    mask[:, SAMPLE_COL:] = np.where(seen & (r[:, None] < NSAMP), 0.0, MASKED)
    return c, mask


def later(n, k=1):
    return not isinstance(n, int) or n >= k


def by_pairs(eng, start, stop, step, head=2, tail=0):
    for n in range(start, start + head):
        step(n, n // 2, n % 2)
    with eng.Fori(0, (stop - tail - start - head) // 2) as i:
        for p in range(2):
            step(i * 2 + (start + head + p), i + (start + head) // 2, p)
    for n in range(stop - tail, stop):
        step(n, n // 2, n % 2)


class Memory:

    def __init__(self, nc):
        base = -(-nc.sbuf_base // 64) * 64
        size = (nc.sbuf_top - base) // 64 * 64
        self.size = size

        def at(name, shape, dtype, offset):
            width = int(np.prod(shape[1:])) * 4
            assert 0 <= offset and offset + width <= size, (name, offset, width, size)
            return nc.alloc_sbuf_tensor_at(name, shape, dtype, offset=base + offset)

        def run(offset, *specs):
            out = []
            for name, shape, dtype in specs:
                out.append(at(name, shape, dtype, offset))
                offset += -(-int(np.prod(shape[1:])) * 4 // 32) * 32
            return out, offset

        self.at, self.run = at, run
        tok = 4 * T
        (self.const, self.vec, self.bias, self.biasT, self.pages, self.carry), low = run(
            0, ("const", [P, C_WIDTH], F32), ("vec", [P, 64], F32), ("bias", [P, H], F32),
            ("biasT", [P, H, NT], F32), ("pages", [1, NB * NPAGE], I32), ("carry", [P, NB, HT], F32))
        self.low = low
        self.after_q = low + PAIRS * tok
        (self.qT, self.kT, self.v_nat, self.v_new, self.uT), self.after_qkv = run(
            low, ("qT", [P, PAIRS, T], F32), ("kT", [P, PAIRS, T], F32),
            ("v_nat", [P, SEQ // P, AW], F32), ("v_new", [NSAMP, AW], F32), ("uT", [P, PT, UW], F32))
        top = size - 2 * KD * tok
        self.xn_hi, self.xn_lo = run(top, ("xn_hi", [P, KD, T], F32R), ("xn_lo", [P, KD, T], F32R))[0]
        self.top = top
        self.top_o = size - 3 * PAIRS * tok
        self.oT, self.pool_hi, self.pool_lo = run(
            self.top_o, ("oT", [P, PAIRS, T], F32), ("pool_hi", [P, PT, T], F32R),
            ("pool_lo", [P, PT, T], F32R))[0]
        self.free = -(-4 * (C_WIDTH + 64) // 32) * 32
        (self.mix_hi, self.mix_lo), self.after_mix = run(
            self.free, ("mix_hi", [P, KD, T], F32R), ("mix_lo", [P, KD, T], F32R))
        (self.hn_hi, self.hn_lo) = run(top, ("hn_hi", [P, KD, T], F32R), ("hn_lo", [P, KD, T], F32R))[0]
        (self.hT, self.total, self.rstd2), end = run(
            top - (KD + 2) * tok, ("hT", [P, KD, T], F32), ("total", [P, T], F32), ("rstd2", [P, T], F32))
        assert end <= top
        self.before_h = top - (KD + 2) * tok

    def c(self, col, rows=P, width=P):
        return self.const[0:rows, col:col + width]


class Weights:

    KT = 8

    def __init__(self, nc, buffers, semaphores, first=0):
        self.nc, self.buffers, self.semaphores, self.first = nc, buffers, semaphores, first
        self.raw, self.hi, self.lo = buffers
        self.loaded, self.hi_made, self.lo_made, self.used = semaphores

    @classmethod
    def place(cls, nc, ctx, mem, phase, offset):
        shape = [P, cls.KT, P]
        specs = [(f"{phase}_{part}{b}", shape, F32 if part == "raw" else F32R) for part, b in (
            ("raw", 0), ("raw", 1), ("hi", 0), ("lo", 0), ("hi", 1), ("lo", 1))]
        (raw0, raw1, hi0, lo0, hi1, lo1), end = mem.run(offset, *specs)
        semaphores = [[ctx.enter_context(nc.semaphore(f"{phase}_w_{event}{b}")) for b in range(2)]
                      for event in ("loaded", "hi_made", "lo_made", "used")]
        return cls(nc, ((raw0, raw1), (hi0, hi1), (lo0, lo1)), semaphores), end

    def after(self, slots):
        return Weights(self.nc, self.buffers, self.semaphores, self.first + slots)

    def load(self, sp, n, b, src, kts=KT):
        n = n + self.first
        if later(n):
            sp.wait_ge(self.lo_made[b], n)
        sp.dma_start(self.raw[b][:, 0:kts, :], src).then_inc(self.loaded[b], 16)

    def split_hi(self, act, n, b, kts=KT):
        n = n + self.first
        act.wait_ge(self.loaded[b], n * 16 + 16)
        if later(n):
            act.wait_ge(self.used[b], n)
        self.nc.scalar.copy(self.hi[b][:, 0:kts, :], self.raw[b][:, 0:kts, :]).then_inc(self.hi_made[b], 1)

    def split_lo(self, dve, n, b, kts=KT):
        n = n + self.first
        dve.wait_ge(self.hi_made[b], n + 1)
        self.nc.vector.tensor_tensor(self.lo[b][:, 0:kts, :], self.raw[b][:, 0:kts, :],
                                     self.hi[b][:, 0:kts, :].bitcast(F32),
                                     ALU.subtract).then_inc(self.lo_made[b], 1)

    def multiply(self, pe, n, b, banks, x_hi, x_lo, kt0=0, kts=KT, start=True, stop=True, at=0,
                 x_ready=None, last=True):
        pe.wait_ge(self.lo_made[b], n + (self.first + 1))
        for k in range(kts):
            if x_ready:
                x_ready(kt0 + k)
            for i, (w, x) in enumerate(((self.hi, x_hi), (self.hi, x_lo), (self.lo, x_hi))):
                for half in range(2):
                    mm = self.nc.tensor.matmul(
                        banks[:, half, 0:HALF], w[b][:, at + k, :], x(kt0 + k, half),
                        start=start and k == 0 and i == 0, stop=stop and k == kts - 1 and i == 2)
        if last:
            mm.then_inc(self.used[b], 1)

    def wait_slot(self, eng, n):
        eng.wait_ge(self.used[1], n + (self.first + 1))


def tile_of(x):
    return lambda k, half: x[:, k, half * HALF:(half + 1) * HALF]


def halves(banks):
    return banks[:, :, 0:HALF]


def by_halves(x):
    return x.rearrange("p (h t) -> p h t", h=2)


def inputs_to_attention(nc, mem, ps, a, o, scratch, merge):
    with ExitStack() as ctx:
        W, end = Weights.place(nc, ctx, mem, "b", mem.after_qkv)
        (rstd,), end = mem.run(end, ("rstd1", [P, T], F32))
        w_in = a["w_in"][0].rearrange("(b k p) c -> b p k c", b=2, p=P)
        with nc.Block(no_gpsimd_drain=True) as block:
            x_steps, x_parts, spread, rstd_made, wait_stored = norm_inputs(
                nc, block, ctx, mem, ps, a, scratch, W, w_in, rstd, end)
            start, kept = project_in(nc, block, ctx, mem, ps, a, o, scratch, W, w_in, end, rstd,
                                     x_steps, x_parts, spread, rstd_made, wait_stored)
            prompt = attend_prompt(nc, block, ctx, mem, ps, a, start, kept)
            attend_cache(nc, block, ctx, mem, ps, a, prompt, merge)


def norm_inputs(nc, block, ctx, mem, ps, a, scratch, W, w_in, rstd, after):
    sem = lambda name: ctx.enter_context(nc.semaphore("a_" + name))
    tiles = TOKEN_TILES
    NU = KD // 4
    RING = 4
    KEEP = 8
    tensors, end = mem.run(
        mem.low, *[(f"a_x{i}", [P, D], F32) for i in range(len(tiles))],
        ("a_xg", [P, RING, 4, P], F32), ("a_xt", [P, KEEP, 4, P], F32), ("a_diag", [P, len(tiles), P], F32),
        ("a_vrows", [KD, P], F32), ("a_vrest", [V_ROWS - KD, P], F32), ("a_brow", [1, H], F32),
        ("a_ms", [P, 8], F32), ("a_root", [P, 8], F32), ("a_inv", [P, 8], F32))
    assert end <= mem.after_qkv
    junk = mem.at("a_junk", [P, D], F32, after)
    xin = tensors[0:len(tiles)]
    xg, xt, diag, vrows, vrest, brow, ms, root, inv = tensors[len(tiles):]
    x_in = [[sem(f"x_in{i}_{c}") for c in range(1 if i else NU)] for i in range(len(tiles))]
    const_in, g_in, params_in = sem("const_in"), sem("g_in"), sem("params_in")
    g_turned, g_made, vec_made, bias_made = sem("g_turned"), sem("g_made"), sem("vec_made"), sem("bias_made")
    ms_set, squared, var_made, rooted, inverted, diag_made, spread, rstd_made = (
        sem("ms_set"), sem("squared"), sem("var_made"), sem("rooted"), sem("inverted"), sem("diag_made"),
        sem("spread"), sem("rstd_made"))
    turned, weighted, x_kept, hi_made, lo_made = (
        sem("turned"), sem("weighted"), sem("x_kept"), sem("hi_made"), sem("lo_made"))
    raw_out = [sem(f"raw_out{i}") for i in range(KEEP)]
    units = [(i, j) for i in range(len(tiles)) for j in range(NU)]
    COLS = len(tiles)
    SPLIT_AT = (11, len(units) - 1)
    n_params = 2 + 4 + 2

    def source(i):
        if i < SEQ // P:
            return a["x_prompt"][0, i * P:(i + 1) * P, :]
        return a["x_sample"].rearrange("b t d -> (b t) d")

    @block.sync
    def _(sp):
        def load_x(i):
            n, w = tiles[i][1], D // len(x_in[i])
            for c, here in enumerate(x_in[i]):
                sp.dma_start(xin[i][0:n, c * w:(c + 1) * w], source(i)[:, c * w:(c + 1) * w]).then_inc(here, 16)

        rows = lambda name: a[name][0].rearrange("(k p) -> k p", p=P)

        def load_params():
            for name, row in (("norm2_g", V_NORM2), ("pool_scale", V_PSCALE)):
                sp.dma_start(vrest[row - KD:row, :], rows(name)).then_inc(params_in, 16)
            for name, row in (("q_norm_g", V_QG), ("k_norm_g", V_KG)):
                for e in range(2):
                    sp.dma_start(vrest[row - KD:row - KD + 1, e * HD:(e + 1) * HD], a[name]).then_inc(params_in, 16)
            sp.dma_start(brow[:, :], a["sb_bias"]).then_inc(params_in, 16)
            sp.dma_start(mem.pages[:, :], a["page_table"].rearrange("b n -> (b n)").unsqueeze(0)).then_inc(params_in, 16)

        sp.dma_start(mem.const[:, :], a["const"]).then_inc(const_in, 16)
        sp.dma_start(vrows[:, :], rows("norm1_g")).then_inc(g_in, 16)
        load_x(0)
        load_x(1)
        LAG = 2

        def keep(u):
            (i, j), (t0, n) = units[u], tiles[units[u][0]]
            sp.dma_start(scratch["xT"][4 * j:4 * j + 4, :, t0:t0 + n].rearrange("k p t -> p k t"),
                         xt[:, u % KEEP, :, 0:n]).then_inc(raw_out[u % KEEP], 16)

        for u in range(len(units)):
            sp.wait_ge(x_kept, u + 1)
            if u >= LAG:
                keep(u - LAG)
            if u in (0, 2, 6):
                load_x({0: 2, 2: 3, 6: 4}[u])
            if u == 8:
                load_params()
            if u in (4, 9):
                b = (4, 9).index(u)
                W.load(sp, 0, b, w_in[b][:, :, 0:P])
        for u in range(len(units) - LAG, len(units)):
            keep(u)

    def wait_stored(sp):
        for r in range(KEEP):
            sp.wait_ge(raw_out[r], 16 * len(range(r, len(units), KEEP)))

    @block.tensor
    def _(pe):
        pe.wait_ge(const_in, 16)
        pe.wait_ge(g_in, 16)
        nc.tensor.transpose(ps[:, 0, 0:KD], vrows[:, :], mem.c(C_IDENT, KD, KD)).then_inc(g_turned, 1)
        for u, (i, j) in enumerate(units):
            n = tiles[i][1]
            pe.wait_ge(x_in[i][0 if i else j], 16)
            if u >= RING:
                pe.wait_ge(x_kept, u - RING + 1)
            for k in range(4):
                tr = nc.tensor.transpose(ps[:, 2 + u % RING, k * P:k * P + n],
                                         xin[i][0:n, (4 * j + k) * P:(4 * j + k + 1) * P], mem.c(C_IDENT, n, n))
            tr.then_inc(turned, 1)
        pe.wait_ge(g_made, 1)

    def spread_vectors(pe):
        pe.wait_ge(diag_made, COLS)
        pe.wait_ge(params_in, 16 * n_params)
        pe.wait_ge(x_kept, len(units))
        for i, (t0, n) in enumerate(tiles):
            nc.tensor.matmul(ps[:, 6 + t0 // SEQ, t0 % SEQ:t0 % SEQ + n], mem.c(C_ONES, n), diag[0:n, i, 0:n],
                             start=True, stop=True)
        nc.tensor.transpose(ps[:, 5, 0:V_ROWS - KD], vrest[:, :], mem.c(C_IDENT, V_ROWS - KD, V_ROWS - KD))
        nc.tensor.matmul(ps[:, 4, 0:H], mem.c(C_ONES, 1), brow[:, :],
                         start=True, stop=True).then_inc(spread, 1)

    @block.scalar
    def _(act):
        act.wait_ge(ms_set, 1)
        for i, (t0, n) in enumerate(tiles):
            for j in range(NU):
                u = NU * i + j
                act.wait_ge(weighted, u + 1)
                nc.scalar.copy(mem.xn_hi[:, 4 * j:4 * j + 4, t0:t0 + n], xg[:, u % RING, :, 0:n]).then_inc(hi_made, 1)
                if u in SPLIT_AT:
                    W.split_hi(act, 0, SPLIT_AT.index(u))
            for here in x_in[i]:
                act.wait_ge(here, 16)
            if i:
                act.wait_ge(squared, i)
            nc.scalar.activation(junk[0:n, :], xin[i][0:n, :], ACT.Square, accum_out=ms[0:n, i:i + 1]).then_inc(squared, 1)
        act.wait_ge(var_made, 1)
        nc.scalar.activation(root[:, 0:COLS], ms[:, 0:COLS], ACT.Sqrt).then_inc(rooted, 1)
        act.wait_ge(spread, 1)
        nc.scalar.copy(rstd[:, 0:SEQ], ps[:, 6, :])
        nc.scalar.copy(rstd[:, SEQ:T], ps[:, 7, 0:NSAMP]).then_inc(rstd_made, 1)
        nc.scalar.copy(mem.bias[:, :], ps[:, 4, 0:H]).then_inc(bias_made, 1)
        act.wait_ge(bias_made, 1)
        nc.scalar.copy(mem.biasT[:, :, :], mem.bias[:, :].unsqueeze(2).to_broadcast([P, H, NT])).then_inc(bias_made, 1)

    @block.vector
    def _(dve):
        nc.vector.memset(ms[:, :], 1.0).then_inc(ms_set, 1)
        dve.wait_ge(g_turned, 1)
        nc.vector.tensor_copy(mem.vec[:, 0:KD], ps[:, 0, 0:KD]).then_inc(g_made, 1)
        dve.wait_ge(g_made, 1)
        for u, (i, j) in enumerate(units):
            n = tiles[i][1]
            dve.wait_ge(turned, u + 1)
            if u >= RING:
                dve.wait_ge(lo_made, u - RING + 1)
            g = mem.vec[:, V_NORM1 + 4 * j:V_NORM1 + 4 * j + 4].unsqueeze(2).to_broadcast([P, 4, n])
            src = ps[:, 2 + u % RING, :].rearrange("p (k t) -> p k t", k=4)[:, :, 0:n]
            nc.vector.tensor_tensor(xg[:, u % RING, :, 0:n], src, g, ALU.mult).then_inc(weighted, 1)
            if u >= KEEP:
                dve.wait_ge(raw_out[u % KEEP], 16 * (u // KEEP))
            nc.vector.tensor_copy(xt[:, u % KEEP, :, 0:n], src).then_inc(x_kept, 1)
            if u in SPLIT_AT:
                W.split_lo(dve, 0, SPLIT_AT.index(u))
        dve.wait_ge(squared, COLS)
        nc.vector.tensor_scalar(ms[:, 0:COLS], ms[:, 0:COLS], 1.0 / D, EPS, ALU.mult, ALU.add).then_inc(var_made, 1)
        dve.wait_ge(rooted, 1)
        nc.vector.reciprocal(inv[:, 0:COLS], root[:, 0:COLS]).then_inc(inverted, 1)
        dve.wait_ge(inverted, 1)
        for i in range(COLS):
            nc.vector.tensor_scalar(diag[:, i, :], mem.c(C_IDENT), inv[:, i:i + 1], None, ALU.mult).then_inc(diag_made, 1)
        dve.wait_ge(spread, 1)
        nc.vector.tensor_copy(mem.vec[:, KD:V_ROWS], ps[:, 5, 0:V_ROWS - KD]).then_inc(vec_made, 1)
        dve.wait_ge(vec_made, 1)
        nc.vector.tensor_scalar(mem.vec[:, V_QG:V_QG + 1], mem.vec[:, V_QG:V_QG + 1], HD ** -0.5,
                                None, ALU.mult).then_inc(vec_made, 1)
        dve.wait_ge(vec_made, 2)

    @block.gpsimd
    def _(pool):
        for u, (i, j) in enumerate(units):
            t0, n = tiles[i]
            pool.wait_ge(hi_made, u + 1)
            nc.gpsimd.tensor_tensor(mem.xn_lo[:, 4 * j:4 * j + 4, t0:t0 + n], xg[:, u % RING, :, 0:n],
                                    mem.xn_hi[:, 4 * j:4 * j + 4, t0:t0 + n].bitcast(F32),
                                    ALU.subtract).then_inc(lo_made, 1)

    return lambda k: len(units) - NU + k // 4 + 1, lo_made, spread_vectors, rstd_made, wait_stored


Q, K, V, U, GATE = range(5)
KIND_START = (0, 8, 16, 24, 32, IN_TILES)
GATES_KEPT = 32 * 8 + 16 * (IN_TILES - 32) // 2


def kind_of(n):
    return max(k for k in range(5) if KIND_START[k] <= n)


def project_in(nc, block, ctx, mem, ps, a, o, scratch, W, w_in, offset, rstd, x_steps, x_parts, spread, rstd_made,
               wait_stored):
    sem = lambda name: ctx.enter_context(nc.semaphore("b_" + name))
    (raw0, raw1, sq, root, inv, kn0, kn1, nat0, nat1, natS0, natS1), end = mem.run(
        offset, ("b_t0", [P, T], F32), ("b_t1", [P, T], F32), ("b_sq", [P, T], F32),
        ("b_root", [P, T], F32), ("b_inv", [P, T], F32), ("b_kn0", [P, T], F32), ("b_kn1", [P, T], F32),
        ("b_nat0", [P, 4, P], F32), ("b_nat1", [P, 4, P], F32),
        ("b_natS0", [NSAMP, P], F32), ("b_natS1", [NSAMP, P], F32))
    start = PromptStart(nc, ctx, mem, end, offset + 5 * 4 * T)
    assert start.end <= mem.top, (start.end, mem.top)
    res, kn, nat, nat_s = (raw0, raw1), (kn0, kn1), (nat0, nat1), (natS0, natS1)
    res_made = sem("res_made")
    gate_made = sem("gate_made")
    squared, summed, rooted = sem("squared"), sem("summed"), sem("rooted")
    inverted, normed = sem("inverted"), sem("normed")
    u_placed = sem("u_placed")
    turned, nat_made = sem("turned"), sem("nat_made")
    kept = [sem(f"kept{i}") for i in range(2)]
    v_out = sem("v_out")
    mm_banks = [ps[:, 2 * p:2 * p + 2, :] for p in range(2)]
    sum_banks = ps[:, 4:6, :]
    first_turned = KIND_START[K]
    k_out = [o["k_prompt"][0, 0].rearrange("(b p) h d -> p b (h d)", p=P),
             o["k_sample"][0].rearrange("b t h d -> (b t) (h d)")]
    state = a["state_pool"][0]
    for_each = lambda eng, step: [by_pairs(eng, KIND_START[k], KIND_START[k + 1], lambda n, i, p, k=k: step(
        n, i, p, k, kind_of(n - 1) if isinstance(n, int) and n else k,
        kind_of(n - 2) if isinstance(n, int) and n > 1 else k), head=4 if k == K else 2, tail=2 * (k == GATE)) for k in range(5)]

    @block.sync
    def _(sp):
        def columns(n, b):
            return w_in[b][:, :, bass.ds(n * P, P)]

        def step(n, i, p, kind, k1, k2):
            if not (isinstance(n, int) and n == IN_TILES - 1):
                for b in range(2):
                    W.load(sp, n + 1, b, columns(n + 1, b))
            if later(n, 2):
                store(n - 2, i - 1, p, k2)
            if isinstance(n, int) and n == KIND_START[GATE]:
                store_values()
            if isinstance(n, int) and n == KIND_START[GATE] + 1:
                sp.wait_ge(normed, KIND_START[V])
                start.load(sp, a)

        def store_values():
            sp.wait_ge(nat_made, KIND_START[U] - first_turned)
            sp.dma_start(o["v_prompt"][0, 0].rearrange("(b p) h d -> p b (h d)", p=P),
                         mem.v_nat[:, :, :]).then_inc(v_out, 16)
            sp.dma_start(o["v_sample"][0].rearrange("b t h d -> (b t) (h d)"), mem.v_new[:, :]).then_inc(v_out, 16)

        def store(n, i, p, kind):
            if kind in (K, U):
                cols = bass.ds((n - KIND_START[kind]) * P, P)
                sp.wait_ge(nat_made, n - (first_turned - 1))
                if kind == K:
                    sp.dma_start(k_out[0][:, :, cols], nat[p][:, :, :]).then_inc(kept[p], 16)
                    sp.dma_start(k_out[1][:, cols], nat_s[p][:, :]).then_inc(kept[p], 16)
                else:
                    sp.dma_start(o["pool_prompt"][0, 0][:, cols], nat[p][P - HIST:P, 0, :]).then_inc(kept[p], 16)
                    sp.dma_start(o["pool_sample"][0][:, HIST - NT:HIST, cols],
                                 nat_s[p][:, :]).then_inc(kept[p], 16)
            if kind == GATE:
                sp.wait_ge(gate_made, n - (KIND_START[GATE] - 1))
                sp.dma_start(scratch["gates"][bass.ds(n - KIND_START[GATE], 1), :, :].rearrange("a p t -> p a t"),
                             res[p][:, :].unsqueeze(1)).then_inc(kept[p], 16)

        sp.dma_start(o["pool_sample"][0][:, 0:HIST - NT, :], state[:, NT:HIST, :]).then_inc(v_out, 16)
        for_each(sp, step)
        for n in (IN_TILES - 2, IN_TILES - 1):
            store(n, n // 2, n % 2, GATE)
        sp.wait_ge(v_out, 48)
        wait_stored(sp)

    @block.tensor
    def _(pe):
        def step(n, i, p, kind, k1, k2):
            if later(n, 2):
                pe.wait_ge(res_made, n - 1)
            if isinstance(n, int) and n == IN_TILES - 1:
                pe.wait_ge(nat_made, KIND_START[GATE] - first_turned)
                start.turn(pe, ps)
            first = isinstance(n, int) and n == 0
            x_ready = (lambda k: pe.wait_ge(x_parts, x_steps(k))) if first else None
            early = W.KT // 2
            W.multiply(pe, n, 0, mm_banks[p], tile_of(mem.xn_hi), tile_of(mem.xn_lo), 0, early, stop=False,
                       x_ready=x_ready, last=False)
            if later(n) and k1 in (Q, K):
                pe.wait_ge(squared, n)
                if later(n, 2):
                    pe.wait_ge(rooted, n - 1)
                for h in range(2):
                    mm = nc.tensor.matmul(sum_banks[:, h, 0:HALF], mem.c(C_PAIR),
                                          sq[:, h * HALF:(h + 1) * HALF], start=True, stop=True)
                mm.then_inc(summed, 1)
            W.multiply(pe, n, 0, mm_banks[p], tile_of(mem.xn_hi), tile_of(mem.xn_lo), early, W.KT - early,
                       start=False, stop=False, at=early, x_ready=x_ready)
            if first:
                spread(pe)
            W.multiply(pe, n, 1, mm_banks[p], tile_of(mem.xn_hi), tile_of(mem.xn_lo), W.KT, start=False,
                       x_ready=x_ready)
            if k1 in (K, V, U) and later(n, first_turned + 1):
                src = (kn if k1 == K else res)[1 - p]
                m = n - first_turned
                if k1 == K:
                    pe.wait_ge(normed, n)
                else:
                    pe.wait_ge(res_made, n)
                if later(n, first_turned + 2):
                    pe.wait_ge(nat_made, m - 1)
                for t in range(3 if k1 == U else 0, 4):
                    nc.tensor.transpose(ps[:, 6, (t % (3 if k1 == U else 4)) * P:(t % (3 if k1 == U else 4) + 1) * P],
                                        src[:, t * P:(t + 1) * P], mem.c(C_IDENT))
                nc.tensor.transpose(ps[0:NSAMP, 7, 0:P], src[:, SEQ:T], mem.c(C_IDENT)).then_inc(turned, 1)

        for_each(pe, step)

    @block.scalar
    def _(act):
        def step(n, i, p, kind, k1, k2):
            last = isinstance(n, int) and n == IN_TILES - 1
            if later(n) and k1 in (Q, K):
                act.wait_ge(summed, n)
                if later(n, 2):
                    act.wait_ge(inverted, n - 1)
                nc.scalar.activation(by_halves(root[:, :]), halves(sum_banks), ACT.Sqrt,
                                     scale=1.0 / HD, bias=mem.vec[:, 63:64]).then_inc(rooted, 1)
            if not last:
                W.split_hi(act, n + 1, 0)
                W.split_hi(act, n + 1, 1)
            act.wait_ge(res_made, n + 1)
            if kind == GATE:
                nc.scalar.activation(res[p][:, :], res[p][:, :], ACT.Sigmoid).then_inc(gate_made, 1)
            if kind in (Q, K):
                if later(n):
                    act.wait_ge(summed, n)
                nc.scalar.square(sq[:, :], res[p][:, :]).then_inc(squared, 1)
            if k1 in (K, V, U) and later(n, first_turned + 1):
                to_natural(n - 1, i, p, k1)

        def to_natural(n, i, p, kind):
            act.wait_ge(turned, n - (first_turned - 1))
            q = 1 - p
            if kind == V:
                cols = bass.ds((n - KIND_START[V]) * P, P)
                nc.scalar.copy(mem.v_nat[:, :, cols], ps[:, 6, :].rearrange("p (b c) -> p b c", c=P))
                nc.scalar.copy(mem.v_new[:, cols], ps[0:NSAMP, 7, 0:P]).then_inc(nat_made, 1)
                return
            pair = i - q if isinstance(i, int) else i - q
            before = pair - KIND_START[K] // 2 if kind == K else pair - KIND_START[U] // 2 + 4
            if not isinstance(before, int) or before > 0:
                act.wait_ge(kept[q], before * 32)
            if kind == K:
                nc.scalar.copy(nat[q][:, :, :], ps[:, 6, :].rearrange("p (b c) -> p b c", c=P))
            else:
                nc.scalar.copy(nat[q][:, 0, :], ps[:, 6, 0:P])
            nc.scalar.copy(nat_s[q][:, :], ps[0:NSAMP, 7, 0:P]).then_inc(nat_made, 1)

        for_each(act, step)

    @block.vector
    def _(dve):
        def step(n, i, p, kind, k1, k2):
            last = isinstance(n, int) and n == IN_TILES - 1
            if last:
                start.place(dve, ps)
            q = 1 - p
            if later(n) and k1 in (Q, K):
                dve.wait_ge(rooted, n)
                if later(n, 2):
                    dve.wait_ge(normed, n - 1)
                nc.vector.reciprocal(inv[:, :], root[:, :]).then_inc(inverted, 1)
                dve.wait_ge(inverted, n)
                g = mem.vec[:, (V_QG, V_KG)[k1]:(V_QG, V_KG)[k1] + 1]
                m = n - (KIND_START[k1] + 1)
                to = (mem.qT, mem.kT)[k1][:, bass.ds(m, 1), :].rearrange("p a t -> p (a t)")
                first = nc.vector.scalar_tensor_tensor(out=to, in0=res[q][:, :], scalar=g, in1=inv[:, :],
                                                       op0=ALU.mult, op1=ALU.mult)
                if k1 == Q:
                    first.then_inc(normed, 1)
                else:
                    if later(n, first_turned + 3):
                        dve.wait_ge(turned, n - (first_turned + 2))
                    nc.vector.scalar_tensor_tensor(out=kn[q][:, :], in0=res[q][:, :], scalar=g, in1=inv[:, :],
                                                   op0=ALU.mult, op1=ALU.mult).then_inc(normed, 1)
            if not last:
                W.split_lo(dve, n + 1, 0)
            if later(n) and k1 == U:
                dve.wait_ge(res_made, n)
                m = bass.ds(n - (KIND_START[U] + 1), 1)
                nc.vector.tensor_copy(mem.uT[:, m, HIST:HIST + SEQ], res[q][:, 0:SEQ].unsqueeze(1))
                nc.vector.tensor_copy(
                    mem.uT[:, m, HIST + SEQ:UW].rearrange("p a (b s) -> p (a b) s", b=NB)[:, :, HIST:SEG],
                    res[q][:, SEQ:T].rearrange("p (b t) -> p b t", b=NB)).then_inc(u_placed, 1)
            W.wait_slot(dve, n)
            if later(n, 2):
                if k2 in (Q, K):
                    dve.wait_ge(normed, n - 1)
                if k2 in (V, U):
                    dve.wait_ge(turned, n - (first_turned + 1))
                if k2 == U:
                    dve.wait_ge(u_placed, n - (KIND_START[U] + 1))
                if k2 == GATE and later(n, KIND_START[GATE] + 2):
                    dve.wait_ge(kept[p], 32 * 8 + (i - KIND_START[GATE] // 2) * 16)
            nc.vector.tensor_tensor(by_halves(res[p][:, :]), halves(mm_banks[p]), by_halves(rstd[:, :]),
                                    ALU.mult).then_inc(res_made, 1)
            if not last:
                W.split_lo(dve, n + 1, 1)

        nc.vector.memset(mem.vec[:, 63:64], EPS)
        dve.wait_ge(rstd_made, 1)
        for_each(dve, step)

    return start, kept


class PromptStart:

    def __init__(self, nc, ctx, mem, offset, state_at):
        sem = lambda name: ctx.enter_context(nc.semaphore("s_" + name))
        self.nc, self.mem, self.begin = nc, mem, offset
        (self.mask, self.ks0, self.qs0, self.vs0, self.vn0), self.end = mem.run(
            offset, ("s_mask", [P, SCORES], F32), ("s_ks0", [P, SEQ + P], F32), ("s_qs0", [P, T], F32),
            ("s_vs0", [P, SEQ // P, P], F32), ("s_vn0", [NSAMP, P], F32))
        self.state = mem.at("s_state", [NB * HIST, PW], F32, state_at)
        self.state_in, self.mask_in, self.state_turned, self.u_ready, self.keys_staged, self.values_staged = (
            sem("state_in"), sem("mask_in"), sem("state_turned"), sem("u_ready"), sem("keys_staged"), sem("values_staged"))

    def load(self, sp, a):
        mem = self.mem
        sp.dma_start(self.state[:, :], a["state_pool"][0].rearrange("b r c -> (b r) c")).then_inc(self.state_in, 16)
        sp.dma_start(self.mask[:, :], a["mask"]).then_inc(self.mask_in, 16)
        sp.dma_start(self.qs0[:, :], mem.qT[:, 0, :]).then_inc(self.keys_staged, 16)
        sp.dma_start(self.ks0[:, 0:T], mem.kT[:, 0, :]).then_inc(self.keys_staged, 16)
        sp.dma_start(self.vs0[:, :, :], mem.v_nat[:, :, 0:P]).then_inc(self.values_staged, 16)
        sp.dma_start(self.vn0[:, :], mem.v_new[:, 0:P]).then_inc(self.values_staged, 16)

    def turn(self, pe, ps):
        pe.wait_ge(self.state_in, 16)
        for m in range(PT):
            tr = self.nc.tensor.transpose(ps[:, 6 + m // 4, m % 4 * P:m % 4 * P + NB * HIST],
                                          self.state[:, m * P:(m + 1) * P], self.mem.c(C_IDENT, NB * HIST, NB * HIST))
        tr.then_inc(self.state_turned, 1)

    def place(self, dve, ps):
        dve.wait_ge(self.state_turned, 1)
        for m in range(PT):
            cp = self.nc.vector.tensor_copy(
                self.mem.uT[:, m, HIST + SEQ:UW].rearrange("p (b s) -> p b s", b=NB)[:, :, 0:HIST],
                ps[:, 6 + m // 4, m % 4 * P:m % 4 * P + NB * HIST].rearrange("p (b s) -> p b s", b=NB))
        cp.then_inc(self.u_ready, 1)


def attend_prompt(nc, block, ctx, mem, ps, a, start, kept):
    sem = lambda name: ctx.enter_context(nc.semaphore("c_" + name))
    SC = [P, SCORES]
    (zb0, zb1, zb2, zb3, soft, w0, w1, sp_, ks1, vs1, vn1), end = mem.run(
        mem.after_qkv, ("c_zb0", SC, F32), ("c_zb1", SC, F32), ("c_zb2", SC, F32), ("c_zb3", SC, F32),
        ("c_soft", SC, F32), ("c_w0", SC, F32), ("c_w1", SC, F32), ("c_sp", SC, F32),
        ("c_ks1", [P, SEQ + P], F32), ("c_vs1", [P, SEQ // P, P], F32), ("c_vn1", [NSAMP, P], F32))
    assert end <= start.begin, (end, start.begin)
    (hi, lo, qs1, win0, win1), end = mem.run(
        start.end, ("c_hi", SC, F32R), ("c_lo", SC, F32R), ("c_qs1", [P, T], F32),
        ("c_win0", [P, UW], F32), ("c_win1", [P, UW], F32))
    assert end <= mem.top_o, (end, mem.top_o)
    mask, zb, wt = start.mask, (zb0, zb1, zb2, zb3), (w0, w1)
    ks, qs, vs, vn = (start.ks0, ks1), (start.qs0, qs1), (start.vs0, vs1), (start.vn0, vn1)
    tri, ones = (mem.at(f"c_{n}", [P, P], F32R, mem.after_q + i * 4 * P)[:, :] for i, n in enumerate(("tri", "ones")))
    keys_staged, values_staged = ([first, sem(f"{x}_staged1")] for x, first in (
        ("keys", start.keys_staged), ("values", start.values_staged)))
    padded = sem("padded")
    scored, biased, softened = (
        sem("scored"), sem("biased"), sem("softened"))
    summed, decayed, weighted, applied, o_kept = (
        sem("summed"), sem("decayed"), sem("weighted"), sem("applied"), sem("o_kept"))
    triangle_made, sp_made, hi_made, lo_made, pool_step = (
        sem("triangle_made"), sem("sp_made"), sem("hi_made"), sem("lo_made"), sem("pool_step"))
    z_ps = ps[:, 0:3, :].rearrange("p b c -> p (b c)")
    cum_ps = ps[:, 3:6, :].rearrange("p b c -> p (b c)")
    steps = [0]
    exists = lambda j: not isinstance(j, int) or j < H
    heads = lambda eng, body: (body(0), _loop(eng, 1, H // 4 - 1, body), body(H // 4 - 1))

    @block.sync
    def _(sp):
        def stage_keys(r, q):
            if later(r, 2):
                sp.wait_ge(scored, 2 * (r - 1))
            pair = bass.ds(r, 1)
            sp.dma_start(qs[q][:, :].unsqueeze(1), mem.qT[:, pair, :]).then_inc(keys_staged[q], 16)
            sp.dma_start(ks[q][:, 0:T].unsqueeze(1), mem.kT[:, pair, :]).then_inc(keys_staged[q], 16)

        def stage_values(r, q):
            if later(r, 2):
                sp.wait_ge(applied, 2 * (r - 1))
            cols = bass.ds(r * P, P)
            sp.dma_start(vs[q][:, :, :], mem.v_nat[:, :, cols]).then_inc(values_staged[q], 16)
            sp.dma_start(vn[q][:, :], mem.v_new[:, cols]).then_inc(values_staged[q], 16)

        def stage(r, q):
            if not (isinstance(r, int) and r == PAIRS - 1):
                stage_keys(r + 1, 1 - q)
            if later(r):
                stage_values(r, q)

        sp.wait_ge(scored, 1)
        for p in range(2):
            sp.wait_ge(kept[p], GATES_KEPT)
        by_pairs(sp, 0, PAIRS, lambda r, i, q: stage(r, q), tail=2)

    @block.tensor
    def _(pe):
        def score(j, u):
            pair, e = u // 2 % 2, HD * (u % 2)
            pe.wait_ge(keys_staged[pair], 16 * j_pair(j, u) + 32 - 16 * pair)
            if later(j):
                pe.wait_ge(biased, j)
            for col, kb in SCORE_SEGS:
                nc.tensor.matmul(z_ps[:, col:col + SEQ - kb * P], ks[pair][e:e + HD, kb * P:(kb + 1) * P],
                                 qs[pair][e:e + HD, kb * P:SEQ], start=True, stop=True)
            nc.tensor.matmul(z_ps[:, SAMPLE_COL:SCORES], ks[pair][e:e + HD, SEQ:SEQ + P],
                             qs[pair][e:e + HD, SEQ:T], start=True, stop=True).then_inc(scored, 1)

        def accumulate(j, u):
            if later(j):
                pe.wait_ge(decayed, j)
            def add(part, col, kb):
                for col2, kb2 in sorted(SCORE_SEGS, key=lambda x: x[1]):
                    if kb2 >= kb:
                        nc.tensor.matmul(cum_ps[:, col + (kb2 - kb) * P:col + SEQ - kb * P],
                                         tri if kb2 == kb else ones,
                                         part[:, col2:col2 + SEQ - kb2 * P],
                                         start=kb2 == kb and part is hi, stop=kb2 == 3 and part is lo)

            for part, made in ((hi, hi_made), (lo, lo_made)):
                pe.wait_ge(made, j + 1)
                for col, kb in SCORE_SEGS[0:3]:
                    add(part, col, kb)
            for part in (hi, lo):
                add(part, *SCORE_SEGS[3])
            for part in (hi, lo):
                mm = nc.tensor.matmul(cum_ps[:, SAMPLE_COL:SCORES], tri,
                                      part[:, SAMPLE_COL:SCORES], start=part is hi, stop=part is lo)
            mm.then_inc(summed, 1)

        def apply(j, u):
            pair, e = u // 2 % 2, HD * (u % 2)
            pe.wait_ge(weighted, j + 1)
            if e == 0 and later(j):
                pe.wait_ge(o_kept, j_pair(j, u))
            pe.wait_ge(values_staged[pair], 16 * j_pair(j, u) + 32 - 16 * pair)
            w = wt[u % 2]
            for col, kb in sorted(SCORE_SEGS, key=lambda x: x[1]):
                nc.tensor.matmul(ps[e:e + HD, 6, kb * P:SEQ], vs[pair][:, kb, e:e + HD],
                                 w[:, col:col + SEQ - kb * P], start=kb == 0, stop=kb == 3)
            nc.tensor.matmul(ps[e:e + HD, 7, 0:NSAMP], vn[pair][:, e:e + HD],
                             w[0:NSAMP, SAMPLE_COL:SCORES], start=True, stop=True).then_inc(applied, 1)

        def body(i):
            for u in range(4):
                j = i * 4 + u
                if exists(j + 2):
                    score(j + 2, u + 2)
                accumulate(j, u)
                if later(j):
                    apply(j - 1, u - 1)

        pe.wait_ge(padded, 1)
        pe.wait_ge(start.u_ready, 1)
        score(0, 0)
        score(1, 1)
        pe.wait_ge(triangle_made, 1)
        heads(pe, body)
        apply(H - 1, 3)

    @block.scalar
    def _(act):
        def size(j, u):
            act.wait_ge(biased, j + 1)
            if later(j):
                act.wait_ge(sp_made, j)
            nc.scalar.activation(soft[:, :], zb[u % 4][:, :], ACT.Abs).then_inc(softened, 1)
            act.wait_ge(softened, j * 3 + 1)
            nc.scalar.activation(soft[:, :], soft[:, :], ACT.Exp, scale=-1.0).then_inc(softened, 1)

        def softplus_tail(j):
            act.wait_ge(softened, j * 3 + 2)
            nc.scalar.activation(soft[:, :], soft[:, :], ACT.Ln, bias=1.0).then_inc(softened, 1)

        def weight(j, u):
            act.wait_ge(decayed, j + 1)
            if later(j, 2):
                act.wait_ge(applied, j - 1)
            nc.scalar.activation(wt[u % 2][:, :], zb[u % 4][:, :], ACT.Exp).then_inc(weighted, 1)

        def keep(j, u):
            act.wait_ge(applied, j + 1)
            r = bass.ds(j_pair(j, u), 1)
            nc.scalar.copy(mem.oT[:, r, 0:SEQ], ps[:, 6, :].unsqueeze(1))
            nc.scalar.copy(mem.oT[:, r, SEQ:T], ps[:, 7, 0:NSAMP].unsqueeze(1)).then_inc(o_kept, 1)

        def body(i):
            for u in range(4):
                j = i * 4 + u
                if exists(j + 1):
                    softplus_tail(j + 1)
                if u % 2 and later(j, 2):
                    keep(j - 2, u)
                if exists(j + 2):
                    size(j + 2, u + 2)
                weight(j, u)

        act.preload_act_table_set("natural_log_exp_and_others")
        for p in range(2):
            act.wait_ge(kept[p], GATES_KEPT)
        size(0, 0)
        softplus_tail(0)
        size(1, 1)
        heads(act, body)
        keep(H - 1, 3)

    @block.vector
    def _(dve):
        for b in range(2):
            nc.vector.memset(ks[b][:, SEQ + NSAMP:], 0.0)
        nc.vector.memset(mem.uT[:, :, 0:HIST], 0.0).then_inc(padded, 1)
        def bias(j, u):
            dve.wait_ge(scored, j + 1)
            if later(j, 4):
                dve.wait_ge(weighted, j - 3)
            nc.vector.scalar_tensor_tensor(out=zb[u % 4][:, :], in0=z_ps[:, 0:SCORES],
                                           scalar=mem.bias[:, bass.ds(j, 1)], in1=mask[:, :],
                                           op0=ALU.add, op1=ALU.add).then_inc(biased, 1)

        def softplus(j, u):
            dve.wait_ge(softened, j * 3 + 3)
            if later(j):
                dve.wait_ge(lo_made, j)
            nc.vector.scalar_tensor_tensor(out=sp_[:, :], in0=zb[u % 4][:, :], scalar=0.0,
                                           in1=soft[:, :], op0=ALU.max, op1=ALU.add).then_inc(sp_made, 1)

        def part(j):
            dve.wait_ge(sp_made, j + 1)
            if later(j):
                dve.wait_ge(summed, j)
            nc.vector.tensor_copy(hi[:, :], sp_[:, :]).then_inc(hi_made, 1)
            nc.vector.tensor_copy(
                mem.carry[:, :, :].rearrange("p b (h t) -> p b h t", t=NT)[:, :, bass.ds(j, 1), :],
                sp_[:, SAMPLE_COL:SCORES].rearrange("p (b t) -> p b t", t=NT).unsqueeze(2))
            dve.wait_ge(hi_made, j + 1)
            nc.vector.tensor_tensor(lo[:, :], sp_[:, :], hi[:, :].bitcast(F32), ALU.subtract).then_inc(lo_made, 1)

        def decay(j, u):
            dve.wait_ge(summed, j + 1)
            nc.vector.tensor_tensor(zb[u % 4][:, :], zb[u % 4][:, :], cum_ps[:, 0:SCORES],
                                    ALU.subtract).then_inc(decayed, 1)

        def body(i):
            for u in range(4):
                j = i * 4 + u
                if exists(j + 2):
                    bias(j + 2, u + 2)
                if exists(j + 1):
                    softplus(j + 1, u + 1)
                decay(j, u)
                if exists(j + 1):
                    part(j + 1)

        dve.wait_ge(start.mask_in, 16)
        dve.wait_ge(keys_staged[0], 32)
        nc.vector.tensor_copy(tri, mem.c(C_TRI))
        nc.vector.tensor_copy(ones, mem.c(C_ONES)).then_inc(triangle_made, 1)
        bias(0, 0)
        bias(1, 1)
        softplus(0, 0)
        part(0)
        heads(dve, body)

    @block.gpsimd
    def _(pool):
        def link(ins):
            steps[0] += 1
            ins.then_inc(pool_step, 1)
            pool.wait_ge(pool_step, steps[0])

        def new_tokens(x, part):
            if part == 0:
                return x[:, HIST:HIST + SEQ]
            return x[:, HIST + SEQ:UW].rearrange("p (b s) -> p b s", b=NB)[:, :, HIST:SEG]

        def pool_tile(m):
            g = m * P // (PW // len(WINDOWS))
            w = WINDOWS[g]
            src, bufs, n, first = mem.uT[:, m, :], (win0[:, :], win1[:, :]), 1, 0
            turn = 0
            while n < w:
                first += n
                link(nc.gpsimd.tensor_tensor(bufs[turn][:, first:UW], src[:, first:UW],
                                             src[:, first - n:UW - n], ALU.add))
                src, turn, n = bufs[turn], 1 - turn, 2 * n
            corr = mem.const[:, C_CORR + 16 * g:C_CORR + 16 * g + 16]
            link(nc.gpsimd.tensor_tensor(src[:, HIST:HIST + 16], src[:, HIST:HIST + 16], corr, ALU.mult))
            link(nc.gpsimd.tensor_scalar(bufs[turn][:, HIST:UW], src[:, HIST:UW], 1.0 / w, None, ALU.mult))
            link(nc.gpsimd.tensor_tensor(src[:, HIST:UW], bufs[turn][:, HIST:UW], mem.uT[:, m, HIST:UW],
                                         ALU.subtract))
            for part, (t0, t1) in enumerate(((0, SEQ), (SEQ, T))):
                to = [x[:, m, t0:t1] if part == 0 else x[:, m, t0:t1].rearrange("p (b t) -> p b t", b=NB)
                      for x in (mem.pool_hi, mem.pool_lo)]
                link(nc.gpsimd.tensor_copy(to[0], new_tokens(src, part)))
                link(nc.gpsimd.tensor_tensor(to[1], new_tokens(src, part), to[0].bitcast(F32), ALU.subtract))

        pool.wait_ge(padded, 1)
        pool.wait_ge(start.u_ready, 1)
        pool.wait_ge(scored, 1)
        for m in range(PT):
            pool_tile(m)

    return {"keys_staged": keys_staged, "biased": biased, "decayed": decayed, "applied": applied, "o_kept": o_kept,
            "pooled": (pool_step, steps[0])}


def j_pair(j, u):
    if isinstance(j, int):
        return j // 2
    return (j - u % 2) // 2


def _loop(eng, start, stop, body):
    with eng.Fori(start, stop) as i:
        body(i)


def attend_cache(nc, block, ctx, mem, ps, a, prompt, after):
    GP = 4
    GROUPS = NPAGE // GP
    LAST = NB * GROUPS - 1
    sem = lambda name: ctx.enter_context(nc.semaphore("d_" + name))
    page = lambda name, dtype: [(f"d_{name}{j}", [P, AW], dtype) for j in range(GP)]
    group = lambda *names: [(f"d_{name}", [P, GP * HT], F32) for name in names]
    v_hi_specs = page("v_hi", F32R)
    low, end = mem.run(mem.after_q + 2 * 4 * P, *page("k", F32), *page("v", F32), *v_hi_specs[:3],
                       *group("soft", "zb0", "zb1"))
    assert end <= after.begin, (end, after.begin)
    high, end = mem.run(
        after.first_end, v_hi_specs[3], *page("v_lo", F32R),
        *[(f"d_kt_{part}{i}", [P, PAIRS, 2 * PAGE], F32R) for part in ("hi", "lo") for i in range(2)],
        *group("sp0", "sp1", "w"),
        ("d_wp0", [P, GP, 2, HT], F32R), ("d_wp1", [P, GP, 2, HT], F32R),
        ("d_lost0", [P, GP + 1, HT], F32), ("d_lost1", [P, GP + 1, HT], F32),
        ("d_qb", [P, PAIRS * (P + 2 * NT)], F32R), ("d_zr", [P, GP * PAGE], F32), ("d_zero", [P, HT], F32),
        ("d_oacc", [P, AW], F32))
    assert end <= mem.top_o, (end, mem.top_o)
    kp, vp, v_hi, (soft, *zb) = low[0:4], low[4:8], low[8:11] + high[0:1], low[11:14]
    v_lo, kt_hi, kt_lo, sp_, wf, wp, lost = high[1:5], high[5:7], high[7:9], high[9:11], high[11], high[12:14], high[14:16]
    qb, zr, zero, oacc = high[16:20]
    k_in = [sem(f"k_in{j}") for j in range(GP)]
    v_in = [sem(f"v_in{j}") for j in range(GP)]
    k_turned, kt_hi_made, kt_lo_made = sem("k_turned"), sem("kt_hi_made"), sem("kt_lo_made")
    v_hi_made, v_lo_made, v_tail_made = sem("v_hi_made"), sem("v_lo_made"), sem("v_tail_made")
    DVE_TAIL = 2
    q_hi_made, q_lo_made, q_zeroed, zeroed = sem("q_hi_made"), sem("q_lo_made"), sem("q_zeroed"), sem("zeroed")
    scored, rows_kept, turned, biased = sem("scored"), sem("rows_kept"), sem("turned"), sem("biased")
    sized, softened, sp_made, lost_made = sem("sized"), sem("softened"), sem("sp_made"), sem("lost_made")
    summed, decayed, weighted = sem("summed"), sem("decayed"), sem("weighted")
    w_hi_made, w_lo_made = sem("w_hi_made"), sem("w_lo_made")
    applied, acc_kept, extracted, added = sem("applied"), sem("acc_kept"), sem("extracted"), sem("added")
    LOST_STEPS = GROUPS * GP
    LOST_BEFORE = [0] + [1 + GP * s for s in range(1, GROUPS)]

    def lost_ready(b, s):
        if s < 0:
            b, s = b - 1, s + GROUPS
        return b * LOST_STEPS + (LOST_BEFORE[s] + GP - 1 + (s == 0))

    UNITS = 2 * GP
    cache = [a[n][0].rearrange("n p h d -> n p (h d)") for n in ("cache_k", "cache_v")]
    n_pages = cache[0].shape[0]
    stride = P + 2 * NT
    q_cols = lambda e, lo: qb[e * HD:(e + 1) * HD, :].rearrange("p (a c) -> p a c", c=stride)[
        :, :, lo * HT + NT * e:lo * HT + NT * e + NT]
    q_src = lambda b, e: mem.qT[e * HD:(e + 1) * HD, :, bass.ds(b * NT + SEQ, NT)]
    turned_z = ps[:, 5, 0:GP * HT]
    sums = ps[:, 5, GP * HT:2 * GP * HT]
    own = ps[:, 5, GP * HT:GP * HT + PAIRS * 2 * NT]

    def exists(g):
        return not isinstance(g, int) or 0 <= g <= LAST

    def prompt_done(eng):
        eng.wait_ge(prompt["applied"], H)
        eng.wait_ge(*prompt["pooled"])

    def steps(eng, body):
        body(0)
        _loop(eng, 1, NB - 1, body)
        body(NB - 1)

    @block.sync
    def _(sp):
        def load(b, s, which, j):
            g = b * GROUPS + s
            if not exists(g):
                return
            at = b * NPAGE + (NPAGE * (s // GROUPS) + NPAGE - GP * (s % GROUPS + 1) + j)
            page = sp.value_load(mem.pages[0:1, bass.ds(at, 1)], min_val=0, max_val=n_pages - 1)
            if later(g):
                if which == 0:
                    sp.wait_ge(k_turned, (g - 1) * UNITS + (2 * j + 2))
                else:
                    sp.wait_ge(v_lo_made, (g - 1) * GP + (j + 1))
            sp.dma_start((kp, vp)[which][j][:, :], cache[which][bass.ds(page, 1), :, :].rearrange(
                "a p c -> p (a c)")).then_inc((k_in, v_in)[which][j], 16)

        def body(b):
            for s in range(GROUPS):
                load(b, s + 1, 0, 2)
                load(b, s - 1, 1, 3)
                load(b, s + 1, 0, 3)
                load(b, s, 1, 0)
                load(b, s + 2, 0, 0)
                load(b, s, 1, 1)
                load(b, s + 2, 0, 1)
                load(b, s, 1, 2)

        for q in range(2):
            sp.wait_ge(prompt["keys_staged"][q], PAIRS * 16)
        for j in range(GP):
            load(0, 0, 0, j)
        prompt_done(sp)
        for j in range(2):
            load(0, 1, 0, j)
        steps(sp, body)
        load(NB - 1, GROUPS - 1, 1, 3)
        after.load(sp, 0, 0, 0)

    @block.tensor
    def _(pe):
        def turn(g, k):
            if not exists(g):
                return
            j, half = k // 2, k % 2
            pe.wait_ge(k_in[j], g * 16 + 16)
            if later(g) or k >= 4:
                pe.wait_ge(kt_lo_made, g * UNITS + (k - 3))
            for r in range(4):
                tr = nc.tensor.transpose(ps[:, k % 4, r * P:(r + 1) * P],
                                         kp[j][:, (4 * half + r) * P:(4 * half + r + 1) * P], mem.c(C_IDENT))
            tr.then_inc(k_turned, 1)

        def score(g, sub, half):
            pe.wait_ge(kt_lo_made, g * UNITS + 4 * (sub + 1))
            if half == 0 and (later(g) or sub):
                pe.wait_ge(rows_kept, g * 2 + sub)
            for p in range(half * PAIRS // 2, (half + 1) * PAIRS // 2):
                for kt in (kt_hi, kt_lo):
                    mm = nc.tensor.matmul(ps[:, 4, sub * 2 * PAGE:(sub + 1) * 2 * PAGE],
                                          qb[:, p * P:(p + 1) * P], kt[sub][:, p, :],
                                          start=p == 0 and kt is kt_hi, stop=p == PAIRS - 1 and kt is kt_lo)
            if half:
                mm.then_inc(scored, 1)

        def turn_scores(g):
            if not exists(g):
                return
            pe.wait_ge(rows_kept, g * 2 + 2)
            if later(g):
                pe.wait_ge(biased, g)
            for j in range(GP):
                mm = nc.tensor.matmul(ps[:, 5, j * HT:(j + 1) * HT], zr[:, j * PAGE:(j + 1) * PAGE],
                                      mem.c(C_FOLD, P, HT), start=True, stop=True)
            mm.then_inc(turned, 1)

        def accumulate(b, s):
            g = b * GROUPS + s
            if not exists(g):
                return
            pe.wait_ge(sp_made, g + 1)
            pe.wait_ge(lost_made, lost_ready(b, s))
            pe.wait_ge(biased, g + 1)
            if later(g):
                pe.wait_ge(decayed, g)
            if s == 2 and later(b):
                pe.wait_ge(added, b)
            nc.tensor.matmul(sums, mem.c(C_TRI), sp_[s % 2][:, :], start=True, stop=False)
            nc.tensor.matmul(sums, mem.c(C_ONES), lost[s % 2][:, 1:GP + 1, :].rearrange("p g c -> p (g c)"),
                             start=False, stop=True).then_inc(summed, 1)

        def apply(b, s, j):
            g = b * GROUPS + s
            if not exists(g):
                return
            place = s % GROUPS
            pe.wait_ge(w_lo_made, g + 1)
            if isinstance(g, int) and g == LAST and j >= GP - DVE_TAIL:
                pe.wait_ge(v_tail_made, j + 1 - (GP - DVE_TAIL))
            else:
                pe.wait_ge(v_lo_made, g * GP + (j + 1))
            if isinstance(g, int) and g == 0 and j == 0:
                pe.wait_ge(prompt["o_kept"], PAIRS)
            if place == 0 and j == 0 and later(b):
                pe.wait_ge(acc_kept, b)
            for half in range(2):
                for v in (v_hi, v_lo):
                    mm = nc.tensor.matmul(ps[:, 6 + half, :], wp[s % 2][:, j, :, :].rearrange("p a c -> p (a c)"),
                                          v[j][:, half * 512:(half + 1) * 512],
                                          start=place == 0 and j == 0 and v is v_hi,
                                          stop=place == GROUPS - 1 and j == GP - 1 and v is v_lo)
            mm.then_inc(applied, 1)

        def extract(b, g):
            pe.wait_ge(acc_kept, b)
            pe.wait_ge(decayed, g + 1)
            for p in range(PAIRS):
                mm = nc.tensor.matmul(own[:, p * 2 * NT:(p + 1) * 2 * NT], oacc[:, p * P:(p + 1) * P],
                                      mem.c(C_FOLD + p * 2 * NT, P, 2 * NT), start=True, stop=True)
            mm.then_inc(extracted, 1)

        def body(b):
            for s in range(GROUPS):
                g = b * GROUPS + s
                turn(g, 4)
                turn_scores(g - 1)
                turn(g, 5)
                if s == 0:
                    pe.wait_ge(q_lo_made, b + 1)
                score(g, 0, 0)
                turn(g, 6)
                score(g, 0, 1)
                turn(g, 7)
                apply(b, s - 2, 0)
                turn(g + 1, 0)
                apply(b, s - 2, 1)
                turn(g + 1, 1)
                accumulate(b, s - 1)
                turn(g + 1, 2)
                apply(b, s - 2, 2)
                score(g, 1, 0)
                turn(g + 1, 3)
                apply(b, s - 2, 3)
                score(g, 1, 1)
                if s == 2 and later(b):
                    extract(b, g - 1)

        pe.wait_ge(prompt["biased"], H)
        pe.wait_ge(prompt["decayed"], H)
        for k in range(4):
            turn(0, k)
        steps(pe, body)
        turn_scores(LAST)
        for j in range(GP):
            apply(NB - 1, GROUPS - 2, j)
        accumulate(NB - 1, GROUPS - 1)
        for j in range(GP):
            apply(NB - 1, GROUPS - 1, j)
        extract(NB, LAST)

    @block.scalar
    def _(act):
        def part_keys(g, k):
            if not exists(g):
                return
            j, half = k // 2, k % 2
            act.wait_ge(k_turned, g * UNITS + k + 1)
            if k % 4 == 0 and later(g):
                act.wait_ge(scored, (g - 1) * 2 + k // 4 + 1)
            nc.scalar.copy(kt_hi[j // 2][:, 4 * half:4 * half + 4, j % 2 * PAGE:(j % 2 + 1) * PAGE],
                           ps[:, k % 4, :].rearrange("p (r c) -> p r c", c=P)).then_inc(kt_hi_made, 1)

        def part_queries(b):
            if later(b):
                act.wait_ge(scored, b * (2 * GROUPS))
            else:
                act.wait_ge(q_zeroed, 1)
            for e in range(2):
                cp = nc.scalar.copy(q_cols(e, 0), q_src(b, e))
            cp.then_inc(q_hi_made, 1)

        def keep_rows(g, sub):
            if not exists(g):
                return
            act.wait_ge(scored, g * 2 + sub + 1)
            if later(g):
                act.wait_ge(turned, g)
            cols = slice(sub * 2 * PAGE, (sub + 1) * 2 * PAGE)
            nc.scalar.copy(zr[:, cols], ps[:, 4, cols]).then_inc(rows_kept, 1)

        def softplus_tail(g):
            if not exists(g):
                return
            act.wait_ge(sized, g + 1)
            nc.scalar.activation(soft[:, :], soft[:, :], ACT.Exp).then_inc(softened, 1)
            act.wait_ge(softened, g * 2 + 1)
            nc.scalar.activation(soft[:, :], soft[:, :], ACT.Ln, bias=1.0).then_inc(softened, 1)

        def weight(g, par):
            if not exists(g):
                return
            act.wait_ge(decayed, g + 1)
            if later(g):
                act.wait_ge(w_lo_made, g)
            nc.scalar.activation(wf[:, :], zb[par][:, :], ACT.Exp).then_inc(weighted, 1)

        def keep_acc(b):
            act.wait_ge(applied, b * NPAGE)
            nc.scalar.copy(oacc[:, :], ps[:, 6:8, :].rearrange("p b c -> p (b c)")).then_inc(acc_kept, 1)

        def body(b):
            for s in range(GROUPS):
                g = b * GROUPS + s
                keep_rows(g - 1, 1)
                if s == 0:
                    part_queries(b)
                if s == 2 and later(b):
                    keep_acc(b)
                part_keys(g, 4)
                part_keys(g, 5)
                softplus_tail(g - 1)
                part_keys(g, 6)
                keep_rows(g, 0)
                part_keys(g, 7)
                for k in range(3):
                    part_keys(g + 1, k)
                weight(g - 1, (s - 1) % 2)
                part_keys(g + 1, 3)

        prompt_done(act)
        for k in range(4):
            part_keys(0, k)
        steps(act, body)
        keep_rows(LAST, 1)
        softplus_tail(LAST)
        weight(LAST, 1)
        after.split_hi(act, 0, 0)
        keep_acc(NB)

    @block.vector
    def _(dve):
        def part_keys(g, k):
            if not exists(g):
                return
            j, half = k // 2, k % 2
            dve.wait_ge(kt_hi_made, g * UNITS + k + 1)
            at = (slice(None), slice(4 * half, 4 * half + 4), slice(j % 2 * PAGE, (j % 2 + 1) * PAGE))
            nc.vector.tensor_tensor(kt_lo[j // 2][at], ps[:, k % 4, :].rearrange("p (r c) -> p r c", c=P),
                                    kt_hi[j // 2][at].bitcast(F32), ALU.subtract).then_inc(kt_lo_made, 1)

        def part_queries(b):
            dve.wait_ge(q_hi_made, b + 1)
            for e in range(2):
                op = nc.vector.tensor_tensor(q_cols(e, 1), q_src(b, e), q_cols(e, 0).bitcast(F32), ALU.subtract)
            op.then_inc(q_lo_made, 1)

        def part_values(g, j):
            if not exists(g):
                return
            dve.wait_ge(v_in[j], g * 16 + 16)
            if later(g):
                dve.wait_ge(applied, (g - 1) * GP + (j + 1))
            nc.vector.tensor_copy(v_hi[j][:, :], vp[j][:, :]).then_inc(v_hi_made, 1)

        def decay(g, par):
            if not exists(g):
                return
            dve.wait_ge(summed, g + 1)
            nc.vector.tensor_tensor(zb[par][:, :], zb[par][:, :], sums, ALU.subtract).then_inc(decayed, 1)

        def part_weights(g, par):
            if not exists(g):
                return
            dve.wait_ge(weighted, g + 1)
            if later(g, 2):
                dve.wait_ge(applied, (g - 1) * GP)
            w = wf[:, :].rearrange("p (j c) -> p j c", j=GP)
            nc.vector.tensor_copy(wp[par][:, :, 0, :], w).then_inc(w_hi_made, 1)
            dve.wait_ge(w_hi_made, g + 1)
            nc.vector.tensor_tensor(wp[par][:, :, 1, :], w, wp[par][:, :, 0, :].bitcast(F32),
                                    ALU.subtract).then_inc(w_lo_made, 1)

        def bias(g, par):
            if not exists(g):
                return
            dve.wait_ge(turned, g + 1)
            if later(g, 2):
                dve.wait_ge(weighted, g - 1)
            nc.vector.tensor_tensor(
                zb[par][:, :].rearrange("p (j c) -> p j c", j=GP),
                turned_z.rearrange("p (j c) -> p j c", j=GP),
                mem.biasT[:, :, :].rearrange("p h t -> p (h t)").unsqueeze(1).to_broadcast([P, GP, HT]),
                ALU.add).then_inc(biased, 1)
            dve.wait_ge(biased, g + 1)
            if later(g):
                dve.wait_ge(sp_made, g)
            nc.vector.scalar_tensor_tensor(out=soft[:, :], in0=zb[par][:, :], scalar=-1.0, in1=zb[par][:, :],
                                           op0=ALU.mult, op1=ALU.min).then_inc(sized, 1)

        def softplus(b, s):
            g, par = b * GROUPS + s, s % 2
            if not exists(g):
                return
            dve.wait_ge(softened, g * 2 + 2)
            if later(g, 2):
                dve.wait_ge(summed, g - 1)
                dve.wait_ge(lost_made, lost_ready(b, s - 2) + (s % GROUPS != 1))
            nc.vector.scalar_tensor_tensor(out=sp_[par][:, :], in0=zb[par][:, :], scalar=0.0, in1=soft[:, :],
                                           op0=ALU.max, op1=ALU.add).then_inc(sp_made, 1)

        def add(b):
            dve.wait_ge(extracted, b)
            for e in range(2):
                to = mem.oT[e * HD:(e + 1) * HD, :, bass.ds(b * NT + (SEQ - NT), NT)]
                op = nc.vector.tensor_tensor(to, own[e * HD:(e + 1) * HD, :].rearrange(
                    "p (a c) -> p a c", c=2 * NT)[:, :, e * NT:(e + 1) * NT], to, ALU.add)
            op.then_inc(added, 1)

        def body(b):
            for s in range(GROUPS):
                g = b * GROUPS + s
                if s == 0:
                    part_queries(b)
                part_keys(g, 4)
                part_values(g - 2, 3)
                bias(g - 1, (s - 1) % 2)
                part_keys(g, 5)
                if s == 3 and later(b):
                    add(b)
                softplus(b, s - 1)
                part_keys(g, 6)
                part_keys(g, 7)
                part_keys(g + 1, 0)
                part_values(g - 1, 0)
                part_keys(g + 1, 1)
                part_values(g - 1, 1)
                decay(g - 1, (s - 1) % 2)
                part_keys(g + 1, 2)
                part_weights(g - 1, (s - 1) % 2)
                part_keys(g + 1, 3)
                part_values(g - 1, 2)

        prompt_done(dve)
        nc.vector.memset(qb[:, :].bitcast(F32), 0.0).then_inc(q_zeroed, 1)
        dve.wait_ge(q_zeroed, 1)
        for k in range(4):
            part_keys(0, k)
        steps(dve, body)
        bias(LAST, 1)
        part_values(LAST - 1, 3)
        softplus(NB - 1, GROUPS - 1)
        part_values(LAST, 0)
        part_values(LAST, 1)
        decay(LAST, 1)
        part_weights(LAST, 1)
        part_values(LAST, 2)
        part_values(LAST, 3)
        for j in range(GP - DVE_TAIL, GP):
            dve.wait_ge(v_hi_made, LAST * GP + (j + 1))
            nc.vector.tensor_tensor(v_lo[j][:, :], vp[j][:, :], v_hi[j][:, :].bitcast(F32),
                                    ALU.subtract).then_inc(v_tail_made, 1)
        add(NB)

    @block.gpsimd
    def _(pool):
        def part_values(g, j):
            if not exists(g):
                return
            pool.wait_ge(v_hi_made, g * GP + (j + 1))
            nc.gpsimd.tensor_tensor(v_lo[j][:, :], vp[j][:, :], v_hi[j][:, :].bitcast(F32),
                                    ALU.subtract).then_inc(v_lo_made, 1)

        def lose(b, s):
            if s < 0:
                b, s = b - 1, s + GROUPS
            g = b * GROUPS + s
            if not exists(g):
                return
            par = s % 2
            done = b * LOST_STEPS + LOST_BEFORE[s]
            pool.wait_ge(sp_made, g + 1)
            if later(g):
                pool.wait_ge(summed, g)
            if later(g):
                pool.wait_ge(lost_made, done)
            if s == 0:
                nc.gpsimd.tensor_tensor(lost[0][:, GP, :],
                                        mem.carry[:, bass.ds(b, 1), :].rearrange("p a c -> p (a c)"),
                                        zero[:, :], ALU.add).then_inc(lost_made, 1)
                done += 1
            for i, j in enumerate(range(GP - 1, -1, -1)):
                if j == 0 and s == GROUPS - 1:
                    break
                to = lost[par][:, j, :] if j else lost[1 - par][:, GP, :]
                pool.wait_ge(lost_made, done + i)
                nc.gpsimd.tensor_tensor(to, lost[par][:, j + 1, :],
                                        sp_[par][:, j * HT:(j + 1) * HT], ALU.add).then_inc(lost_made, 1)

        def body(b):
            for s in range(GROUPS):
                g = b * GROUPS + s
                part_values(g - 2, 3)
                lose(b, s - 1)
                for j in range(3):
                    part_values(g - 1, j)

        prompt_done(pool)
        nc.gpsimd.memset(zero[:, :], 0.0).then_inc(zeroed, 1)
        pool.wait_ge(zeroed, 1)
        steps(pool, body)
        part_values(LAST - 1, 3)
        lose(NB - 1, GROUPS - 1)
        for j in range(GP - DVE_TAIL):
            part_values(LAST, j)


class MergeWeights:

    PK = PT // len(WINDOWS)
    GM = KD // len(WINDOWS)
    AK = (PAIRS - 3, 3)
    KTS = (AK[0], AK[1] + PK)

    def __init__(self, nc, ctx, mem, a):
        self.slots, self.end = Weights.place(nc, ctx, mem, "w", mem.after_mix)
        self.begin = mem.after_mix
        self.first_end = self.begin + 3 * 4 * Weights.KT * P
        self.pool_in = ctx.enter_context(nc.semaphore("pool_w_in"))
        self.w_attn = a["w_attn_proj"][0].rearrange("(k p) c -> p k c", p=P)
        self.w_pool = a["w_pool"][0].rearrange("g (k p) c -> g p k c", p=P)

    def load(self, sp, m, g, j):
        W, AK, PK = self.slots, self.AK, self.PK
        W.load(sp, m, 0, self.w_attn[:, 0:AK[0], bass.ds(m * P, P)], AK[0])
        W.load(sp, m, 1, self.w_attn[:, AK[0]:PAIRS, bass.ds(m * P, P)], AK[1])
        sp.dma_start(W.raw[1][:, AK[1]:AK[1] + PK, :], self.w_pool[bass.ds(g, 1), :, :, j * P:(j + 1) * P].rearrange(
            "g p k c -> p (g k) c")).then_inc(self.pool_in, 16)

    def split_hi(self, act, m, b):
        if b == 1:
            act.wait_ge(self.pool_in, m * 16 + 16)
        self.slots.split_hi(act, m, b, self.KTS[b])

    def split_lo(self, dve, m, b):
        self.slots.split_lo(dve, m, b, self.KTS[b])


def merge_to_end(nc, mem, ps, a, o, scratch, first):
    with ExitStack() as ctx:
        W, w_end = first.slots, first.end
        W_out, W_ffn = W.after(KD), W.after(2 * KD)
        small, end = mem.run(w_end, *[(f"small{i}", [P, T], F32) for i in range(3)])
        assert end <= mem.before_h, (end, mem.before_h)
        with nc.Block(no_gpsimd_drain=True) as block:
            gated, mixed = merge_branches(nc, block, ctx, mem, ps, a, scratch, first, W_out)
            h_ready = project_out(nc, block, ctx, mem, ps, a, scratch, W_out, W_ffn, small, gated, mixed)
            feed_forward(nc, block, ctx, mem, ps, a, o, W_ffn, w_end, h_ready)


def merge_branches(nc, block, ctx, mem, ps, a, scratch, weights, W_next):
    sem = lambda name: ctx.enter_context(nc.semaphore("e_" + name))
    specs = [("e_o_hi", [P, PAIRS, T], F32R), ("e_o_lo", [P, PAIRS, T], F32R)] + [
        (f"e_{n}{i}", [P, T], F32) for n in ("gate_a", "gate_p", "mixed") for i in range(2)] + [
        ("e_part_a", [P, T], F32), ("e_part_p", [P, T], F32)]
    tensors, end = mem.run(mem.before_h, *specs)
    assert end <= mem.top_o, (end, mem.top_o)
    o_hi, o_lo = tensors[0:2]
    gate_a, gate_p, mixed = tensors[2:4], tensors[4:6], tensors[6:8]
    part_a, part_p = tensors[8:10]
    o_hi_made, o_lo_made = sem("o_hi_made"), sem("o_lo_made")
    gates_in = [sem(f"gates_in{i}") for i in range(2)]
    gated, mixed_made, hi_made, lo_made = sem("gated"), sem("mixed_made"), sem("hi_made"), sem("lo_made")
    W, PK, GM, AK = weights.slots, weights.PK, weights.GM, weights.AK
    banks = [[ps[:, 4 * p + 2 * i:4 * p + 2 * i + 2, :] for i in range(2)] for p in range(2)]
    groups = lambda eng, body: (body(0), _loop(eng, 1, len(WINDOWS) - 1, body), body(len(WINDOWS) - 1))
    last = lambda m: isinstance(m, int) and m == KD - 1

    @block.sync
    def _(sp):
        def load(m, g, j):
            if later(m):
                weights.load(sp, m, g, j)
            for buf, first in ((gate_a, 0), (gate_p, KD)):
                if later(m, 2):
                    sp.wait_ge(mixed_made, m - 1)
                sp.dma_start(buf[j % 2][:, :].unsqueeze(1), scratch["gates"][bass.ds(m + first, 1), :, :].rearrange(
                    "a p t -> p a t")).then_inc(gates_in[j % 2], 16)

        def body(g):
            for j in range(GM):
                load(g * GM + j, g, j)

        groups(sp, body)

    @block.tensor
    def _(pe):
        def body(g):
            for j in range(GM):
                m, p = g * GM + j, j % 2
                if later(m, 2):
                    pe.wait_ge(gated, 2 * (m - 1))
                ready = None
                if isinstance(m, int) and m == 0:
                    ready = lambda k: pe.wait_ge(o_lo_made, k + 1)
                W.multiply(pe, m, 0, banks[p][0], tile_of(o_hi), tile_of(o_lo), 0, AK[0], stop=False, x_ready=ready)
                W.multiply(pe, m, 1, banks[p][0], tile_of(o_hi), tile_of(o_lo), AK[0], AK[1], start=False,
                           x_ready=ready, last=False)
                group_tile = lambda x: lambda k, half: x[:, bass.ds(g * PK + k, 1), half * HALF:(half + 1) * HALF]
                W.multiply(pe, m, 1, banks[p][1], group_tile(mem.pool_hi), group_tile(mem.pool_lo), 0, PK, at=AK[1])

        groups(pe, body)

    @block.scalar
    def _(act):
        def body(g):
            for j in range(GM):
                m = g * GM + j
                for b in range(2):
                    if last(m):
                        W_next.split_hi(act, 0, b)
                    else:
                        weights.split_hi(act, m + 1, b)
                act.wait_ge(mixed_made, m + 1)
                nc.scalar.copy(mem.mix_hi[:, bass.ds(m, 1), :], mixed[j % 2][:, :].unsqueeze(1)).then_inc(hi_made, 1)

        weights.split_hi(act, 0, 1)
        for k in range(PAIRS):
            nc.scalar.copy(o_hi[:, k, :], mem.oT[:, k, :]).then_inc(o_hi_made, 1)
        groups(act, body)

    @block.vector
    def _(dve):
        def gate(m, p):
            dve.wait_ge(gates_in[p], (m - p) // 2 * 32 + 32)
            W.wait_slot(dve, m)
            if later(m):
                dve.wait_ge(mixed_made, m)
            nc.vector.tensor_tensor(by_halves(part_a[:, :]), halves(banks[p][0]),
                                    by_halves(gate_a[p][:, :]), ALU.mult).then_inc(gated, 1)
            nc.vector.scalar_tensor_tensor(out=by_halves(part_p[:, :]), in0=halves(banks[p][1]),
                                           scalar=mem.vec[:, bass.ds(m + V_PSCALE, 1)],
                                           in1=by_halves(gate_p[p][:, :]), op0=ALU.mult,
                                           op1=ALU.mult).then_inc(gated, 1)

        def body(g):
            for j in range(GM):
                m = g * GM + j
                if last(m):
                    W_next.split_lo(dve, 0, 0)
                    part(m - 1, 1 - j % 2)
                    gate(m, j % 2)
                    W_next.split_lo(dve, 0, 1)
                    continue
                for b in range(2):
                    weights.split_lo(dve, m + 1, b)
                gate(m, j % 2)
                if later(m):
                    part(m - 1, 1 - j % 2)

        def part(m, p):
            dve.wait_ge(hi_made, m + 1)
            nc.vector.tensor_tensor(mem.mix_lo[:, bass.ds(m, 1), :], mixed[p][:, :].unsqueeze(1),
                                    mem.mix_hi[:, bass.ds(m, 1), :].bitcast(F32), ALU.subtract).then_inc(lo_made, 1)

        for b in range(2):
            weights.split_lo(dve, 0, b)
        for k in range(PAIRS):
            dve.wait_ge(o_hi_made, k + 1)
            nc.vector.tensor_tensor(o_lo[:, k, :], mem.oT[:, k, :], o_hi[:, k, :].bitcast(F32),
                                    ALU.subtract).then_inc(o_lo_made, 1)
        groups(dve, body)
        part(KD - 1, (KD - 1) % 2)

    @block.gpsimd
    def _(pool):
        def body(g):
            for j in range(GM):
                m = g * GM + j
                pool.wait_ge(gated, 2 * m + 2)
                if later(m, 2):
                    pool.wait_ge(lo_made, m - 1)
                nc.gpsimd.tensor_tensor(mixed[j % 2][:, :], part_a[:, :], part_p[:, :], ALU.add).then_inc(mixed_made, 1)

        groups(pool, body)

    return gated, lo_made


def project_out(nc, block, ctx, mem, ps, a, scratch, W, W_next, small, gated, mixed):
    sem = lambda name: ctx.enter_context(nc.semaphore("f_" + name))
    (x0, x1, sq), total = small, mem.total
    xr = (x0, x1)
    x_in = [sem(f"x_in{i}") for i in range(2)]
    h_made, hi_made, lo_made, squared, totalled = (
        sem("h_made"), sem("hi_made"), sem("lo_made"), sem("squared"), sem("totalled"))
    cleared = sem("cleared")
    w_out = a["w_out"][0].rearrange("(b k p) c -> b p k c", b=2, p=P)
    banks = [ps[:, 2 * p:2 * p + 2, :] for p in range(2)]
    is_last = lambda m: isinstance(m, int) and m == KD - 1

    @block.sync
    def _(sp):
        def load(m, i, p):
            for b in range(2):
                W.load(sp, m, b, w_out[b][:, :, bass.ds(m * P, P)])
            if later(m, 2):
                sp.wait_ge(h_made, m - 1)
            sp.dma_start(xr[p][:, :].unsqueeze(1), scratch["xT"][bass.ds(m, 1), :, :].rearrange(
                "a p t -> p a t")).then_inc(x_in[p], 16)

        by_pairs(sp, 0, KD, load)

    @block.tensor
    def _(pe):
        def step(m, i, p):
            if later(m, 2):
                pe.wait_ge(h_made, m - 1)
            else:
                pe.wait_ge(gated, 2 * KD - 2)
            for b in range(2):
                if isinstance(m, int) and m == 0:
                    pe.wait_ge(mixed, (KD - 1, KD)[b])
                W.multiply(pe, m, b, banks[p], tile_of(mem.mix_hi), tile_of(mem.mix_lo), b * W.KT,
                           start=b == 0, stop=b == 1)

        by_pairs(pe, 0, KD, step)

    @block.scalar
    def _(act):
        def step(m, i, p):
            for b in range(2):
                (W_next if is_last(m) else W).split_hi(act, 0 if is_last(m) else m + 1, b)
            act.wait_ge(h_made, m + 1)
            if later(m):
                act.wait_ge(totalled, m)
            h = mem.hT[:, bass.ds(m, 1), :]
            nc.scalar.activation(mem.hn_hi[:, bass.ds(m, 1), :], h, ACT.Copy,
                                 scale=mem.vec[:, bass.ds(m + V_NORM2, 1)]).then_inc(hi_made, 1)
            nc.scalar.square(sq[:, :].unsqueeze(1), h).then_inc(squared, 1)

        by_pairs(act, 0, KD, step, tail=2)

    @block.vector
    def _(dve):
        def step(m, i, p):
            for b in range(2):
                (W_next if is_last(m) else W).split_lo(dve, 0 if is_last(m) else m + 1, b)
            dve.wait_ge(x_in[p], i * 16 + 16)
            W.wait_slot(dve, m)
            nc.vector.tensor_tensor(by_halves(mem.hT[:, bass.ds(m, 1), :].rearrange("p a t -> p (a t)")),
                                    halves(banks[p]), by_halves(xr[p][:, :]), ALU.add).then_inc(h_made, 1)
            dve.wait_ge(hi_made, m + 1)
            nc.vector.scalar_tensor_tensor(out=mem.hn_lo[:, bass.ds(m, 1), :], in0=mem.hT[:, bass.ds(m, 1), :],
                                           scalar=mem.vec[:, bass.ds(m + V_NORM2, 1)],
                                           in1=mem.hn_hi[:, bass.ds(m, 1), :].bitcast(F32),
                                           op0=ALU.mult, op1=ALU.subtract).then_inc(lo_made, 1)

        by_pairs(dve, 0, KD, step, tail=2)

    @block.gpsimd
    def _(pool):
        nc.gpsimd.memset(total[:, :], 0.0).then_inc(cleared, 1)
        pool.wait_ge(cleared, 1)

        def step(m, i, p):
            pool.wait_ge(squared, m + 1)
            if later(m):
                pool.wait_ge(totalled, m)
            nc.gpsimd.tensor_tensor(total[:, :], total[:, :], sq[:, :], ALU.add).then_inc(totalled, 1)

        by_pairs(pool, 0, KD, step)

    return h_made, lo_made, totalled


def feed_forward(nc, block, ctx, mem, ps, a, o, W, w_end, h_ready):
    SLOTS = 2 * CF + KD
    DOWN = (6, CF - 6)
    FULL = (Weights.KT, Weights.KT)
    sem = lambda name: ctx.enter_context(nc.semaphore("g_" + name))
    (act_hi, act_lo, gate, up, silu, hidden, y0, y1), end = mem.run(
        mem.free, ("g_act_hi", [P, CF, T], F32R), ("g_act_lo", [P, CF, T], F32R), ("g_gate", [P, T], F32),
        ("g_up", [P, T], F32), ("g_silu", [P, T], F32), ("g_hidden", [P, T], F32),
        ("g_y0", [P, T], F32), ("g_y1", [P, T], F32))
    assert end <= mem.after_mix, (end, mem.after_mix)
    (out0, out1, outS0, outS1), end = mem.run(
        w_end, ("g_out0", [P, SEQ // P, P], F32), ("g_out1", [P, SEQ // P, P], F32),
        ("g_outS0", [NSAMP, P], F32), ("g_outS1", [NSAMP, P], F32))
    assert end <= mem.before_h
    y, out, out_s = (y0, y1), (out0, out1), (outS0, outS1)
    h_made, h_parts, totalled = h_ready
    summed, rooted, inverted = sem("summed"), sem("rooted"), sem("inverted")
    turned, out_made, stored = sem("turned"), sem("out_made"), [sem(f"stored{i}") for i in range(2)]
    y_out = [o["y_prompt"][0].rearrange("(b p) d -> p b d", p=P), o["y_sample"].rearrange("b t d -> (b t) d")]
    vacated = sem("vacated")
    silu_made, hidden_made, hi_made, lo_made = sem("silu_made"), sem("hidden_made"), sem("hi_made"), sem("lo_made")
    w_gu = a["w_gate_up"][0].rearrange("(b k p) c -> b p k c", b=2, p=P)
    w_down = a["w_down"][0].rearrange("(f p) c -> p f c", p=P)
    banks = [ps[:, 2 * p:2 * p + 2, :] for p in range(2)]

    def chunk(eng, c, hidden_slots, down_slot):
        hidden_slots(c, 0, FULL)
        with eng.Fori(1, CF - 1) as f:
            hidden_slots(c, f, FULL)
        hidden_slots(c, CF - 1, DOWN)
        for m in range(4):
            down_slot(c, m, m % 2, DOWN)
        with eng.Fori(2, KD // 2 - 1) as i:
            for p in range(2):
                down_slot(c, i * 2 + p, p, DOWN)
        down_slot(c, KD - 2, 0, DOWN)
        down_slot(c, KD - 1, 1, None if isinstance(c, int) and c == CHUNKS - 1 else FULL)

    def chunks(eng, hidden_slots, down_slot):
        chunk(eng, 0, hidden_slots, down_slot)
        with eng.Fori(1, CHUNKS - 1) as c:
            chunk(eng, c, hidden_slots, down_slot)
        chunk(eng, CHUNKS - 1, hidden_slots, down_slot)

    is_last = lambda c: isinstance(c, int) and c == CHUNKS - 1
    hidden_n = lambda c, f, which: c * SLOTS + f * 2 + which
    down_n = lambda c, m: c * SLOTS + m + 2 * CF

    @block.sync
    def _(sp):
        def hidden_slots(c, f, after):
            for which in range(2):
                for b in range(2):
                    W.load(sp, hidden_n(c, f, which), b,
                           w_gu[b][:, :, bass.ds((c * CF + f + which * FT) * P, P)])

        def down_slot(c, m, p, after):
            for b in range(2):
                W.load(sp, down_n(c, m), b, w_down[:, bass.ds(c * CF + b * DOWN[0], DOWN[b]), bass.ds(m * P, P)],
                       DOWN[b])
            if is_last(c) and later(m, 2):
                store(m - 2, p)

        def store(m, p):
            sp.wait_ge(out_made, m + 1)
            cols = bass.ds(m * P, P)
            sp.dma_start(y_out[0][:, :, cols], out[p][:, :, :]).then_inc(stored[p], 16)
            sp.dma_start(y_out[1][:, cols], out_s[p][:, :]).then_inc(stored[p], 16)

        chunks(sp, hidden_slots, down_slot)
        for m in (KD - 2, KD - 1):
            store(m, m % 2)
        for p in range(2):
            sp.wait_ge(stored[p], KD // 2 * 32)

    @block.tensor
    def _(pe):
        def hidden_slots(c, f, after):
            for which in range(2):
                n = hidden_n(c, f, which)
                if later(n, 2):
                    pe.wait_ge(vacated, n - 1)
                else:
                    pe.wait_ge(h_made, KD - 1 + n)
                for b in range(2):
                    if isinstance(n, int) and n == 0:
                        pe.wait_ge(h_parts, (KD - 1, KD)[b])
                    W.multiply(pe, n, b, banks[which], tile_of(mem.hn_hi), tile_of(mem.hn_lo), b * W.KT,
                               start=b == 0, stop=b == 1)
                if isinstance(n, int) and n == 0:
                    pe.wait_ge(totalled, KD)
                    for half in range(2):
                        mm = nc.tensor.matmul(ps[:, 4 + half, 0:HALF], mem.c(C_ONES),
                                              mem.total[:, half * HALF:(half + 1) * HALF], start=True, stop=True)
                    mm.then_inc(summed, 1)

        def turn(n, m, p):
            pe.wait_ge(vacated, n + 1)
            if later(m, 2):
                pe.wait_ge(out_made, m - 1)
            for t in range(SEQ // P):
                nc.tensor.transpose(ps[:, 4 + p, t * P:(t + 1) * P], y[p][:, t * P:(t + 1) * P], mem.c(C_IDENT))
            nc.tensor.transpose(ps[0:NSAMP, 6 + p, 0:P], y[p][:, SEQ:T], mem.c(C_IDENT)).then_inc(turned, 1)

        def down_slot(c, m, p, after):
            n = down_n(c, m)
            pe.wait_ge(vacated, n - 1)
            for b in range(2):
                if b == 1 and is_last(c) and later(m):
                    turn(n - 1, m - 1, 1 - p)
                pe.wait_ge(lo_made, c * CF + (DOWN[0] if b == 0 else CF))
                W.multiply(pe, n, b, banks[p], tile_of(act_hi), tile_of(act_lo), b * DOWN[0], DOWN[b],
                           start=b == 0, stop=b == 1)

        chunks(pe, hidden_slots, down_slot)
        turn(down_n(CHUNKS - 1, KD - 1), KD - 1, 1)

    @block.scalar
    def _(act):
        def split_next(n, after):
            if after is not None:
                for b in range(2):
                    W.split_hi(act, n + 1, b, after[b])

        def hidden_slots(c, f, after):
            n, h = hidden_n(c, f, 0), c * CF + f
            split_next(n, FULL)
            if isinstance(n, int) and n == 0:
                act.wait_ge(summed, 1)
                nc.scalar.activation(by_halves(mem.total[:, :]), ps[:, 4:6, 0:HALF], ACT.Sqrt, scale=1.0 / D,
                                     bias=mem.vec[:, 63:64]).then_inc(rooted, 1)
            act.wait_ge(vacated, n + 1)
            if later(h):
                act.wait_ge(hidden_made, h)
            nc.scalar.activation(silu[:, :], gate[:, :], ACT.Silu).then_inc(silu_made, 1)
            split_next(n + 1, after)
            act.wait_ge(hidden_made, h + 1)
            if later(c):
                W.wait_slot(act, c * SLOTS - 1)
            nc.scalar.copy(act_hi[:, bass.ds(f, 1), :], hidden[:, :].unsqueeze(1)).then_inc(hi_made, 1)

        def keep(m, p):
            act.wait_ge(turned, m + 1)
            if later(m, 2):
                act.wait_ge(stored[p], (m - p) // 2 * 32)
            nc.scalar.copy(out[p][:, :, :], ps[:, 4 + p, :].rearrange("p (b c) -> p b c", c=P))
            nc.scalar.copy(out_s[p][:, :], ps[0:NSAMP, 6 + p, 0:P]).then_inc(out_made, 1)

        def down_slot(c, m, p, after):
            split_next(down_n(c, m), after)
            if is_last(c) and later(m):
                keep(m - 1, 1 - p)

        chunks(act, hidden_slots, down_slot)
        keep(KD - 1, 1)

    @block.vector
    def _(dve):
        def split_next(n, after):
            if after is not None:
                for b in range(2):
                    W.split_lo(dve, n + 1, b, after[b])

        def scale(n, p, to):
            W.wait_slot(dve, n)
            nc.vector.tensor_tensor(by_halves(to[:, :]), halves(banks[p]), by_halves(mem.rstd2[:, :]),
                                    ALU.mult).then_inc(vacated, 1)

        def hidden_slots(c, f, after):
            n, h = hidden_n(c, f, 0), c * CF + f
            split_next(n, FULL)
            if isinstance(n, int) and n == 0:
                dve.wait_ge(rooted, 1)
                nc.vector.reciprocal(mem.rstd2[:, :], mem.total[:, :]).then_inc(inverted, 1)
                dve.wait_ge(inverted, 1)
            if later(h):
                dve.wait_ge(silu_made, h)
            scale(n, 0, gate)
            split_next(n + 1, after)
            if later(h):
                dve.wait_ge(hidden_made, h)
            scale(n + 1, 1, up)
            dve.wait_ge(silu_made, h + 1)
            dve.wait_ge(vacated, n + 2)
            if later(h):
                dve.wait_ge(lo_made, h)
            nc.vector.tensor_tensor(hidden[:, :], silu[:, :], up[:, :], ALU.mult).then_inc(hidden_made, 1)
            dve.wait_ge(hi_made, h + 1)
            nc.vector.tensor_tensor(act_lo[:, bass.ds(f, 1), :], hidden[:, :].unsqueeze(1),
                                    act_hi[:, bass.ds(f, 1), :].bitcast(F32), ALU.subtract).then_inc(lo_made, 1)

        def down_slot(c, m, p, after):
            n = down_n(c, m)
            split_next(n, after)
            W.wait_slot(dve, n)
            if later(c):
                dve.wait_ge(vacated, c * SLOTS)
            h = by_halves(mem.hT[:, bass.ds(m, 1), :].rearrange("p a t -> p (a t)"))
            if is_last(c) and later(m, 2):
                dve.wait_ge(turned, m - 1)
            to = by_halves(y[p][:, :]) if is_last(c) else h
            nc.vector.tensor_tensor(to, halves(banks[p]), h, ALU.add).then_inc(vacated, 1)

        chunks(dve, hidden_slots, down_slot)


OUTPUTS = [
    ("y_prompt", (1, SEQ, D)), ("y_sample", (NB, NT, D)),
    ("k_prompt", (1, 1, SEQ, H, HD)), ("v_prompt", (1, 1, SEQ, H, HD)), ("pool_prompt", (1, 1, HIST, PW)),
    ("k_sample", (1, NB, NT, H, HD)), ("v_sample", (1, NB, NT, H, HD)), ("pool_sample", (1, NB, HIST, PW)),
]

def build(nc, a, o):
    scratch = {
        "xT": nc.dram_tensor("x_feature_major", (KD, P, T), F32, kind="Internal").ap(),
        "gates": nc.dram_tensor("gates", (2 * KD, P, T), F32, kind="Internal").ap(),
    }
    mem = Memory(nc)
    with ExitStack() as ctx, nc.psum_tensor("ps", [P, 8, 512], F32) as ps:
        first = MergeWeights(nc, ctx, mem, a)
        inputs_to_attention(nc, mem, ps, a, o, scratch, first)
        merge_to_end(nc, mem, ps, a, o, scratch, first)


def kernel(**inputs):
    import concourse.bacc as bacc
    from concourse.bass_utils import run_bass_kernel_spmd

    nc = bacc.Bacc("TRN2", target_bir_lowering=False, num_devices=1)
    arrays = {name: np.ascontiguousarray(x) for name, x in inputs.items()}
    arrays["const"], arrays["mask"] = constants()
    a = {name: nc.dram_tensor(name, x.shape, mybir.dt.from_np(x.dtype), kind="ExternalInput").ap()
         for name, x in arrays.items()}
    o = {name: nc.dram_tensor(name, shape, F32, kind="ExternalOutput").ap() for name, shape in OUTPUTS}
    build(nc, a, o)
    got = run_bass_kernel_spmd(nc, [arrays], core_ids=[0]).results[0]
    return tuple(got[name] for name, _ in OUTPUTS)
```
